# Optimizing a Trainium2 kernel written in Bass

```python
import math, functools
import jax, jax.numpy as jnp
from jax import lax
import numpy as np

D_MODEL = 2048
BATCH = 1
SEQ = 256
DEPTH = 1
DEC_BATCH = 8
DEC_SEQ = 16
PAST_LEN = 128

CHUNK = 64
Q_BLOCK = 128
N_DIFF_HEADS = D_MODEL // 256
DIFF_QK_DIM = 64
DIFF_V_DIM = 2 * DIFF_QK_DIM
N_SB_HEADS = D_MODEL // 256
SB_HEAD_DIM = 128
DIFF_QK_COLS = N_DIFF_HEADS * 2 * DIFF_QK_DIM
DIFF_WIDTH = N_DIFF_HEADS * DIFF_V_DIM
SB_WIDTH = N_SB_HEADS * SB_HEAD_DIM
MIX_WIDTH = DIFF_WIDTH + SB_WIDTH
IN_SPLITS = (DIFF_QK_COLS, 2 * DIFF_QK_COLS, 2 * DIFF_QK_COLS + DIFF_WIDTH,
             2 * DIFF_QK_COLS + DIFF_WIDTH + SB_WIDTH,
             2 * DIFF_QK_COLS + DIFF_WIDTH + 2 * SB_WIDTH)
IN_COLS = 2 * DIFF_QK_COLS + DIFF_WIDTH + 3 * SB_WIDTH
PEER_HEADS = 8
PEER_N_KEYS = 128
PEER_EXPERTS = PEER_N_KEYS * PEER_N_KEYS
PEER_QUERY_DIM = 256
PEER_SUBKEY_DIM = PEER_QUERY_DIM // 2
PEER_TOPK = 16
PEER_TOKEN_BLOCK = 128
DEEPNORM_ALPHA = (2.0 * DEPTH) ** 0.25
DEEPNORM_BETA = (8.0 * DEPTH) ** -0.25
LN_EPS = 1e-5
SUBLN_EPS = 1e-5

kernel_name = "diff_stickbreak_peer_streaming_step"

def layer_norm(x, g, b):
    xf = x.astype(jnp.float32)
    mu = jnp.mean(xf, axis=-1, keepdims=True)
    var = jnp.mean(jnp.square(xf - mu), axis=-1, keepdims=True)
    return ((xf - mu) * lax.rsqrt(var + LN_EPS) * g + b).astype(x.dtype)

def alibi_slopes(n_heads):
    return jnp.exp2(-8.0 * (jnp.arange(n_heads, dtype=jnp.float32) + 1.0) / n_heads)

def diff_attention(q, q_pos, k, v, k_pos, lam, lam_init, subln_g):
    s = jnp.einsum('bqhcd,bkhcd->bhcqk', q.astype(jnp.float32), k.astype(jnp.float32)) * (DIFF_QK_DIM ** -0.5)
    dist = jnp.abs(q_pos[:, None] - k_pos[None, :]).astype(jnp.float32)
    bias = -alibi_slopes(N_DIFF_HEADS)[:, None, None, None] * dist
    mask = (k_pos[None, :] // CHUNK) <= (q_pos[:, None] // CHUNK)
    s = jnp.where(mask, s + bias, -jnp.inf)
    p = jax.nn.softmax(s, axis=-1)
    w = p[:, :, 0] - lam * p[:, :, 1]
    o = jnp.einsum('bhqk,bkhd->bqhd', w, v.astype(jnp.float32))
    o = o * lax.rsqrt(jnp.mean(o * o, axis=-1, keepdims=True) + SUBLN_EPS) * subln_g * (1.0 - lam_init)
    return o.astype(v.dtype)

def stick_breaking_attention(q, q_pos, k, v, k_pos):
    z = jnp.einsum('bqhd,bkhd->bhqk', q.astype(jnp.float32), k.astype(jnp.float32)) * (SB_HEAD_DIM ** -0.5)
    mask = k_pos[None, :] < q_pos[:, None]
    log_keep = jnp.where(mask, jax.nn.log_sigmoid(-z), 0.0)
    rev = lax.cumsum(log_keep, axis=3, reverse=True)
    later = jnp.concatenate([rev[..., 1:], jnp.zeros_like(rev[..., :1])], axis=-1)
    a = jnp.where(mask, jnp.exp(jax.nn.log_sigmoid(z) + later), 0.0)
    o = jnp.einsum('bhqk,bkhd->bqhd', a, v.astype(jnp.float32))
    return o.astype(v.dtype)

def sweep_query_blocks(fn, q, q_pos, k, v, k_pos):
    b, tq = q.shape[0], q.shape[1]
    if tq <= Q_BLOCK:
        return fn(q, q_pos, k, v, k_pos)
    nb = tq // Q_BLOCK
    qb = jnp.moveaxis(q.reshape((b, nb, Q_BLOCK) + q.shape[2:]), 1, 0)
    pb = q_pos.reshape(nb, Q_BLOCK)
    ob = lax.map(lambda a: fn(a[0], a[1], k, v, k_pos), (qb, pb))
    return jnp.moveaxis(ob, 0, 1).reshape((b, tq) + ob.shape[3:])

def peer_block(xb, w_q, subkeys, u_tab, v_tab):
    n = xb.shape[0]
    q = jnp.einsum('nd,de->ne', xb, w_q).reshape(n, PEER_HEADS, 2, PEER_SUBKEY_DIM)
    s = jnp.einsum('nhcd,hckd->nhck', q.astype(jnp.float32), subkeys.astype(jnp.float32))
    s1, i1 = lax.top_k(s[:, :, 0], PEER_TOPK)
    s2, i2 = lax.top_k(s[:, :, 1], PEER_TOPK)
    cand = (s1[..., :, None] + s2[..., None, :]).reshape(n, PEER_HEADS, PEER_TOPK * PEER_TOPK)
    cidx = (i1[..., :, None] * PEER_N_KEYS + i2[..., None, :]).reshape(n, PEER_HEADS, PEER_TOPK * PEER_TOPK)
    top, pos = lax.top_k(cand, PEER_TOPK)
    eidx = jnp.take_along_axis(cidx, pos, axis=-1)
    g = jax.nn.softmax(top, axis=-1)
    u = u_tab[eidx]
    act = jax.nn.gelu(jnp.einsum('nd,nhkd->nhk', xb, u).astype(jnp.float32), approximate=False) * g
    return jnp.einsum('nhk,nhkd->nd', act.astype(xb.dtype), v_tab[eidx])

def peer_ffn(x, w_q, subkeys, u_tab, v_tab):
    b, t, d = x.shape
    xf = x.reshape(b * t, d)
    n = xf.shape[0]
    pad = (-n) % PEER_TOKEN_BLOCK
    xp = jnp.pad(xf, ((0, pad), (0, 0))).reshape(-1, PEER_TOKEN_BLOCK, d)
    out = lax.map(lambda xb: peer_block(xb, w_q, subkeys, u_tab, v_tab), xp)
    return out.reshape(-1, d)[:n].reshape(b, t, d)

def trunk_layer(x, past, lam_init, w_in, w_out, lam_q1, lam_k1, lam_q2, lam_k2, subln_g,
                ln1_g, ln1_b, ln2_g, ln2_b, peer_w_q, peer_subkeys, peer_u, peer_v):
    b, t, _ = x.shape
    h = jnp.einsum('btd,de->bte', x, w_in)
    qd, kd, vd, qs, ks, vs = jnp.split(h, IN_SPLITS, axis=-1)
    qd = qd.reshape(b, t, N_DIFF_HEADS, 2, DIFF_QK_DIM)
    kd = kd.reshape(b, t, N_DIFF_HEADS, 2, DIFF_QK_DIM)
    vd = vd.reshape(b, t, N_DIFF_HEADS, DIFF_V_DIM)
    qs = qs.reshape(b, t, N_SB_HEADS, SB_HEAD_DIM)
    ks = ks.reshape(b, t, N_SB_HEADS, SB_HEAD_DIM)
    vs = vs.reshape(b, t, N_SB_HEADS, SB_HEAD_DIM)
    new_rows = (kd, vd, ks, vs)
    if past is None:
        past_len = 0
        kd_all, vd_all, ks_all, vs_all = new_rows
    else:
        past_len = past[0].shape[1]
        kd_all, vd_all, ks_all, vs_all = [jnp.concatenate([p, r], axis=1) for p, r in zip(past, new_rows)]
    q_pos = past_len + jnp.arange(t, dtype=jnp.int32)
    k_pos = jnp.arange(past_len + t, dtype=jnp.int32)
    lam = (jnp.exp(jnp.sum(lam_q1.astype(jnp.float32) * lam_k1.astype(jnp.float32)))
           - jnp.exp(jnp.sum(lam_q2.astype(jnp.float32) * lam_k2.astype(jnp.float32))) + lam_init)
    diff_fn = functools.partial(diff_attention, lam=lam, lam_init=lam_init, subln_g=subln_g)
    o_diff = sweep_query_blocks(diff_fn, qd, q_pos, kd_all, vd_all, k_pos)
    o_sb = sweep_query_blocks(stick_breaking_attention, qs, q_pos, ks_all, vs_all, k_pos)
    mixed = jnp.concatenate([o_diff.reshape(b, t, DIFF_WIDTH), o_sb.reshape(b, t, SB_WIDTH)], axis=-1)
    x = layer_norm(DEEPNORM_ALPHA * x + jnp.einsum('bte,ed->btd', mixed, w_out), ln1_g, ln1_b)
    x = layer_norm(DEEPNORM_ALPHA * x + peer_ffn(x, peer_w_q, peer_subkeys, peer_u, peer_v), ln2_g, ln2_b)
    return x, new_rows

def setup_inputs(seed: int = 0) -> dict:
    key = jax.random.key(seed)
    ks = jax.random.split(key, 32)
    f32 = jnp.float32

    def nrm(k, shape, scale):
        return jax.random.normal(k, shape, f32) * scale

    s_in = D_MODEL ** -0.5
    beta = DEEPNORM_BETA
    w_in = jnp.concatenate([
        nrm(ks[6], (DEPTH, D_MODEL, DIFF_QK_COLS), s_in),
        nrm(ks[7], (DEPTH, D_MODEL, DIFF_QK_COLS), s_in),
        nrm(ks[8], (DEPTH, D_MODEL, DIFF_WIDTH), s_in * beta),
        nrm(ks[9], (DEPTH, D_MODEL, SB_WIDTH), s_in),
        nrm(ks[10], (DEPTH, D_MODEL, SB_WIDTH), s_in),
        nrm(ks[11], (DEPTH, D_MODEL, SB_WIDTH), s_in * beta),
    ], axis=-1)
    return {
        "x_prompt": nrm(ks[0], (BATCH, SEQ, D_MODEL), 1.0),
        "x_sample": nrm(ks[1], (DEC_BATCH, DEC_SEQ, D_MODEL), 1.0),
        "cache_diff_k": nrm(ks[2], (DEPTH, DEC_BATCH, PAST_LEN, N_DIFF_HEADS, 2, DIFF_QK_DIM), 1.0),
        "cache_diff_v": nrm(ks[3], (DEPTH, DEC_BATCH, PAST_LEN, N_DIFF_HEADS, DIFF_V_DIM), beta),
        "cache_sb_k": nrm(ks[4], (DEPTH, DEC_BATCH, PAST_LEN, N_SB_HEADS, SB_HEAD_DIM), 1.0),
        "cache_sb_v": nrm(ks[5], (DEPTH, DEC_BATCH, PAST_LEN, N_SB_HEADS, SB_HEAD_DIM), beta),
        "w_in": w_in,
        "w_out": nrm(ks[12], (DEPTH, MIX_WIDTH, D_MODEL), MIX_WIDTH ** -0.5 * beta),
        "lam_q1": nrm(ks[13], (DEPTH, DIFF_QK_DIM), 0.1),
        "lam_k1": nrm(ks[14], (DEPTH, DIFF_QK_DIM), 0.1),
        "lam_q2": nrm(ks[15], (DEPTH, DIFF_QK_DIM), 0.1),
        "lam_k2": nrm(ks[16], (DEPTH, DIFF_QK_DIM), 0.1),
        "subln_g": 1.0 + nrm(ks[17], (DEPTH, DIFF_V_DIM), 0.02),
        "ln1_g": 1.0 + nrm(ks[18], (DEPTH, D_MODEL), 0.02),
        "ln1_b": nrm(ks[19], (DEPTH, D_MODEL), 0.02),
        "ln2_g": 1.0 + nrm(ks[20], (DEPTH, D_MODEL), 0.02),
        "ln2_b": nrm(ks[21], (DEPTH, D_MODEL), 0.02),
        "peer_w_q": nrm(ks[22], (DEPTH, D_MODEL, PEER_HEADS * PEER_QUERY_DIM), s_in),
        "peer_subkeys": nrm(ks[23], (DEPTH, PEER_HEADS, 2, PEER_N_KEYS, PEER_SUBKEY_DIM), PEER_SUBKEY_DIM ** -0.5),
        "peer_u": nrm(ks[24], (DEPTH, PEER_EXPERTS, D_MODEL), s_in * beta),
        "peer_v": nrm(ks[25], (DEPTH, PEER_EXPERTS, D_MODEL), beta),
    }

def reference(x_prompt, x_sample, cache_diff_k, cache_diff_v, cache_sb_k, cache_sb_v,
              w_in, w_out, lam_q1, lam_k1, lam_q2, lam_k2, subln_g,
              ln1_g, ln1_b, ln2_g, ln2_b, peer_w_q, peer_subkeys, peer_u, peer_v):
    y_prompt, y_sample = x_prompt, x_sample
    rows_p, rows_s = [], []
    for l in range(DEPTH):
        lam_init = 0.8 - 0.6 * math.exp(-0.3 * l)
        params = (w_in[l], w_out[l], lam_q1[l], lam_k1[l], lam_q2[l], lam_k2[l], subln_g[l],
                  ln1_g[l], ln1_b[l], ln2_g[l], ln2_b[l], peer_w_q[l], peer_subkeys[l], peer_u[l], peer_v[l])
        y_prompt, rp = trunk_layer(y_prompt, None, lam_init, *params)
        past = (cache_diff_k[l], cache_diff_v[l], cache_sb_k[l], cache_sb_v[l])
        y_sample, rs = trunk_layer(y_sample, past, lam_init, *params)
        rows_p.append(rp)
        rows_s.append(rs)
    new_diff_k_prompt = jnp.stack([r[0] for r in rows_p])
    new_diff_v_prompt = jnp.stack([r[1] for r in rows_p])
    new_sb_k_prompt = jnp.stack([r[2] for r in rows_p])
    new_sb_v_prompt = jnp.stack([r[3] for r in rows_p])
    new_diff_k_sample = jnp.stack([r[0] for r in rows_s])
    new_diff_v_sample = jnp.stack([r[1] for r in rows_s])
    new_sb_k_sample = jnp.stack([r[2] for r in rows_s])
    new_sb_v_sample = jnp.stack([r[3] for r in rows_s])
    return (y_prompt, y_sample, new_diff_k_prompt, new_diff_v_prompt, new_sb_k_prompt, new_sb_v_prompt,
            new_diff_k_sample, new_diff_v_sample, new_sb_k_sample, new_sb_v_sample)


_drawn_inputs = setup_inputs


def setup_inputs(seed=0):
    import zlib

    import numpy as np

    out = dict(_drawn_inputs(seed))
    spreads = {}
    factors = {'lam_k1': 3.155,
     'lam_k2': 2.995,
     'subln_g': 4.46,
     'ln2_g': 8.254,
     'ln2_b': 7.942,
     'cache_sb_k': 3.627}
    for name, (base, spread) in spreads.items():
        noise = np.random.default_rng([zlib.crc32(name.encode()), seed]).standard_normal(out[name].shape)
        drawn = base * np.exp(spread * noise) if base else spread * noise
        out[name] = __import__('jax').numpy.asarray(drawn.astype(out[name].dtype))
    for name, factor in factors.items():
        out[name] = (out[name] * factor).astype(out[name].dtype)
    return out
```

```python
import math
from contextlib import ExitStack

import concourse.bass as bass
from concourse import mybir

F32 = mybir.dt.float32
I32 = mybir.dt.int32
U32 = mybir.dt.uint32
ALU = mybir.AluOpType
ACT = mybir.ActivationFunctionType
AX_X = mybir.AxisListType.X

P = 128
D = 2048
DT = D // P
NB = 3
T = NB * P
H = 8
STREAMS, FRAMES = 8, 16
CHUNK = 64
DIFF_SCALE = 64 ** -0.5
SB_SCALE = 128 ** -0.5
LAM_INIT = 0.8 - 0.6 * math.exp(0.0)
ALPHA = 2.0 ** 0.25
EPS = 1e-5
KEYS = 128
K = 16
EXPERTS = KEYS * KEYS
HIDDEN = 1e30
LOW = -3e38
ROW = 2048
U_SLOTS, V_SLOTS = 4, 8
DIAGS = 4
HEADS = NB * H


def build(nc, x_t, x_rows, w_heads, kd_cache, ks_cache, vd_cache, vs_cache, w_out, lam_vecs, subln,
          ln1, ln2, w_q, subkeys, peer_u, peer_v, y_out, kd_out, ks_out, v_out):
    ctx = ExitStack()
    with ctx:
        def sb(name, shape, dt=F32):
            return ctx.enter_context(nc.sbuf_tensor(name, shape, dt))

        def sem(name):
            return ctx.enter_context(nc.semaphore(name))

        arena = sb("arena", [P, 12, ROW])
        flat = arena[:, :, :].rearrange("p s c -> p (s c)")
        xT = flat[:, 0:DT * T].rearrange("p (t n) -> p t n", t=DT)
        squares = flat[:, 0:H * T]
        x1T = xT
        mixedT = flat[:, 3 * ROW:3 * ROW + 2 * H * T].rearrange("p (t n) -> p t n", t=2 * H)
        w_slot = [arena[:, 6 + i, :] for i in range(6)]
        w_v = flat[:, 10 * ROW:12 * ROW].rearrange("p (t n) -> p t n", t=DT)
        u_row = [arena[:, 3 + i, :] for i in range(U_SLOTS)]
        v_row = [arena[:, i, :] for i in (7, 8, 9, 10, 11, 0, 1, 2)]

        x1 = sb("x1", [P, NB, D])
        ln_rows = sb("ln_rows", [P, 2, D])
        cache = sb("cache", [P, 4, STREAMS * P])
        kd_past, ks_past, vd_past, vs_past = (cache[:, i, :].rearrange("p (b n) -> p b n", b=STREAMS)
                                              for i in range(4))
        subkT = cache[:, 0:2, :].rearrange("p a n -> p (a n)").rearrange("p (g k) -> p g k", g=2 * H)
        queryT = cache[:, 2, 0:2 * T].rearrange("p (c n) -> p c n", c=2)
        key_scores = cache[:, 3, 0:2 * T].rearrange("p (c b k) -> p c b k", c=2, b=NB)

        scratch = sb("scratch", [P, 9600])
        taken = [0]

        def cut(n):
            taken[0] += n
            assert taken[0] <= 9600
            return scratch[:, taken[0] - n:taken[0]]

        qk = cut(5 * T).rearrange("p (s n) -> p s n", s=5)
        qd_half = [qk[:, 0, :], qk[:, 4, :]]
        v_new = cut(NB * 256).rearrange("p (b n) -> p b n", b=NB)
        probs = cut(NB * 512).rearrange("p (b c n) -> p b c n", b=NB, c=2)
        weights = cut(5 * P).rearrange("p (s n) -> p s n", s=5)
        sticks = cut(5 * P).rearrange("p (s n) -> p s n", s=5)
        logit = cut(5 * P)
        soft = cut(5 * P)
        suffix = cut(5 * P)
        pastT = cut(3 * P).rearrange("p (s n) -> p s n", s=3)
        weightsT = cut(10 * P).rearrange("p (s n) -> p s n", s=10)
        head_loop_end = taken[0]
        taken[0] = 0
        rest = cut(2 * T).rearrange("p (c b k) -> p c b k", c=2, b=NB)
        cand = cut(NB * K * K).rearrange("p (b i j) -> p b i j", b=NB, i=K)
        cand_rest = cut(NB * K * K).rearrange("p (b i j) -> p b i j", b=NB, i=K)
        hit = cut(2 * NB * K * K).rearrange("p (c b i j) -> p c b i j", c=2, b=NB, i=K)
        taken[0] = 0
        normed = cut(D)
        diag = cut(DIAGS * P).rearrange("p (s n) -> p s n", s=DIAGS)
        del head_loop_end

        ident = sb("ident", [P, P])
        ident_alpha = sb("ident_alpha", [P, P])
        mean_mat = sb("mean_mat", [P, P])
        zeros = sb("zeros", [P, 256])
        dist = sb("dist", [P, 2, 256])
        stick_mask = sb("stick_mask", [P, 5 * P])
        ramp = sb("ramp", [P, 256])
        slopes = sb("slopes", [P, H])
        frame_i = sb("frame_i", [P, 1], I32)
        frame_f = sb("frame_f", [P, 1])
        eps = sb("eps", [P, 1])
        lam_in = sb("lam_in", [P, 4, 64])
        lam_prod = sb("lam_prod", [P, 2, 64])
        lam_dot = sb("lam_dot", [P, 2])
        lam_exp = sb("lam_exp", [P, 2])
        lam_diff = sb("lam_diff", [P, 1])
        neg_lam = sb("neg_lam", [P, 1])
        gain = sb("gain", [P, 1])
        gain8 = sb("gain8", [P, 1])
        row_min = sb("row_min", [P, NB, 2])
        row_sum = sb("row_sum", [P, NB, 2])
        row_inv = sb("row_inv", [P, NB, 2])
        lam_inv = sb("lam_inv", [P, NB, 1])
        stats = sb("stats", [P, NB, 4, 6])
        moments = sb("moments", [P, NB, 2])
        stdev = sb("stdev", [P, NB])
        rstd = sb("rstd", [P, NB])
        shift = sb("shift", [P, NB])
        half_top = sb("half_top", [P, 2, NB, K])
        half_idx = sb("half_idx", [P, 2, NB, K], U32)
        half_idx_f = sb("half_idx_f", [P, 2, NB, K])
        top = sb("top", [P, NB, K])
        top_pos = sb("top_pos", [P, NB, K], U32)
        pos_ij = sb("pos_ij", [P, 2, NB, K], U32)
        pos_ij_f = sb("pos_ij_f", [P, 2, NB, K])
        picked = sb("picked", [P, 2, NB, K])
        expert_f = sb("expert_f", [P, NB, K])
        iota16 = sb("iota16", [P, K])
        over_max = sb("over_max", [P, NB, K])
        expo = sb("expo", [P, NB, K])
        expo_sum = sb("expo_sum", [P, NB])
        expo_inv = sb("expo_inv", [P, NB])
        expert = sb("expert", [P, NB, H, K], U32)
        gate = sb("gate", [P, NB, H, K])
        idx_u = sb("idx_u", [P, 2, K], U32)
        idx_v = sb("idx_v", [P, 2, K], U32)
        dots = sb("dots", [P, K])
        gelu = sb("gelu", [P, K])
        coef = sb("coef", [P, 2, K])

        bank = [ctx.enter_context(nc.psum_tensor(f"bank{i}", [P, 512], F32)) for i in range(8)]
        diff_ps = [bank[0][:, :], bank[2][:, 0:256], bank[1][:, :]]
        stick02_ps, stick1_ps = bank[3][:, :], bank[2][:, 256:384]
        pastT_ps = bank[4][:, 0:3 * P].rearrange("p (s n) -> p s n", s=3)
        wT_ps = [bank[0][:, 0:384], bank[1][:, 0:384], bank[2][:, 0:512]]
        oT_ps = [bank[3][:, 0:T], bank[4][:, 0:T]]

        consts_loaded, x_loaded, rows_loaded, ln_loaded, subkeys_loaded = map(
            sem, ("consts_loaded", "x_loaded", "rows_loaded", "ln_loaded", "subkeys_loaded"))
        pool_init, dve_init, act_init = sem("pool_init"), sem("dve_init"), sem("act_init")
        w_loaded = [sem(f"w_loaded{i}") for i in range(5)]
        past_loaded = [sem(f"past_loaded{i}") for i in range(4)]
        stored = [sem(n) for n in ("kd_stored", "ks_stored", "v_stored")]
        qk_projected, v_projected = sem("qk_projected"), sem("v_projected")
        qd_half_copied, qk_evacuated, v_evacuated = sem("qd_half_copied"), sem("qk_evacuated"), sem("v_evacuated")
        pastT_scored, pastT_copied, scores_ready = sem("pastT_scored"), sem("pastT_copied"), sem("scores_ready")
        scores_read, logits_ready = sem("scores_read"), sem("logits_ready")
        min_ready, probs_ready, inv_ready = sem("min_ready"), sem("probs_ready"), sem("inv_ready")
        half_weights, weights_ready = sem("half_weights"), sem("weights_ready")
        neg_abs_ready, soft_ready, softplus_ready = sem("neg_abs_ready"), sem("soft_ready"), sem("softplus_ready")
        suffix_ready, exponent_ready, sticks_ready = sem("suffix_ready"), sem("exponent_ready"), sem("sticks_ready")
        transposed, wT_copied, values_done, oT_copied = (
            sem("transposed"), sem("wT_copied"), sem("values_done"), sem("oT_copied"))
        squared, meaned, rms_ready, rms_inv, diff_normed = (
            sem("squared"), sem("meaned"), sem("rms_ready"), sem("rms_inv"), sem("diff_normed"))
        wo_loaded = [sem(f"wo_loaded{i}") for i in range(4)]
        wo_used, out_projected, stats_ready = sem("wo_used"), sem("out_projected"), sem("stats_ready")
        residual_ready = [sem(f"residual_ready{b}") for b in range(NB)]
        ln1_step, ln1_sd, ln1_scaled, ln1_done = sem("ln1_step"), sem("ln1_sd"), sem("ln1_scaled"), sem("ln1_done")
        x1_transposed, x1T_copied = sem("x1_transposed"), sem("x1T_copied")
        wq_loaded = [sem("wq_loaded0"), sem("wq_loaded1")]
        query_done, query_copied, key_scored, key_copied = (
            sem("query_done"), sem("query_copied"), sem("key_scored"), sem("key_copied"))
        half_read, topk_step, over_ready, expo_ready, gates_ready = (
            sem("half_read"), sem("topk_step"), sem("over_ready"), sem("expo_ready"), sem("gates_ready"))
        idx_copied = sem("idx_copied")
        u_loaded = [sem(f"u_loaded{i}") for i in range(U_SLOTS)]
        v_loaded = [sem(f"v_loaded{i}") for i in range(V_SLOTS)]
        u_dotted, gelu_ready, coef_ready, diag_ready, v_added = (
            sem("u_dotted"), sem("gelu_ready"), sem("coef_ready"), sem("diag_ready"), sem("v_added"))
        ln2_step, ln2_weighted, ln2_sd, ln2_scaled, y_ready, y_stored = (
            sem("ln2_step"), sem("ln2_weighted"), sem("ln2_sd"), sem("ln2_scaled"), sem("y_ready"), sem("y_stored"))

        block = ctx.enter_context(nc.Block())

        LEAD = 1
        POOL_CONSTS = 35

        waits_passed = {"dve": sem("dve_waits_passed"), "pool": sem("pool_waits_passed")}

        def wait_apart(eng, who, signal, value):
            eng.wait_ge(signal, value)
            eng.sem_inc(waits_passed[who], 1)

        @block.sync
        def _(sp):
            def load_head(h):
                for s in range(4):
                    if not isinstance(h, int) or h > 0:
                        sp.wait_ge(qk_projected, (h - 1) * 4 + s + 1)
                    sp.dma_start(w_slot[s], w_heads[h, :, s * ROW:(s + 1) * ROW]).then_inc(w_loaded[s], 16)
                if not isinstance(h, int) or h > 0:
                    sp.wait_ge(v_projected, (h - 1) * NB + NB)
                sp.dma_start(flat[:, 10 * ROW:12 * ROW], w_heads[h, :, 4 * ROW:6 * ROW]).then_inc(w_loaded[4], 16)

            def load_past(h):
                for s, src in enumerate((kd_cache, ks_cache, vd_cache, vs_cache)):
                    if not isinstance(h, int) or h > 0:
                        sp.wait_ge(scores_ready if s < 2 else values_done, h)
                    sp.dma_start(cache[:, s, :], src[h]).then_inc(past_loaded[s], 16)

            sp.dma_start(flat[:, 0:DT * T], x_t).then_inc(x_loaded, 16)
            sp.dma_start(lam_in[:, :, :], lam_vecs).then_inc(consts_loaded, 16)
            sp.dma_start(gain[:, :], subln).then_inc(consts_loaded, 16)
            load_head(0)
            load_past(0)
            sp.dma_start(x1[:, :, :], x_rows).then_inc(rows_loaded, 16)
            sp.dma_start(ln_rows[:, :, :], ln1).then_inc(ln_loaded, 16)
            with sp.Fori(1, H) as h:
                load_head(h)
                load_past(h)

            def load_wo(n, g):
                sp.dma_start(w_slot[g], w_out[n, g]).then_inc(wo_loaded[g], 16)

            sp.wait_ge(qk_projected, 4 * H)
            for g in range(4):
                load_wo(0, g)
            sp.wait_ge(v_projected, NB * H)
            for c in range(2):
                sp.dma_start(w_slot[4 + c], w_q[c]).then_inc(wq_loaded[c], 16)
            sp.wait_ge(values_done, H)
            sp.dma_start(subkT, subkeys).then_inc(subkeys_loaded, 16)
            with sp.Fori(1, 4) as n:
                for g in range(4):
                    if g < 3:
                        sp.wait_ge(wo_used, (n - 1) * 3 + g + 1)
                    else:
                        sp.wait_ge(out_projected, n * NB)
                    load_wo(n, g)
            sp.wait_ge(ln1_done, NB)
            sp.dma_start(ln_rows[:, :, :], ln2).then_inc(ln_loaded, 16)
            with sp.Fori(1, H) as h:
                for c in range(2):
                    sp.wait_ge(query_done, (h - 1) * 2 + c + 1)
                    sp.dma_start(w_slot[4 + c], w_q[h * 2 + c]).then_inc(wq_loaded[c], 16)
            for b in range(NB):
                sp.wait_ge(y_ready, b + 1)
                sp.dma_start(y_out[b], normed).then_inc(y_stored, 16)
            sp.wait_ge(y_stored, 16 * NB)
            for s in stored:
                sp.wait_ge(s, 16 * H)

        @block.gpsimd
        def _(pool):
            n = [0]

            def const(ins):
                n[0] += 1
                ins.then_inc(pool_init, 1)
                pool.wait_ge(pool_init, n[0])

            def hide(tile, fill, pattern, base, mult, op=ALU.is_ge):
                const(pool.affine_select(out=tile, in_=tile, pattern=pattern, compare_op=op, fill=fill,
                                         base=base, channel_multiplier=mult))

            def only_own_stream(tile, fill):
                t = tile.rearrange("p (b j) -> p b j", b=STREAMS)
                hide(t, fill, [[-FRAMES, STREAMS], [0, FRAMES]], 0, 1)
                hide(t, fill, [[FRAMES, STREAMS], [0, FRAMES]], FRAMES - 1, -1)

            const(pool.memset(qd_half[0][64:P, :], 0.0))
            const(pool.memset(qd_half[1][0:64, :], 0.0))
            const(pool.memset(ident[:, :], 0.0))
            hide(ident[:, :], 1.0, [[-1, P]], 0, 1, ALU.not_equal)
            const(pool.memset(ident_alpha[:, :], 0.0))
            hide(ident_alpha[:, :], ALPHA, [[-1, P]], 0, 1, ALU.not_equal)
            const(pool.memset(mean_mat[:, :], 1.0 / P))
            const(pool.memset(zeros[:, :], 0.0))
            const(pool.memset(eps[:, :], EPS))
            for h in range(H):
                const(pool.memset(slopes[:, h:h + 1], 2.0 ** (-8.0 * (h + 1) / H)))
            const(pool.iota(iota16[:, :], [[1, K]], base=0, channel_multiplier=0,
                            allow_small_or_imprecise_dtypes=True))
            const(pool.iota(ramp[:, :], [[-1, 256]], base=P, channel_multiplier=1,
                            allow_small_or_imprecise_dtypes=True))
            hide(ramp[:, :], 0.0, [[-1, 256]], P, 1)
            const(pool.iota(dist[:, 1, :], [[1, 256]], base=-P, channel_multiplier=-1,
                            allow_small_or_imprecise_dtypes=True))
            hide(dist[:, 1, :], 0.0, [[1, 256]], -P, -1)
            const(pool.tensor_tensor(dist[:, 1, :], dist[:, 1, :], ramp[:, :], ALU.add))
            const(pool.tensor_copy(dist[:, 0, P:256], dist[:, 1, P:256]))
            only_own_stream(dist[:, 0, P:256], HIDDEN)
            const(pool.memset(dist[0:CHUNK, 1, P + CHUNK:256], HIDDEN))
            const(pool.iota(dist[:, 0, 0:P], [[-1, P]], base=P, channel_multiplier=0,
                            allow_small_or_imprecise_dtypes=True))
            const(pool.iota(frame_i[:, :], [[0, 1]], base=0, channel_multiplier=1))
            const(pool.memset(stick_mask[:, :], 0.0))
            for at in (P, 3 * P, 4 * P):
                hide(stick_mask[:, at:at + P], -HIDDEN, [[-1, P]], 0, 1, ALU.is_gt)
            only_own_stream(stick_mask[:, P:256], -HIDDEN)
            assert n[0] == POOL_CONSTS, n[0]

            def store_head(h):
                for s, out in ((1, kd_out), (3, ks_out)):
                    wait_apart(pool, "pool", qk_evacuated, h * 4 + s + 1)
                    pool.dma_start(out[h], qk[:, s, :]).then_inc(stored[s // 2], 16)
                wait_apart(pool, "pool", v_evacuated, h * NB + NB)
                pool.dma_start(v_out[h], v_new).then_inc(stored[2], 16)

            with pool.Fori(0, H) as h:
                store_head(h)

            def take_idx(dst, head_block, head):
                pool.tensor_copy(dst, expert[:, head_block, head, :]).then_inc(idx_copied, 1)

            def gather_u(g, k, par):
                if not isinstance(g, int) or g > 0 or k >= U_SLOTS:
                    wait_apart(pool, "pool", u_dotted, g * K + k - U_SLOTS + 1)
                pool.indirect_dma_start(
                    out=u_row[k % U_SLOTS], out_offset=None, in_=peer_u,
                    in_offset=bass.IndirectOffsetOnAxis(ap=idx_u[:, par, k:k + 1], axis=0),
                ).then_inc(u_loaded[k % U_SLOTS], 16)

            def gather_v(g, k, par):
                if not isinstance(g, int) or g > 0 or k >= V_SLOTS:
                    wait_apart(pool, "pool", v_added, g * K + k - V_SLOTS + 1)
                pool.indirect_dma_start(
                    out=v_row[k % V_SLOTS], out_offset=None, in_=peer_v,
                    in_offset=bass.IndirectOffsetOnAxis(ap=idx_v[:, par, k:k + 1], axis=0),
                ).then_inc(v_loaded[k % V_SLOTS], 16)

            pool.wait_ge(gates_ready, H)
            pool.wait_ge(query_done, 2 * H)
            take_idx(idx_u[:, 0, :], 0, 0)
            pool.wait_ge(idx_copied, 1)
            for k in range(K):
                gather_u(0, k, 0)

            def step(b, i, par, last):
                g = b * H + i
                first = isinstance(g, int) and g == 0
                if not last:
                    if not first:
                        wait_apart(pool, "pool", u_dotted, g * K)
                    nb, ni = (b + 1, 0) if isinstance(i, int) and i == H - 1 else (b, i + 1)
                    take_idx(idx_u[:, 1 - par, :], nb, ni)
                if not first and not (isinstance(g, int) and g == 1):
                    wait_apart(pool, "pool", v_added, (g - 1) * K)
                take_idx(idx_v[:, par, :], b, i)
                wait_apart(pool, "pool", idx_copied, g * 2 + (2 if last else 3))
                for k in range(K):
                    gather_v(g, k, par)
                    if not last:
                        gather_u(g + 1, k, 1 - par)

            for b in range(NB):
                step(b, 0, 0, False)
                step(b, 1, 1, False)
                with pool.Fori(1, H // 2 - 1) as pair:
                    step(b, pair * 2, 0, False)
                    step(b, pair * 2 + 1, 1, False)
                step(b, H - 2, 0, False)
                step(b, H - 1, 1, b == NB - 1)

        @block.scalar
        def _(act):
            for s in (oT_copied, sticks_ready, query_copied, key_copied):
                act.sem_inc(s, LEAD)
            act.wait_ge(dve_init, 2)
            act.activation(lam_exp[:, :], lam_dot[:, :], ACT.Exp).then_inc(act_init, 1)

            def copy_qk(h, s):
                act.wait_ge(qk_projected, h * 4 + s + 1)
                if s in (1, 3) and not (isinstance(h, int) and h == 0):
                    act.wait_ge(stored[s // 2], h * 16)
                src = bank[5 + s % 3][:, 0:T]
                if s == 0:
                    act.activation(qd_half[0][0:64, :], src[0:64, :], ACT.Copy, scale=DIFF_SCALE)\
                       .then_inc(qd_half_copied, 1)
                    act.activation(qd_half[1][64:P, :], src[64:P, :], ACT.Copy, scale=DIFF_SCALE)\
                       .then_inc(qk_evacuated, 1)
                else:
                    act.activation(qk[:, s, :], src, ACT.Copy).then_inc(qk_evacuated, 1)

            def copy_v(h):
                for b in range(NB):
                    act.wait_ge(v_projected, h * NB + b + 1)
                    if b == 0 and not (isinstance(h, int) and h == 0):
                        act.wait_ge(stored[2], h * 16)
                    act.activation(v_new[:, b, :], bank[5 + (4 + b) % 3][:, 0:256], ACT.Copy)\
                       .then_inc(v_evacuated, 1)

            def attend(h, ahead):
                act.wait_ge(pastT_scored, h + 1)
                act.activation(pastT, pastT_ps, ACT.Copy).then_inc(pastT_copied, 1)
                for b in range(NB):
                    act.wait_ge(min_ready, h * NB + b + 1)
                    lo = P if b == 1 else 0
                    for c in range(2):
                        act.activation(probs[:, b, c, lo:256], probs[:, b, c, lo:256], ACT.Exp,
                                       bias=row_min[:, b, c:c + 1], scale=-1.0,
                                       accum_out=row_sum[:, b, c:c + 1]).then_inc(probs_ready, 1)
                if ahead:
                    copy_qk(h + 1, 0)
                act.wait_ge(neg_abs_ready, h + 1)
                act.activation(soft, soft, ACT.Exp).then_inc(soft_ready, 1)
                act.wait_ge(soft_ready, h * 2 + 1)
                act.activation(soft, soft, ACT.Ln, bias=1.0).then_inc(soft_ready, 1)
                if ahead:
                    copy_qk(h + 1, 1)
                act.wait_ge(exponent_ready, h + 1)
                act.activation(sticks.rearrange("p s n -> p (s n)"), suffix, ACT.Exp).then_inc(sticks_ready, 1)
                if ahead:
                    copy_qk(h + 1, 2)
                    copy_qk(h + 1, 3)
                act.wait_ge(transposed, h + 1 + LEAD)
                for j, (lo, hi) in enumerate(((0, 3), (3, 6), (6, 10))):
                    act.activation(weightsT[:, lo:hi, :].rearrange("p s n -> p (s n)"), wT_ps[j], ACT.Copy)\
                       .then_inc(wT_copied, 1)
                act.wait_ge(values_done, h + 1)
                act.activation(mixedT[:, h, :], oT_ps[0], ACT.Copy).then_inc(oT_copied, 1)
                act.activation(mixedT[:, h + H, :], oT_ps[1], ACT.Copy).then_inc(oT_copied, 1)
                if ahead:
                    copy_v(h + 1)

            for s in range(4):
                copy_qk(0, s)
            copy_v(0)
            with act.Fori(0, H - 1) as h:
                attend(h, True)
            attend(H - 1, False)

            act.wait_ge(oT_copied, 2 * H + LEAD)
            mixed_diff = mixedT[:, 0:H, :].rearrange("p t n -> p (t n)")
            for j in range(6):
                act.activation(squares[:, j * 512:(j + 1) * 512], mixed_diff[:, j * 512:(j + 1) * 512],
                               ACT.Square).then_inc(squared, 1)
            for j in range(6):
                act.wait_ge(meaned, j + 1)
                act.activation(squares[:, j * 512:(j + 1) * 512], bank[3 + j % 5][:, :], ACT.Sqrt,
                               bias=eps[:, :]).then_inc(rms_ready, 1)

            act.wait_ge(ln1_step, 1)
            act.activation(stdev[:, :], moments[:, :, 1], ACT.Sqrt, bias=eps[:, :]).then_inc(ln1_sd, 1)
            act.wait_ge(ln1_step, 3)
            for b in range(NB):
                act.activation(x1[:, b, :], x1[:, b, :], ACT.Identity, scale=rstd[:, b:b + 1],
                               bias=shift[:, b:b + 1]).then_inc(ln1_scaled, 1)
            for b in range(NB):
                for j in range(4):
                    act.wait_ge(x1_transposed, b * 4 + j + 1)
                    act.activation(x1T[:, 4 * j:4 * j + 4, b * P:(b + 1) * P],
                                   bank[(b * 4 + j) % 4][:, :].rearrange("p (t n) -> p t n", t=4),
                                   ACT.Copy).then_inc(x1T_copied, 1)

            with act.Fori(0, H) as h:
                for c in range(2):
                    act.wait_ge(query_done, h * 2 + c + 1)
                    act.activation(queryT[:, c, :], bank[4 + c][:, 0:T], ACT.Copy).then_inc(query_copied, 1)
                for c in range(2):
                    act.wait_ge(key_scored, h * 2 + c + 1)
                    act.wait_ge(half_read, h + LEAD)
                    act.activation(key_scores[:, c, :, :].rearrange("p b k -> p (b k)"), bank[6 + c][:, 0:T],
                                   ACT.Copy).then_inc(key_copied, 1)
                act.wait_ge(over_ready, h + 1)
                act.activation(expo[:, :, :], over_max[:, :, :], ACT.Exp).then_inc(expo_ready, 1)

            def activate(g):
                act.wait_ge(u_dotted, g * K + K)
                act.activation(gelu[:, :], dots[:, :], ACT.Gelu).then_inc(gelu_ready, 1)

            def spread(g, par):
                act.wait_ge(coef_ready, g + 1)
                for k in range(K):
                    if not isinstance(g, int) or g > 0 or k >= DIAGS:
                        act.wait_ge(v_added, g * K + k - DIAGS + 1)
                    act.activation(diag[:, k % DIAGS, :], ident[:, :], ACT.Copy, scale=coef[:, par, k:k + 1])\
                       .then_inc(diag_ready, 1)

            activate(0)
            for b in range(NB):
                for par in range(2):
                    spread(b * H + par, par)
                    activate(b * H + par + 1)
                with act.Fori(1, H // 2 - 1) as pair:
                    g = b * H + pair * 2
                    spread(g, 0)
                    activate(g + 1)
                    spread(g + 1, 1)
                    activate(g + 2)
                g = b * H + H - 2
                spread(g, 0)
                activate(g + 1)
                spread(g + 1, 1)
                if b < NB - 1:
                    activate(g + 2)
                act.wait_ge(ln2_step, b * 3 + 1)
                act.activation(stdev[:, b:b + 1], moments[:, b, 1:2], ACT.Sqrt, bias=eps[:, :]).then_inc(ln2_sd, 1)
                act.wait_ge(ln2_step, b * 3 + 3)
                if b > 0:
                    act.wait_ge(y_stored, 16 * b)
                for j in range(4):
                    act.activation(normed[:, j * 512:(j + 1) * 512], bank[4 * (b % 2) + j][:, :], ACT.Identity,
                                   scale=rstd[:, b:b + 1], bias=shift[:, b:b + 1]).then_inc(ln2_scaled, 1)

        @block.tensor
        def _(pe):
            pe.sem_inc(transposed, LEAD)
            pe.wait_ge(x_loaded, 16)

            def project_qk(h, s):
                pe.wait_ge(w_loaded[s], h * 16 + 16)
                if s == 3:
                    pe.wait_ge(qk_evacuated, h * 4 + 1)
                    pe.wait_ge(qd_half_copied, h + 1)
                elif not isinstance(h, int) or h > 0:
                    pe.wait_ge(v_evacuated, (h - 1) * NB + (3, 1, 2)[s])
                for t in range(DT):
                    mm = pe.matmul(bank[5 + s % 3][:, 0:T], w_slot[s][:, t * P:(t + 1) * P], xT[:, t, :],
                                   start=(t == 0), stop=(t == DT - 1))
                mm.then_inc(qk_projected, 1)

            def project_v(h):
                pe.wait_ge(w_loaded[4], h * 16 + 16)
                for b in range(NB):
                    pe.wait_ge(qk_evacuated, h * 4 + b + 2)
                    for t in range(DT):
                        mm = pe.matmul(bank[5 + (4 + b) % 3][:, 0:256], xT[:, t, b * P:(b + 1) * P], w_v[:, t, :],
                                       start=(t == 0), stop=(t == DT - 1))
                    mm.then_inc(v_projected, 1)

            def scores(h):
                pe.wait_ge(qk_evacuated, h * 4 + 4)
                pe.wait_ge(qd_half_copied, h + 1)
                pe.wait_ge(oT_copied, 2 * h + LEAD)
                pe.wait_ge(past_loaded[0], h * 16 + 16)
                pe.wait_ge(past_loaded[1], h * 16 + 16)
                for j in range(STREAMS):
                    own = slice(j * FRAMES, (j + 1) * FRAMES)
                    for c in range(2):
                        pe.matmul(pastT_ps[:, c, own], kd_past[:, j, :], qd_half[c][:, own], start=True, stop=True)
                    mm = pe.matmul(pastT_ps[:, 2, own], ks_past[:, j, :], qk[:, 2, own], start=True, stop=True)
                mm.then_inc(pastT_scored, 1)
                for b in range(NB):
                    q = slice(b * P, (b + 1) * P)
                    k = slice(P, 3 * P) if b == 2 else q
                    n = k.stop - k.start
                    lo = {0: P, 1: 0, 2: 0}[b]
                    width = P if b == 1 else 256
                    for c in range(2):
                        pe.matmul(diff_ps[b][:, c * width + lo:c * width + lo + n], qd_half[c][:, q], qk[:, 1, k],
                                  start=True, stop=True)
                    out = {0: bank[3][:, P:256], 1: stick1_ps, 2: bank[3][:, 256:512]}[b]
                    pe.matmul(out, qk[:, 2, q], qk[:, 3, k], start=True, stop=True)
                pe.wait_ge(pastT_copied, h + 1)
                pe.transpose(diff_ps[0][:, 0:P], pastT[:, 0, :], ident[:, :])
                pe.transpose(diff_ps[0][:, 256:256 + P], pastT[:, 1, :], ident[:, :])
                pe.transpose(bank[3][:, 0:P], pastT[:, 2, :], ident[:, :]).then_inc(scores_ready, 1)

            order = [(weights, 0), (weights, 1), (weights, 2), (weights, 3), (weights, 4), (sticks, 4),
                     (sticks, 0), (sticks, 1), (sticks, 2), (sticks, 3)]

            def turn(h):
                pe.wait_ge(scores_read, h * 5 + 5)
                pe.wait_ge(weights_ready, h * NB + NB)
                pe.wait_ge(sticks_ready, h + 1 + LEAD)
                for n, (src, slot) in enumerate(order):
                    at, first = (0, 0) if n < 3 else (1, 3) if n < 6 else (2, 6)
                    mm = pe.transpose(wT_ps[at][:, (n - first) * P:(n - first + 1) * P], src[:, slot, :], ident[:, :])
                mm.then_inc(transposed, 1)

            def values(h):
                pe.wait_ge(wT_copied, h * 3 + 3)
                pe.wait_ge(v_evacuated, h * NB + NB)
                pe.wait_ge(past_loaded[2], h * 16 + 16)
                pe.wait_ge(past_loaded[3], h * 16 + 16)
                for kind, past in enumerate((vd_past, vs_past)):
                    o = oT_ps[kind]
                    d = slice(kind * P, (kind + 1) * P)
                    past0, own0, own1, past2, own2 = ((0, 1, 2, 3, 4), (6, 7, 5, 8, 9))[kind]
                    pe.matmul(o[:, 0:P], v_new[:, 0, d], weightsT[:, own0, :], start=True, stop=False,
                              skip_group_check=True)
                    for j in range(STREAMS):
                        own = slice(j * FRAMES, (j + 1) * FRAMES)
                        pe.matmul(o[:, own], past[:, j, :], weightsT[:, past0, own], start=False,
                                  stop=(j == STREAMS - 1), skip_group_check=True)
                    pe.matmul(o[:, P:2 * P], v_new[:, 1, d], weightsT[:, own1, :], start=True, stop=True,
                              skip_group_check=True)
                    pe.matmul(o[:, 2 * P:T], v_new[:, 1, d], weightsT[:, past2, :], start=True, stop=False,
                              skip_group_check=True)
                    mm = pe.matmul(o[:, 2 * P:T], v_new[:, 2, d], weightsT[:, own2, :], start=False, stop=True,
                                   skip_group_check=True)
                mm.then_inc(values_done, 1)

            for s in range(4):
                project_qk(0, s)
            project_v(0)
            pe.wait_ge(pool_init, POOL_CONSTS)
            with pe.Fori(0, H - 1) as h:
                scores(h)
                for s in range(4):
                    project_qk(h + 1, s)
                turn(h)
                project_v(h + 1)
                values(h)
            scores(H - 1)
            turn(H - 1)
            values(H - 1)

            pe.wait_ge(oT_copied, 2 * H + LEAD)
            for j in range(6):
                pe.wait_ge(squared, j + 1)
                if j == 5:
                    pe.wait_ge(rms_ready, 1)
                pe.matmul(bank[3 + j % 5][:, :], mean_mat[:, :], squares[:, j * 512:(j + 1) * 512], start=True,
                          stop=True).then_inc(meaned, 1)

            with pe.Fori(0, 4) as n:
                for g in range(4):
                    pe.wait_ge(wo_loaded[g], n * 16 + 16)
                    if g == 2:
                        pe.wait_ge(diff_normed, 6)
                    for b in range(NB):
                        if g == 0:
                            pe.wait_ge(residual_ready[b], n + LEAD)
                        for e in range(4):
                            tile = ((g + 2) % 4) * 4 + e
                            mm = pe.matmul(bank[b][:, :], mixedT[:, tile, b * P:(b + 1) * P],
                                           w_slot[g][:, e * 512:(e + 1) * 512],
                                           start=(g == 0 and e == 0), stop=(g == 3 and e == 3))
                        if g == 3:
                            mm.then_inc(out_projected, 1)
                    if g < 3:
                        mm.then_inc(wo_used, 1)

            for b in range(NB):
                pe.wait_ge(ln1_done, b + 1)
                for j in range(4):
                    n = b * 4 + j
                    if n >= 4:
                        pe.wait_ge(x1T_copied, n - 3)
                    for t in range(4):
                        mm = pe.transpose(bank[n % 4][:, t * P:(t + 1) * P],
                                          x1[:, b, (4 * j + t) * P:(4 * j + t + 1) * P], ident[:, :])
                    mm.then_inc(x1_transposed, 1)

            pe.wait_ge(x1T_copied, 4 * NB)
            pe.wait_ge(subkeys_loaded, 16)
            with pe.Fori(0, H) as h:
                for c in range(2):
                    pe.wait_ge(wq_loaded[c], h * 16 + 16)
                    pe.wait_ge(query_copied, h * 2 + LEAD)
                    for t in range(DT):
                        mm = pe.matmul(bank[4 + c][:, 0:T], w_slot[4 + c][:, t * P:(t + 1) * P], x1T[:, t, :],
                                       start=(t == 0), stop=(t == DT - 1))
                    mm.then_inc(query_done, 1)
                for c in range(2):
                    pe.wait_ge(query_copied, h * 2 + c + 1 + LEAD)
                    pe.wait_ge(key_copied, h * 2 + LEAD)
                    for b in range(NB):
                        mm = pe.matmul(bank[6 + c][:, b * P:(b + 1) * P], queryT[:, c, b * P:(b + 1) * P],
                                       subkT[:, h * 2 + c, :], start=True, stop=True)
                    mm.then_inc(key_scored, 1)

            def add_rows(g, half):
                for k in range(K):
                    pe.wait_ge(diag_ready, g * K + k + 1)
                    pe.wait_ge(v_loaded[k % V_SLOTS], (g * (K // V_SLOTS) + k // V_SLOTS) * 16 + 16)
                    for j in range(4):
                        mm = pe.matmul(bank[4 * half + j][:, :], diag[:, k % DIAGS, :],
                                       v_row[k % V_SLOTS][:, j * 512:(j + 1) * 512], start=False, stop=True,
                                       skip_group_check=True)
                    mm.then_inc(v_added, 1)

            pe.wait_ge(key_copied, 2 * H + LEAD)
            for b in range(NB):
                half = b % 2
                if b >= 2:
                    pe.wait_ge(ln2_scaled, 4 * (b - 1))
                for j in range(4):
                    pe.matmul(bank[4 * half + j][:, :], ident_alpha[:, :], x1[:, b, j * 512:(j + 1) * 512],
                              start=True, stop=False, skip_group_check=True)
                with pe.Fori(0, H) as i:
                    add_rows(b * H + i, half)

        @block.vector
        def _(dve):
            for s in (half_read, *residual_ready):
                dve.sem_inc(s, LEAD)
            dve.wait_ge(consts_loaded, 32)
            for i in range(2):
                dve.tensor_tensor_reduce(lam_prod[:, i, :], lam_in[:, 2 * i, :], lam_in[:, 2 * i + 1, :], 1.0, 0.0,
                                         ALU.mult, ALU.add, lam_dot[:, i:i + 1]).then_inc(dve_init, 1)
            dve.wait_ge(pool_init, POOL_CONSTS)
            dve.tensor_scalar(frame_i[:, :], frame_i[:, :], FRAMES - 1, None, ALU.bitwise_and).then_inc(dve_init, 1)
            dve.wait_ge(dve_init, 3)
            dve.tensor_copy(frame_f[:, :], frame_i[:, :]).then_inc(dve_init, 1)
            dve.tensor_scalar(gain8[:, :], gain[:, :], 1.0 - LAM_INIT, None, ALU.mult).then_inc(dve_init, 1)
            dve.wait_ge(dve_init, 5)
            dve.tensor_scalar(dist[:, 0, 0:P], dist[:, 0, 0:P], frame_f[:, 0:1], None, ALU.add).then_inc(dve_init, 1)
            dve.wait_ge(act_init, 1)
            dve.tensor_tensor(lam_diff[:, :], lam_exp[:, 1:2], lam_exp[:, 0:1], ALU.subtract).then_inc(dve_init, 1)
            dve.wait_ge(dve_init, 7)
            dve.tensor_scalar(neg_lam[:, :], lam_diff[:, :], -LAM_INIT, None, ALU.add).then_inc(dve_init, 1)
            dve.wait_ge(dve_init, 8)

            def attend(h):
                dve.wait_ge(scores_ready, h + 1)
                for b in range(NB):
                    lo = P if b == 1 else 0
                    d = dist[:, min(b, 1):min(b, 1) + 1, lo:256].to_broadcast([P, 2, 256 - lo])
                    dve.scalar_tensor_tensor(
                        out=probs[:, b, :, lo:256], in0=d, scalar=slopes[:, bass.ds(h, 1)],
                        in1=diff_ps[b].rearrange("p (c n) -> p c n", c=2), op0=ALU.mult,
                        op1=ALU.subtract).then_inc(scores_read, 1)
                dve.scalar_tensor_tensor(out=logit[:, 0:512], in0=stick02_ps, scalar=SB_SCALE,
                                         in1=stick_mask[:, 0:512], op0=ALU.mult, op1=ALU.add).then_inc(scores_read, 1)
                dve.scalar_tensor_tensor(out=logit[:, 512:640], in0=stick1_ps, scalar=SB_SCALE,
                                         in1=stick_mask[:, 512:640], op0=ALU.mult, op1=ALU.add)\
                   .then_inc(scores_read, 1)
                for b in range(NB):
                    lo = P if b == 1 else 0
                    dve.wait_ge(scores_read, h * 5 + b + 1)
                    dve.tensor_reduce(row_min[:, b, :], probs[:, b, :, lo:256], AX_X, ALU.min).then_inc(min_ready, 1)
                dve.wait_ge(scores_read, h * 5 + 5)
                dve.scalar_tensor_tensor(out=soft, in0=logit, scalar=-1.0, in1=logit, op0=ALU.mult,
                                         op1=ALU.min).then_inc(neg_abs_ready, 1)
                dve.wait_ge(probs_ready, h * 6 + 6)
                dve.reciprocal(row_inv[:, :, :], row_sum[:, :, :]).then_inc(inv_ready, 1)
                dve.wait_ge(inv_ready, h * 2 + 1)
                dve.tensor_scalar(lam_inv[:, :, :], row_inv[:, :, 1:2], neg_lam[:, 0:1], None, ALU.mult)\
                   .then_inc(inv_ready, 1)
                dve.wait_ge(transposed, h + LEAD)
                for b in range(NB):
                    lo = P if b == 1 else 0
                    w = weights[:, (0, 2, 3)[b]:(2, 3, 5)[b], :].rearrange("p s n -> p (s n)")
                    dve.tensor_scalar(w, probs[:, b, 0, lo:256], row_inv[:, b, 0:1], None, ALU.mult)\
                       .then_inc(half_weights, 1)
                dve.wait_ge(inv_ready, h * 2 + 2)
                for b in range(NB):
                    lo = P if b == 1 else 0
                    w = weights[:, (0, 2, 3)[b]:(2, 3, 5)[b], :].rearrange("p s n -> p (s n)")
                    dve.wait_ge(half_weights, h * NB + b + 1)
                    dve.scalar_tensor_tensor(out=w, in0=probs[:, b, 1, lo:256], scalar=lam_inv[:, b, 0:1], in1=w,
                                             op0=ALU.mult, op1=ALU.add).then_inc(weights_ready, 1)
                dve.wait_ge(soft_ready, h * 2 + 2)
                dve.scalar_tensor_tensor(out=soft, in0=logit, scalar=0.0, in1=soft, op0=ALU.max, op1=ALU.add)\
                   .then_inc(softplus_ready, 1)
                dve.wait_ge(softplus_ready, h + 1)
                dve.wait_ge(sticks_ready, h + LEAD)
                for lo, hi in ((0, 256), (256, 512), (512, 640)):
                    back = slice(hi - 1, lo - 1 if lo else None, -1)
                    dve.tensor_tensor_scan(suffix[:, back], soft[:, back], zeros[:, 0:hi - lo], 0.0, ALU.add,
                                           ALU.add).then_inc(suffix_ready, 1)
                dve.wait_ge(suffix_ready, h * 3 + 3)
                dve.tensor_tensor(suffix, logit, suffix, ALU.subtract).then_inc(exponent_ready, 1)

            with dve.Fori(0, H) as h:
                attend(h)

            for j in range(6):
                cols = slice(j * 512, (j + 1) * 512)
                dve.wait_ge(rms_ready, j + 1)
                dve.reciprocal(squares[:, cols], squares[:, cols]).then_inc(rms_inv, 1)
            for j in range(6):
                cols = slice(j * 512, (j + 1) * 512)
                mixed_diff = mixedT[:, 0:H, :].rearrange("p t n -> p (t n)")[:, cols]
                dve.wait_ge(rms_inv, j + 1)
                dve.scalar_tensor_tensor(out=mixed_diff, in0=mixed_diff, scalar=gain8[:, 0:1],
                                         in1=squares[:, cols], op0=ALU.mult, op1=ALU.mult).then_inc(diff_normed, 1)

            dve.wait_ge(rows_loaded, 16)
            with dve.Fori(0, 4) as n:
                for b in range(NB):
                    part = x1[:, b, :].rearrange("p (n c) -> p n c", n=4)[:, n, :]
                    dve.wait_ge(out_projected, n * NB + b + 1)
                    dve.scalar_tensor_tensor(out=part, in0=part, scalar=ALPHA, in1=bank[b][:, :], op0=ALU.mult,
                                             op1=ALU.add).then_inc(residual_ready[b], 1)
                    dve.wait_ge(residual_ready[b], n + 1 + LEAD)
                    dve.bn_stats(stats[:, b, n, :], part).then_inc(stats_ready, 1)
            dve.wait_ge(stats_ready, 4 * NB)
            for b in range(NB):
                ins = dve.bn_aggr(moments[:, b, :], stats[:, b, :, :].rearrange("p n s -> p (n s)"))
            ins.then_inc(ln1_step, 1)
            dve.wait_ge(ln1_sd, 1)
            dve.reciprocal(rstd[:, :], stdev[:, :]).then_inc(ln1_step, 1)
            dve.wait_ge(ln1_step, 2)
            dve.scalar_tensor_tensor(out=shift[:, :], in0=moments[:, :, 0], scalar=-1.0, in1=rstd[:, :],
                                     op0=ALU.mult, op1=ALU.mult).then_inc(ln1_step, 1)
            dve.wait_ge(ln_loaded, 16)
            for b in range(NB):
                dve.wait_ge(ln1_scaled, b + 1)
                dve.tensor_tensor(x1[:, b, :], x1[:, b, :], ln_rows[:, 0, :], ALU.mult).then_inc(ln1_step, 1)
                dve.wait_ge(ln1_step, 4 + b)
                dve.tensor_tensor(x1[:, b, :], x1[:, b, :], ln_rows[:, 1, :], ALU.add).then_inc(ln1_done, 1)

            PER = 59

            def choose(h):
                n = [0]

                def ahead(ins):
                    n[0] += 1
                    ins.then_inc(topk_step, 1)

                def settle():
                    wait_apart(dve, "dve", topk_step, h * PER + n[0])

                wait_apart(dve, "dve", key_copied, h * 2 + 2 + LEAD)
                pairs = [(c, b) for c in range(2) for b in range(NB)]
                for c, b in pairs:
                    ahead(dve.max(half_top[:, c, b, 0:8], key_scores[:, c, b, :]))
                settle()
                for c, b in pairs:
                    ahead(dve.match_replace(rest[:, c, b, :], half_top[:, c, b, 0:8], key_scores[:, c, b, :], LOW))
                for c, b in pairs:
                    ahead(dve.max_index(half_idx[:, c, b, 0:8], half_top[:, c, b, 0:8], key_scores[:, c, b, :]))
                settle()
                for c, b in pairs:
                    ahead(dve.max(half_top[:, c, b, 8:16], rest[:, c, b, :]))
                settle()
                for c, b in pairs:
                    ins = dve.max_index(half_idx[:, c, b, 8:16], half_top[:, c, b, 8:16], rest[:, c, b, :])
                    if (c, b) != pairs[-1]:
                        ahead(ins)
                    else:
                        ins.then_inc(half_read, 1)
                ahead(dve.tensor_tensor(
                    cand, half_top[:, 0, :, :].rearrange("p b (i o) -> p b i o", o=1).to_broadcast([P, NB, K, K]),
                    half_top[:, 1, :, :].rearrange("p b (o j) -> p b o j", o=1).to_broadcast([P, NB, K, K]), ALU.add))
                settle()
                dve.wait_ge(half_read, h + 1 + LEAD)
                ahead(dve.tensor_copy(half_idx_f[:, :, :, :], half_idx[:, :, :, :]))
                sums = [cand[:, b, :, :].rearrange("p i j -> p (i j)") for b in range(NB)]
                left = [cand_rest[:, b, :, :].rearrange("p i j -> p (i j)") for b in range(NB)]
                for b in range(NB):
                    ahead(dve.max(top[:, b, 0:8], sums[b]))
                settle()
                for b in range(NB):
                    ahead(dve.match_replace(left[b], top[:, b, 0:8], sums[b], LOW))
                for b in range(NB):
                    ahead(dve.max_index(top_pos[:, b, 0:8], top[:, b, 0:8], sums[b]))
                settle()
                for b in range(NB):
                    ahead(dve.max(top[:, b, 8:16], left[b]))
                settle()
                dve.tensor_tensor(over_max[:, :, :], top[:, :, :], top[:, :, 0:1].to_broadcast([P, NB, K]),
                                  ALU.subtract).then_inc(over_ready, 1)
                for b in range(NB):
                    ahead(dve.max_index(top_pos[:, b, 8:16], top[:, b, 8:16], left[b]))
                settle()
                ahead(dve.tensor_scalar(pos_ij[:, 0, :, :], top_pos[:, :, :], 4, None, ALU.logical_shift_right))
                ahead(dve.tensor_scalar(pos_ij[:, 1, :, :], top_pos[:, :, :], K - 1, None, ALU.bitwise_and))
                settle()
                ahead(dve.tensor_copy(pos_ij_f[:, :, :, :], pos_ij[:, :, :, :]))
                settle()
                steps = iota16[:, :].rearrange("p (a b k) -> p a b k", a=1, b=1).to_broadcast([P, NB, K, K])
                for c in range(2):
                    ahead(dve.tensor_tensor(
                        hit[:, c], pos_ij_f[:, c, :, :].rearrange("p b (i o) -> p b i o", o=1)
                        .to_broadcast([P, NB, K, K]), steps, ALU.is_equal))
                settle()
                for c in range(2):
                    ahead(dve.tensor_tensor(
                        hit[:, c], hit[:, c], half_idx_f[:, c, :, :].rearrange("p b (o j) -> p b o j", o=1)
                        .to_broadcast([P, NB, K, K]), ALU.mult))
                settle()
                for c in range(2):
                    ahead(dve.tensor_reduce(picked[:, c, :, :], hit[:, c], AX_X, ALU.add))
                settle()
                ahead(dve.scalar_tensor_tensor(out=expert_f[:, :, :], in0=picked[:, 0, :, :], scalar=float(KEYS),
                                               in1=picked[:, 1, :, :], op0=ALU.mult, op1=ALU.add))
                dve.wait_ge(expo_ready, h + 1)
                ahead(dve.tensor_reduce(expo_sum[:, :], expo[:, :, :], AX_X, ALU.add))
                settle()
                ahead(dve.tensor_copy(expert[:, :, h, :], expert_f[:, :, :]))
                ahead(dve.reciprocal(expo_inv[:, :], expo_sum[:, :]))
                settle()
                assert n[0] == PER, n[0]
                dve.tensor_tensor(gate[:, :, h, :], expo[:, :, :],
                                  expo_inv[:, :].rearrange("p (b o) -> p b o", o=1).to_broadcast([P, NB, K]),
                                  ALU.mult).then_inc(gates_ready, 1)

            for s in stored:
                dve.wait_ge(s, 16 * H)
            with dve.Fori(0, H) as h:
                choose(h)
            dve.wait_ge(gates_ready, H)

            def dot_rows(b, g):
                if not isinstance(g, int) or g > 0:
                    dve.wait_ge(gelu_ready, g)
                for k in range(K):
                    slot = k % U_SLOTS
                    dve.wait_ge(u_loaded[slot], (g * (K // U_SLOTS) + k // U_SLOTS) * 16 + 16)
                    dve.tensor_tensor_reduce(u_row[slot], u_row[slot], x1[:, b, :], 1.0, 0.0, ALU.mult, ALU.add,
                                             dots[:, k:k + 1]).then_inc(u_dotted, 1)

            def weigh(b, i, par):
                g = b * H + i
                dve.wait_ge(gelu_ready, g + 1)
                if not isinstance(g, int) or g > 1:
                    dve.wait_ge(diag_ready, (g - 1) * K)
                dve.tensor_tensor(coef[:, par, :], gelu[:, :], gate[:, b, i, :], ALU.mult).then_inc(coef_ready, 1)

            dot_rows(0, 0)
            weigh(0, 0, 0)
            for b in range(NB):
                g0 = b * H
                dot_rows(b, g0 + 1)
                weigh(b, 1, 1)
                with dve.Fori(1, H // 2) as pair:
                    dot_rows(b, g0 + pair * 2)
                    weigh(b, pair * 2, 0)
                    dot_rows(b, g0 + pair * 2 + 1)
                    weigh(b, pair * 2 + 1, 1)
                if b < NB - 1:
                    dot_rows(b + 1, g0 + H)
                    weigh(b + 1, 0, 0)
                dve.wait_ge(v_added, (b + 1) * H * K)
                for j in range(4):
                    ins = dve.bn_stats(stats[:, b, j, :], bank[4 * (b % 2) + j][:, :])
                    ins.then_inc(stats_ready, 1)
                dve.wait_ge(stats_ready, 4 * NB + 4 * (b + 1))
                dve.bn_aggr(moments[:, b, :], stats[:, b, :, :].rearrange("p n s -> p (n s)")).then_inc(ln2_step, 1)
                dve.wait_ge(ln2_sd, b + 1)
                dve.reciprocal(rstd[:, b:b + 1], stdev[:, b:b + 1]).then_inc(ln2_step, 1)
                dve.wait_ge(ln2_step, b * 3 + 2)
                dve.scalar_tensor_tensor(out=shift[:, b:b + 1], in0=moments[:, b, 0:1], scalar=-1.0,
                                         in1=rstd[:, b:b + 1], op0=ALU.mult, op1=ALU.mult).then_inc(ln2_step, 1)
                dve.wait_ge(ln_loaded, 32)
                dve.wait_ge(ln2_scaled, 4 * (b + 1))
                dve.tensor_tensor(normed, normed, ln_rows[:, 0, :], ALU.mult).then_inc(ln2_weighted, 1)
                dve.wait_ge(ln2_weighted, b + 1)
                dve.tensor_tensor(normed, normed, ln_rows[:, 1, :], ALU.add).then_inc(y_ready, 1)


def kernel(x_prompt, x_sample, cache_diff_k, cache_diff_v, cache_sb_k, cache_sb_v, w_in, w_out, lam_q1, lam_k1,
           lam_q2, lam_k2, subln_g, ln1_g, ln1_b, ln2_g, ln2_b, peer_w_q, peer_subkeys, peer_u, peer_v):
    import numpy as np
    import concourse.bacc as bacc
    from concourse.bass_utils import run_bass_kernel_spmd

    a = np.asarray
    x = np.concatenate([a(x_sample).reshape(P, D), a(x_prompt).reshape(2 * P, D)])
    w = a(w_in)[0]
    cols = lambda k: w[:, k * 1024:(k + 1) * 1024].reshape(DT, P, H, P).transpose(2, 1, 0, 3)
    qd, kd, vd, qs, ks, vs = (cols(k) for k in range(6))
    w_heads = np.concatenate([z.reshape(H, P, ROW) for z in (qd, kd, qs, ks)]
                             + [np.concatenate([vd, vs], axis=3).reshape(H, P, 2 * ROW)], axis=2)
    keysT = lambda z: a(z)[0].reshape(STREAMS, P, H, P).transpose(2, 3, 0, 1).reshape(H, P, STREAMS * P)
    rowsT = lambda z: a(z)[0].reshape(STREAMS, P, H, P).transpose(2, 1, 0, 3).reshape(H, P, STREAMS * P)
    wo = a(w_out)[0].reshape(4, 4, P, 4, 512).transpose(3, 0, 2, 1, 4)[:, [2, 3, 0, 1]].reshape(4, 4, P, ROW)
    wq = a(peer_w_q)[0].reshape(DT, P, 2 * H, P).transpose(2, 1, 0, 3).reshape(2 * H, P, ROW)
    wide = lambda *z: np.broadcast_to(np.stack([a(q)[0] for q in z])[None], (P, len(z), a(z[0]).shape[1]))
    ins = {
        "x_t": x.reshape(T, DT, P).transpose(2, 1, 0).reshape(P, DT * T),
        "x_rows": x.reshape(NB, P, D).transpose(1, 0, 2),
        "w_heads": w_heads,
        "kd_cache": keysT(cache_diff_k), "ks_cache": keysT(cache_sb_k),
        "vd_cache": rowsT(cache_diff_v), "vs_cache": rowsT(cache_sb_v),
        "w_out": wo,
        "lam_vecs": wide(lam_q1, lam_k1, lam_q2, lam_k2),
        "subln": a(subln_g)[0].reshape(P, 1),
        "ln1": wide(ln1_g, ln1_b), "ln2": wide(ln2_g, ln2_b),
        "w_q": wq,
        "subkeys": a(peer_subkeys)[0].reshape(2 * H, KEYS, P).transpose(2, 0, 1),
        "peer_u": a(peer_u)[0], "peer_v": a(peer_v)[0],
    }
    outs = {"y_out": (NB, P, D), "kd_out": (H, P, T), "ks_out": (H, P, T), "v_out": (H, P, NB, 256)}
    nc = bacc.Bacc("TRN2", target_bir_lowering=False, num_devices=1)
    arrays, args = {}, []
    for name, z in ins.items():
        arrays[name] = np.ascontiguousarray(z)
        args.append(nc.dram_tensor(name, z.shape, F32, kind="ExternalInput").ap())
    for name, shape in outs.items():
        args.append(nc.dram_tensor(name, shape, F32, kind="ExternalOutput").ap())
    build(nc, *args)
    r = run_bass_kernel_spmd(nc, [arrays], core_ids=[0]).results[0]

    y = a(r["y_out"]).reshape(T, D)
    kd_new, ks_new = (a(r[n]).reshape(H, P, T).transpose(2, 0, 1) for n in ("kd_out", "ks_out"))
    v_all = a(r["v_out"]).reshape(H, P, NB, 2, P).transpose(2, 1, 3, 0, 4).reshape(T, 2, H, P)
    rows = (kd_new.reshape(T, H, 2, 64), v_all[:, 0], ks_new, v_all[:, 1])
    prompt = [z[P:].reshape((1, 1, 2 * P) + z.shape[1:]) for z in rows]
    sample = [z[:P].reshape((1, STREAMS, FRAMES) + z.shape[1:]) for z in rows]
    out = [y[P:].reshape(1, 2 * P, D), y[:P].reshape(STREAMS, FRAMES, D)] + prompt + sample
    return tuple(np.ascontiguousarray(z) for z in out)
```

```python
import math
from contextlib import ExitStack
from functools import partial

import concourse.bass as bass
from concourse import mybir

F32 = mybir.dt.float32
I32 = mybir.dt.int32
U32 = mybir.dt.uint32
ALU = mybir.AluOpType
ACT = mybir.ActivationFunctionType
AX_X = mybir.AxisListType.X

P = 128
D = 2048
DT = D // P
NB = 3
T = NB * P
H = 8
STREAMS, FRAMES = 8, 16
CHUNK = 64
DIFF_SCALE = 64 ** -0.5
SB_SCALE = 128 ** -0.5
LAM_INIT = 0.8 - 0.6 * math.exp(0.0)
ALPHA = 2.0 ** 0.25
EPS = 1e-5
KEYS = 128
K = 16
EXPERTS = KEYS * KEYS
HIDDEN = 1e30
LOW = -3e38
ROW = 2048
U_SLOTS = V_SLOTS = 4
DIAGS = V_SLOTS
HEADS = NB * H
GROUPS = ((0,), (1, 2))
LANES = 4


def build(nc, x_t, x_rows, w_heads, kd_cache, ks_cache, vd_cache, vs_cache, w_out, lam_vecs, subln,
          ln1, ln2, w_q, subkeys, peer_u, peer_v, y_out, kd_out, ks_out, v_out):
    ctx = ExitStack()
    with ctx:
        def sb(name, shape, dt=F32):
            return ctx.enter_context(nc.sbuf_tensor(name, shape, dt))

        def sem(name):
            return ctx.enter_context(nc.semaphore(name))

        arena = sb("arena", [P, 12, ROW])
        flat = arena[:, :, :].rearrange("p s c -> p (s c)")
        xT = flat[:, 0:DT * T].rearrange("p (t n) -> p t n", t=DT)
        squares = flat[:, 0:H * T]
        x1T = [flat[:, 0:ROW].rearrange("p (t n) -> p t n", t=DT),
               flat[:, ROW:3 * ROW].rearrange("p (t n) -> p t n", t=DT)]
        mixedT = [flat[:, 3 * ROW:4 * ROW].rearrange("p (t n) -> p t n", t=2 * H),
                  flat[:, 4 * ROW:6 * ROW].rearrange("p (t n) -> p t n", t=2 * H)]
        mixed_diff = [flat[:, 3 * ROW + j * 512:3 * ROW + (j + 1) * 512] for j in range(2)] + \
                     [flat[:, 4 * ROW + j * 512:4 * ROW + (j + 1) * 512] for j in range(4)]
        w_slot = [arena[:, 6 + i, :] for i in range(6)]
        w_v = flat[:, 10 * ROW:12 * ROW].rearrange("p (t n) -> p t n", t=DT)

        x1 = sb("x1", [P, NB, D])
        ln_rows = sb("ln_rows", [P, 2, D])
        cache = sb("cache", [P, 4, STREAMS * P])
        kd_past, ks_past, vd_past, vs_past = (cache[:, i, :].rearrange("p (b n) -> p b n", b=STREAMS)
                                              for i in range(4))
        subkT = cache[:, 0:2, :].rearrange("p a n -> p (a n)").rearrange("p (g k) -> p g k", g=2 * H)
        queryT = cache[:, 2, :].rearrange("p (a n) -> p a n", a=2)
        key_scores = cache[:, 3, :].rearrange("p (c l k) -> p c l k", c=2, l=LANES)

        scratch = sb("scratch", [P, 9728])
        taken = [0]

        def cut(n):
            taken[0] += n
            assert taken[0] <= 9728
            return scratch[:, taken[0] - n:taken[0]]

        qk = cut(5 * T).rearrange("p (s n) -> p s n", s=5)
        qd_half = [qk[:, 0, :], qk[:, 4, :]]
        v_new = cut(NB * 256).rearrange("p (b n) -> p b n", b=NB)
        probs = cut(NB * 512).rearrange("p (b c n) -> p b c n", b=NB, c=2)
        weights = cut(5 * P).rearrange("p (s n) -> p s n", s=5)
        sticks = cut(5 * P).rearrange("p (s n) -> p s n", s=5)
        logit = cut(5 * P)
        soft = cut(5 * P)
        suffix = cut(5 * P)
        pastT = cut(3 * P).rearrange("p (s n) -> p s n", s=3)
        weightsT = cut(10 * P).rearrange("p (s n) -> p s n", s=10)
        ramp = cut(256)
        lam_in = cut(4 * 64).rearrange("p (s n) -> p s n", s=4)
        lam_prod = cut(2 * 64).rearrange("p (s n) -> p s n", s=2)
        taken[0] = 0
        rest = cut(2 * LANES * KEYS).rearrange("p (c l k) -> p c l k", c=2, l=LANES)
        sums = cut(2 * LANES * K * K).rearrange("p (c l i j) -> p c l i j", c=2, l=LANES, i=K)
        diag = cut(DIAGS * P).rearrange("p (s n) -> p s n", s=DIAGS)
        spare = [cut(ROW), cut(ROW)]
        normed = cut(D)
        u_row = w_slot[0:U_SLOTS]
        v_row = [arena[:, 3, :], arena[:, 0, :]] + spare
        wq_slot = w_slot[4:6] + spare
        w_pair = w_slot[4:6]

        ident = sb("ident", [P, P])
        ident_alpha = sb("ident_alpha", [P, P])
        mean_mat = sb("mean_mat", [P, P])
        zeros = sb("zeros", [P, 256])
        dist = sb("dist", [P, 2, 256])
        stick_mask = sb("stick_mask", [P, 5 * P])
        slopes = sb("slopes", [P, H])
        frame_i = sb("frame_i", [P, 1], I32)
        frame_f = sb("frame_f", [P, 1])
        eps = sb("eps", [P, 1])
        lam_dot = sb("lam_dot", [P, 2])
        lam_exp = sb("lam_exp", [P, 2])
        lam_diff = sb("lam_diff", [P, 1])
        neg_lam = sb("neg_lam", [P, 1])
        gain = sb("gain", [P, 1])
        gain8 = sb("gain8", [P, 1])
        row_min = sb("row_min", [P, NB, 2])
        row_sum = sb("row_sum", [P, NB, 2])
        row_inv = sb("row_inv", [P, NB, 2])
        lam_inv = sb("lam_inv", [P, NB, 1])
        stats = sb("stats", [P, NB, 4, 6])
        moments = sb("moments", [P, NB, 2])
        stdev = sb("stdev", [P, NB])
        rstd = sb("rstd", [P, NB])
        shift = sb("shift", [P, NB])
        half_top = sb("half_top", [P, 2, LANES, K])
        half_idx = sb("half_idx", [P, 2, LANES, K], U32)
        half_idx_f = sb("half_idx_f", [P, 2, LANES, K])
        top = sb("top", [P, LANES, K])
        top_pos = sb("top_pos", [P, LANES, K], U32)
        pos_ij = sb("pos_ij", [P, 2, LANES, K], U32)
        pos_ij_f = sb("pos_ij_f", [P, 2, LANES, K])
        picked = sb("picked", [P, 2, LANES, K])
        expert_f = sb("expert_f", [P, LANES, K])
        iota16 = sb("iota16", [P, K])
        over_max = sb("over_max", [P, LANES, K])
        expo = sb("expo", [P, LANES, K])
        expo_out = sb("expo_out", [P, LANES, K])
        expo_sum = sb("expo_sum", [P, LANES])
        expo_inv = sb("expo_inv", [P, LANES])
        expert = sb("expert", [P, HEADS, K], U32)
        gate = sb("gate", [P, HEADS, K])
        idx_u = sb("idx_u", [P, 2, K], U32)
        idx_v = sb("idx_v", [P, 2, K], U32)
        dots = sb("dots", [P, K])
        gelu = sb("gelu", [P, K])
        coef = sb("coef", [P, HEADS, K])

        bank = [ctx.enter_context(nc.psum_tensor(f"bank{i}", [P, 512], F32)) for i in range(8)]
        diff_ps = [bank[0][:, :], bank[2][:, 0:256], bank[1][:, :]]
        stick02_ps, stick1_ps = bank[3][:, :], bank[2][:, 256:384]
        pastT_ps = bank[4][:, 0:3 * P].rearrange("p (s n) -> p s n", s=3)
        wT_ps = [bank[0][:, 0:384], bank[1][:, 0:384], bank[2][:, 0:512]]
        oT_ps = [bank[3][:, 0:T], bank[4][:, 0:T]]

        consts_loaded, x_loaded, rows_loaded, ln_loaded, subkeys_loaded = map(
            sem, ("consts_loaded", "x_loaded", "rows_loaded", "ln_loaded", "subkeys_loaded"))
        pool_init, dve_init, act_init = sem("pool_init"), sem("dve_init"), sem("act_init")
        w_loaded = [sem(f"w_loaded{i}") for i in range(5)]
        past_loaded = [sem(f"past_loaded{i}") for i in range(4)]
        stored = [sem(n) for n in ("kd_stored", "ks_stored", "v_stored")]
        qk_projected, v_projected = sem("qk_projected"), sem("v_projected")
        qd_half_copied, qk_evacuated, v_evacuated = sem("qd_half_copied"), sem("qk_evacuated"), sem("v_evacuated")
        pastT_scored, pastT_copied, scores_ready = sem("pastT_scored"), sem("pastT_copied"), sem("scores_ready")
        scores_read, logits_ready = sem("scores_read"), sem("logits_ready")
        min_ready, probs_ready, inv_ready = sem("min_ready"), sem("probs_ready"), sem("inv_ready")
        half_weights, weights_ready = sem("half_weights"), sem("weights_ready")
        neg_abs_ready, soft_ready, softplus_ready = sem("neg_abs_ready"), sem("soft_ready"), sem("softplus_ready")
        suffix_ready, exponent_ready, sticks_ready = sem("suffix_ready"), sem("exponent_ready"), sem("sticks_ready")
        transposed, wT_copied, values_done, oT_copied = (
            sem("transposed"), sem("wT_copied"), sem("values_done"), sem("oT_copied"))
        squared, meaned, rms_ready, rms_inv, diff_normed = (
            sem("squared"), sem("meaned"), sem("rms_ready"), sem("rms_inv"), sem("diff_normed"))
        def sems(name):
            return [sem(f"{name}_block0"), sem(f"{name}_blocks12")]

        wo_loaded = [sem(f"wo_loaded{i}") for i in range(4)]
        wq_loaded = [sem(f"wq_loaded{i}") for i in range(4)]
        pair_loaded = [sem(f"pair_loaded{i}") for i in range(2)]
        wo_used, out_projected, residual_ready, stats_ready = map(
            sems, ("wo_used", "out_projected", "residual_ready", "stats_ready"))
        ln1_step, ln1_sd, ln1_scaled, ln1_done = map(sems, ("ln1_step", "ln1_sd", "ln1_scaled", "ln1_done"))
        x1_transposed, x1T_copied = sems("x1_transposed"), sems("x1T_copied")
        query_done = sems("query_done")
        query_copied, key_scored, key_copied = (
            [[sem(f"{name}_group{g}_head{i}") for i in range(2)] for g in range(2)]
            for name in ("query_copied", "key_scored", "key_copied"))
        half_read, topk_step, over_ready, expo_ready, gates_ready = map(
            sems, ("half_read", "topk_step", "over_ready", "expo_ready", "gates_ready"))
        idx_copied = sem("idx_copied")
        u_loaded = [sem(f"u_loaded{i}") for i in range(U_SLOTS)]
        v_loaded = [sem(f"v_loaded{i}") for i in range(V_SLOTS)]
        u_dotted, gelu_ready, coef_ready, diag_ready, v_added = (
            sem("u_dotted"), sem("gelu_ready"), sem("coef_ready"), sem("diag_ready"), sem("v_added"))
        ln2_stats = sem("ln2_stats")
        ln2_step, ln2_weighted, ln2_sd, ln2_scaled, y_ready, y_stored = (
            sem("ln2_step"), sem("ln2_weighted"), sem("ln2_sd"), sem("ln2_scaled"), sem("y_ready"), sem("y_stored"))

        block = ctx.enter_context(nc.Block())

        LEAD = 1
        POOL_CONSTS = 35

        waits_passed = {"dve": sem("dve_waits_passed"), "pool": sem("pool_waits_passed")}

        def wait_apart(eng, who, signal, value):
            eng.wait_ge(signal, value)
            eng.sem_inc(waits_passed[who], 1)

        @block.sync
        def _(sp):
            def load_head(h):
                for s in range(4):
                    if not isinstance(h, int) or h > 0:
                        sp.wait_ge(qk_projected, (h - 1) * 4 + s + 1)
                    sp.dma_start(w_slot[s], w_heads[h, :, s * ROW:(s + 1) * ROW]).then_inc(w_loaded[s], 16)
                if not isinstance(h, int) or h > 0:
                    sp.wait_ge(v_projected, (h - 1) * NB + NB)
                sp.dma_start(flat[:, 10 * ROW:12 * ROW], w_heads[h, :, 4 * ROW:6 * ROW]).then_inc(w_loaded[4], 16)

            def load_past(h):
                for s, src in enumerate((kd_cache, ks_cache, vd_cache, vs_cache)):
                    if not isinstance(h, int) or h > 0:
                        sp.wait_ge(scores_ready if s < 2 else values_done, h)
                    sp.dma_start(cache[:, s, :], src[h]).then_inc(past_loaded[s], 16)

            sp.dma_start(flat[:, 0:DT * T], x_t).then_inc(x_loaded, 16)
            sp.dma_start(lam_in[:, :, :], lam_vecs).then_inc(consts_loaded, 16)
            sp.dma_start(gain[:, :], subln).then_inc(consts_loaded, 16)
            load_head(0)
            load_past(0)
            sp.dma_start(x1[:, :, :], x_rows).then_inc(rows_loaded, 16)
            sp.dma_start(ln_rows[:, :, :], ln1).then_inc(ln_loaded, 16)
            with sp.Fori(1, H) as h:
                load_head(h)
                load_past(h)

            sp.wait_ge(qk_projected, 4 * H)
            for g in range(4):
                sp.dma_start(w_slot[g], w_out[g]).then_inc(wo_loaded[g], 16)
            sp.wait_ge(v_projected, NB * H)
            for i in range(2):
                sp.dma_start(wq_slot[i], w_q[i]).then_inc(wq_loaded[i], 16)
            sp.wait_ge(values_done, H)
            sp.dma_start(subkT, subkeys).then_inc(subkeys_loaded, 16)
            for s in stored:
                sp.wait_ge(s, 16 * H)
            for i in range(2, 4):
                sp.dma_start(wq_slot[i], w_q[i]).then_inc(wq_loaded[i], 16)
            with sp.Fori(1, 4) as n:
                for g in range(4):
                    sp.wait_ge(wo_used[0], (n - 1) * 4 + g + 1)
                    sp.dma_start(w_slot[g], w_out[n * 4 + g]).then_inc(wo_loaded[g], 16)
            with sp.Fori(1, 4) as j:
                for i in range(4):
                    sp.wait_ge(query_done[0], (j - 1) * 4 + i + 1)
                    sp.dma_start(wq_slot[i], w_q[j * 4 + i]).then_inc(wq_loaded[i], 16)

            for i in range(2):
                sp.wait_ge(query_done[0], 3 * 4 + i + 1)
                sp.dma_start(w_pair[i], w_out[i]).then_inc(pair_loaded[i], 16)
            with sp.Fori(1, 8) as n:
                for i in range(2):
                    sp.wait_ge(wo_used[1], (n - 1) * 2 + i + 1)
                    sp.dma_start(w_pair[i], w_out[n * 2 + i]).then_inc(pair_loaded[i], 16)
            for i in range(2):
                sp.wait_ge(wo_used[1], 14 + i + 1)
                sp.dma_start(w_pair[i], w_q[i]).then_inc(pair_loaded[i], 16)
            sp.wait_ge(ln1_done[1], 2)
            sp.dma_start(ln_rows[:, :, :], ln2).then_inc(ln_loaded, 16)
            with sp.Fori(1, 8) as n:
                for i in range(2):
                    sp.wait_ge(query_done[1], (n - 1) * 2 + i + 1)
                    sp.dma_start(w_pair[i], w_q[n * 2 + i]).then_inc(pair_loaded[i], 16)
            for b in range(NB):
                sp.wait_ge(y_ready, b + 1)
                sp.dma_start(y_out[b], normed).then_inc(y_stored, 16)
            sp.wait_ge(y_stored, 16 * NB)

        @block.gpsimd
        def _(pool):
            n = [0]

            def const(ins):
                n[0] += 1
                ins.then_inc(pool_init, 1)
                pool.wait_ge(pool_init, n[0])

            def hide(tile, fill, pattern, base, mult, op=ALU.is_ge):
                const(pool.affine_select(out=tile, in_=tile, pattern=pattern, compare_op=op, fill=fill,
                                         base=base, channel_multiplier=mult))

            def only_own_stream(tile, fill):
                t = tile.rearrange("p (b j) -> p b j", b=STREAMS)
                hide(t, fill, [[-FRAMES, STREAMS], [0, FRAMES]], 0, 1)
                hide(t, fill, [[FRAMES, STREAMS], [0, FRAMES]], FRAMES - 1, -1)

            const(pool.memset(qd_half[0][64:P, :], 0.0))
            const(pool.memset(qd_half[1][0:64, :], 0.0))
            const(pool.memset(ident[:, :], 0.0))
            hide(ident[:, :], 1.0, [[-1, P]], 0, 1, ALU.not_equal)
            const(pool.memset(ident_alpha[:, :], 0.0))
            hide(ident_alpha[:, :], ALPHA, [[-1, P]], 0, 1, ALU.not_equal)
            const(pool.memset(mean_mat[:, :], 1.0 / P))
            const(pool.memset(zeros[:, :], 0.0))
            const(pool.memset(eps[:, :], EPS))
            for h in range(H):
                const(pool.memset(slopes[:, h:h + 1], 2.0 ** (-8.0 * (h + 1) / H)))
            const(pool.iota(iota16[:, :], [[1, K]], base=0, channel_multiplier=0,
                            allow_small_or_imprecise_dtypes=True))
            const(pool.iota(ramp[:, :], [[-1, 256]], base=P, channel_multiplier=1,
                            allow_small_or_imprecise_dtypes=True))
            hide(ramp[:, :], 0.0, [[-1, 256]], P, 1)
            const(pool.iota(dist[:, 1, :], [[1, 256]], base=-P, channel_multiplier=-1,
                            allow_small_or_imprecise_dtypes=True))
            hide(dist[:, 1, :], 0.0, [[1, 256]], -P, -1)
            const(pool.tensor_tensor(dist[:, 1, :], dist[:, 1, :], ramp[:, :], ALU.add))
            const(pool.tensor_copy(dist[:, 0, P:256], dist[:, 1, P:256]))
            only_own_stream(dist[:, 0, P:256], HIDDEN)
            const(pool.memset(dist[0:CHUNK, 1, P + CHUNK:256], HIDDEN))
            const(pool.iota(dist[:, 0, 0:P], [[-1, P]], base=P, channel_multiplier=0,
                            allow_small_or_imprecise_dtypes=True))
            const(pool.iota(frame_i[:, :], [[0, 1]], base=0, channel_multiplier=1))
            const(pool.memset(stick_mask[:, :], 0.0))
            for at in (P, 3 * P, 4 * P):
                hide(stick_mask[:, at:at + P], -HIDDEN, [[-1, P]], 0, 1, ALU.is_gt)
            only_own_stream(stick_mask[:, P:256], -HIDDEN)
            assert n[0] == POOL_CONSTS, n[0]

            def store_head(h):
                for s, out in ((1, kd_out), (3, ks_out)):
                    wait_apart(pool, "pool", qk_evacuated, h * 4 + s + 1)
                    pool.dma_start(out[h], qk[:, s, :]).then_inc(stored[s // 2], 16)
                wait_apart(pool, "pool", v_evacuated, h * NB + NB)
                pool.dma_start(v_out[h], v_new).then_inc(stored[2], 16)

            with pool.Fori(0, H) as h:
                store_head(h)

            def take_idx(dst, g):
                pool.tensor_copy(dst, expert[:, g, :]).then_inc(idx_copied, 1)

            def gather_u(g, k, par):
                wait_apart(pool, "pool", u_dotted, g * K + k + 1)
                pool.indirect_dma_start(
                    out=u_row[k % U_SLOTS], out_offset=None, in_=peer_u,
                    in_offset=bass.IndirectOffsetOnAxis(ap=idx_u[:, par, k:k + 1], axis=0),
                ).then_inc(u_loaded[k % U_SLOTS], 16)

            def gather_v(g, k, par):
                wait_apart(pool, "pool", v_added, g * K + k + 1)
                pool.indirect_dma_start(
                    out=v_row[k % V_SLOTS], out_offset=None, in_=peer_v,
                    in_offset=bass.IndirectOffsetOnAxis(ap=idx_v[:, par, k:k + 1], axis=0),
                ).then_inc(v_loaded[k % V_SLOTS], 16)

            def step(g, par, last=False):
                if not last:
                    if not (isinstance(g, int) and g == 0):
                        wait_apart(pool, "pool", u_dotted, g * K + U_SLOTS)
                    take_idx(idx_u[:, 1 - par, :], g + 1)
                if not (isinstance(g, int) and g < 2):
                    wait_apart(pool, "pool", v_added, (g - 1) * K + V_SLOTS)
                take_idx(idx_v[:, par, :], g)
                wait_apart(pool, "pool", idx_copied, g * 2 + (2 if last else 3))
                for k in range(K):
                    gather_v(g, k, par)
                    if not last:
                        gather_u(g + 1, k, 1 - par)

            pool.wait_ge(gates_ready[0], 1)
            pool.wait_ge(wo_used[0], 4 * 4)
            take_idx(idx_u[:, 0, :], 0)
            pool.wait_ge(idx_copied, 1)
            for k in range(K):
                gather_u(0, k, 0)
            pool.wait_ge(gates_ready[0], 4)
            pool.wait_ge(query_done[0], 4 * 4)
            step(0, 0)
            step(1, 1)
            with pool.Fori(1, H // 2 - 1) as pair:
                step(pair * 2, 0)
                step(pair * 2 + 1, 1)
            step(H - 2, 0)
            pool.wait_ge(gates_ready[1], 1)
            step(H - 1, 1)
            with pool.Fori(0, H // 2 - 1) as pair:
                step(pair * 2 + H, 0)
                wait_apart(pool, "pool", gates_ready[1], pair + 2)
                step(pair * 2 + H + 1, 1)
            with pool.Fori(H - 1, HEADS // 2 - 1) as pair:
                step(pair * 2, 0)
                step(pair * 2 + 1, 1)
            step(HEADS - 2, 0)
            step(HEADS - 1, 1, last=True)

        @block.scalar
        def _(act):
            for s in (oT_copied, sticks_ready, *query_copied[0], *query_copied[1], *key_copied[0], *key_copied[1]):
                act.sem_inc(s, LEAD)
            act.wait_ge(dve_init, 2)
            act.activation(lam_exp[:, :], lam_dot[:, :], ACT.Exp).then_inc(act_init, 1)

            def copy_qk(h, s):
                act.wait_ge(qk_projected, h * 4 + s + 1)
                if s in (1, 3) and not (isinstance(h, int) and h == 0):
                    act.wait_ge(stored[s // 2], h * 16)
                src = bank[5 + s % 3][:, 0:T]
                if s == 0:
                    act.activation(qd_half[0][0:64, :], src[0:64, :], ACT.Copy, scale=DIFF_SCALE)\
                       .then_inc(qd_half_copied, 1)
                    act.activation(qd_half[1][64:P, :], src[64:P, :], ACT.Copy, scale=DIFF_SCALE)\
                       .then_inc(qk_evacuated, 1)
                else:
                    act.activation(qk[:, s, :], src, ACT.Copy).then_inc(qk_evacuated, 1)

            def copy_v(h):
                for b in range(NB):
                    act.wait_ge(v_projected, h * NB + b + 1)
                    if b == 0 and not (isinstance(h, int) and h == 0):
                        act.wait_ge(stored[2], h * 16)
                    act.activation(v_new[:, b, :], bank[5 + (4 + b) % 3][:, 0:256], ACT.Copy)\
                       .then_inc(v_evacuated, 1)

            def attend(h, ahead):
                act.wait_ge(pastT_scored, h + 1)
                act.activation(pastT, pastT_ps, ACT.Copy).then_inc(pastT_copied, 1)
                for b in range(NB):
                    act.wait_ge(min_ready, h * NB + b + 1)
                    lo = P if b == 1 else 0
                    for c in range(2):
                        act.activation(probs[:, b, c, lo:256], probs[:, b, c, lo:256], ACT.Exp,
                                       bias=row_min[:, b, c:c + 1], scale=-1.0,
                                       accum_out=row_sum[:, b, c:c + 1]).then_inc(probs_ready, 1)
                if ahead:
                    copy_qk(h + 1, 0)
                act.wait_ge(neg_abs_ready, h + 1)
                act.activation(soft, soft, ACT.Exp).then_inc(soft_ready, 1)
                act.wait_ge(soft_ready, h * 2 + 1)
                act.activation(soft, soft, ACT.Ln, bias=1.0).then_inc(soft_ready, 1)
                if ahead:
                    copy_qk(h + 1, 1)
                act.wait_ge(exponent_ready, h + 1)
                act.activation(sticks.rearrange("p s n -> p (s n)"), suffix, ACT.Exp).then_inc(sticks_ready, 1)
                if ahead:
                    copy_qk(h + 1, 2)
                    copy_qk(h + 1, 3)
                act.wait_ge(transposed, h + 1 + LEAD)
                for j, (lo, hi) in enumerate(((0, 3), (3, 6), (6, 10))):
                    act.activation(weightsT[:, lo:hi, :].rearrange("p s n -> p (s n)"), wT_ps[j], ACT.Copy)\
                       .then_inc(wT_copied, 1)
                act.wait_ge(values_done, h + 1)
                for kind in range(2):
                    act.activation(mixedT[0][:, h + kind * H, :], oT_ps[kind][:, 0:P], ACT.Copy)\
                       .then_inc(oT_copied, 1)
                    act.activation(mixedT[1][:, h + kind * H, :], oT_ps[kind][:, P:T], ACT.Copy)\
                       .then_inc(oT_copied, 1)
                if ahead:
                    copy_v(h + 1)

            for s in range(4):
                copy_qk(0, s)
            copy_v(0)
            with act.Fori(0, H - 1) as h:
                attend(h, True)
            attend(H - 1, False)

            act.wait_ge(oT_copied, 4 * H + LEAD)
            for j in range(6):
                act.activation(squares[:, j * 512:(j + 1) * 512], mixed_diff[j], ACT.Square).then_inc(squared, 1)
            for j in range(6):
                act.wait_ge(meaned, j + 1)
                act.activation(squares[:, j * 512:(j + 1) * 512], bank[3 + j % 5][:, :], ACT.Sqrt,
                               bias=eps[:, :]).then_inc(rms_ready, 1)

            def ln1_deviation(grp):
                b0, b1 = GROUPS[grp][0], GROUPS[grp][-1] + 1
                act.wait_ge(ln1_step[grp], 1)
                act.activation(stdev[:, b0:b1], moments[:, b0:b1, 1], ACT.Sqrt, bias=eps[:, :])\
                   .then_inc(ln1_sd[grp], 1)

            def ln1_scale(grp):
                act.wait_ge(ln1_step[grp], 3)
                for b in GROUPS[grp]:
                    act.activation(x1[:, b, :], x1[:, b, :], ACT.Identity, scale=rstd[:, b:b + 1],
                                   bias=shift[:, b:b + 1]).then_inc(ln1_scaled[grp], 1)

            def copy_x1T(grp):
                for i in range(len(GROUPS[grp])):
                    for j in range(4):
                        act.wait_ge(x1_transposed[grp], i * 4 + j + 1)
                        act.activation(x1T[grp][:, 4 * j:4 * j + 4, i * P:(i + 1) * P],
                                       bank[4 + j][:, :].rearrange("p (t n) -> p t n", t=4),
                                       ACT.Copy).then_inc(x1T_copied[grp], 1)

            def copy_query(grp, j, i):
                n = len(GROUPS[grp]) * P
                act.wait_ge(query_done[grp], j * 4 + 2 * i + 2)
                act.activation(queryT[:, i, 0:2 * n], bank[4 + i][:, 0:2 * n], ACT.Copy)\
                   .then_inc(query_copied[grp][i], 1)

            def copy_keys(grp, j, i):
                nb = len(GROUPS[grp])
                act.wait_ge(key_scored[grp][i], j + 1)
                act.wait_ge(half_read[grp], j + LEAD)
                act.activation(key_scores[:, :, i * nb:(i + 1) * nb, :],
                               bank[6 + i][:, 0:2 * nb * KEYS].rearrange("p (c b k) -> p c b k", c=2, b=nb),
                               ACT.Copy).then_inc(key_copied[grp][i], 1)

            def gate_numerators(grp, j):
                n = 2 * len(GROUPS[grp])
                act.wait_ge(over_ready[grp], j + 1)
                act.activation(expo[:, 0:n, :], over_max[:, 0:n, :], ACT.Exp).then_inc(expo_ready[grp], 1)

            ln1_deviation(0)
            ln1_scale(0)
            copy_x1T(0)

            def copies(j):
                for i in range(2):
                    copy_query(0, j, i)
                for i in range(2):
                    copy_keys(0, j, i)

            copies(0)
            with act.Fori(1, 4) as j:
                copies(j)
                gate_numerators(0, j - 1)
            gate_numerators(0, 3)

            def activate(g):
                act.wait_ge(u_dotted, g * K + K + U_SLOTS)
                act.activation(gelu[:, :], dots[:, :], ACT.Gelu).then_inc(gelu_ready, 1)

            def spread(g, quarter):
                if quarter == 0:
                    act.wait_ge(coef_ready, g + 1)
                for k in range(4 * quarter, 4 * quarter + 4):
                    act.wait_ge(v_added, g * K + k + 1)
                    act.activation(diag[:, k % DIAGS, :], ident[:, :], ACT.Copy, scale=coef[:, g, k:k + 1])\
                       .then_inc(diag_ready, 1)

            def spread_all(g):
                for quarter in range(4):
                    spread(g, quarter)

            def ln2_scale(b):
                act.wait_ge(ln2_step, b * 3 + 1)
                act.activation(stdev[:, b:b + 1], moments[:, b, 1:2], ACT.Sqrt, bias=eps[:, :]).then_inc(ln2_sd, 1)
                act.wait_ge(ln2_step, b * 3 + 3)
                if b > 0:
                    act.wait_ge(y_stored, 16 * b)
                for j in range(4):
                    act.activation(normed[:, j * 512:(j + 1) * 512], bank[4 * (b % 2) + j][:, :], ACT.Identity,
                                   scale=rstd[:, b:b + 1], bias=shift[:, b:b + 1]).then_inc(ln2_scaled, 1)

            activate(0)
            with act.Fori(0, 3) as g:
                spread_all(g)
                activate(g + 1)
            spread(3, 0)
            ln1_deviation(1)
            spread(3, 1)
            ln1_scale(1)
            spread(3, 2)
            spread(3, 3)
            copy_x1T(1)
            activate(4)

            def spread_with_queries(g, j):
                spread(g, 0)
                spread(g, 1)
                copy_query(1, j, 0)
                spread(g, 2)
                copy_keys(1, j, 0)
                spread(g, 3)
                copy_query(1, j, 1)
                copy_keys(1, j, 1)

            spread_with_queries(4, 0)
            activate(5)
            with act.Fori(5, H) as g:
                spread_with_queries(g, g - 4)
                gate_numerators(1, g - 5)
                activate(g + 1)
            ln2_scale(0)
            spread_all(H)
            gate_numerators(1, 3)
            activate(H + 1)
            with act.Fori(H + 1, 2 * H) as g:
                spread_all(g)
                activate(g + 1)
            ln2_scale(1)
            with act.Fori(2 * H, HEADS - 1) as g:
                spread_all(g)
                activate(g + 1)
            spread_all(HEADS - 1)
            ln2_scale(2)

        @block.tensor
        def _(pe):
            pe.sem_inc(transposed, LEAD)
            pe.sem_inc(v_added, V_SLOTS)
            pe.wait_ge(x_loaded, 16)

            def project_qk(h, s, between={}):
                pe.wait_ge(w_loaded[s], h * 16 + 16)
                if s == 3:
                    pe.wait_ge(qk_evacuated, h * 4 + 1)
                    pe.wait_ge(qd_half_copied, h + 1)
                elif not isinstance(h, int) or h > 0:
                    pe.wait_ge(v_evacuated, (h - 1) * NB + (3, 1, 2)[s])
                for t in range(DT):
                    mm = pe.matmul(bank[5 + s % 3][:, 0:T], w_slot[s][:, t * P:(t + 1) * P], xT[:, t, :],
                                   start=(t == 0), stop=(t == DT - 1))
                    if t in between:
                        between[t]()
                mm.then_inc(qk_projected, 1)

            def project_v(h, b):
                pe.wait_ge(w_loaded[4], h * 16 + 16)
                pe.wait_ge(qk_evacuated, h * 4 + b + 2)
                for t in range(DT):
                    mm = pe.matmul(bank[5 + (4 + b) % 3][:, 0:256], xT[:, t, b * P:(b + 1) * P], w_v[:, t, :],
                                   start=(t == 0), stop=(t == DT - 1))
                mm.then_inc(v_projected, 1)

            def own_scores(h):
                pe.wait_ge(qk_evacuated, h * 4 + 4)
                pe.wait_ge(qd_half_copied, h + 1)
                pe.wait_ge(oT_copied, 4 * h + LEAD)
                for b in range(NB):
                    q = slice(b * P, (b + 1) * P)
                    k = slice(P, 3 * P) if b == 2 else q
                    n = k.stop - k.start
                    lo = {0: P, 1: 0, 2: 0}[b]
                    width = P if b == 1 else 256
                    for c in range(2):
                        pe.matmul(diff_ps[b][:, c * width + lo:c * width + lo + n], qd_half[c][:, q], qk[:, 1, k],
                                  start=True, stop=True)
                    out = {0: bank[3][:, P:256], 1: stick1_ps, 2: bank[3][:, 256:512]}[b]
                    pe.matmul(out, qk[:, 2, q], qk[:, 3, k], start=True, stop=True)

            def stream_scores(h, j):
                if j == 0:
                    pe.wait_ge(past_loaded[0], h * 16 + 16)
                    pe.wait_ge(past_loaded[1], h * 16 + 16)
                own = slice(j * FRAMES, (j + 1) * FRAMES)
                for c in range(2):
                    pe.matmul(pastT_ps[:, c, own], kd_past[:, j, :], qd_half[c][:, own], start=True, stop=True)
                mm = pe.matmul(pastT_ps[:, 2, own], ks_past[:, j, :], qk[:, 2, own], start=True, stop=True)
                if j == STREAMS - 1:
                    mm.then_inc(pastT_scored, 1)

            def past_scores(h):
                pe.wait_ge(pastT_copied, h + 1)
                pe.transpose(diff_ps[0][:, 0:P], pastT[:, 0, :], ident[:, :])
                pe.transpose(diff_ps[0][:, 256:256 + P], pastT[:, 1, :], ident[:, :])
                pe.transpose(bank[3][:, 0:P], pastT[:, 2, :], ident[:, :]).then_inc(scores_ready, 1)

            order = [(weights, 0), (weights, 1), (weights, 2), (weights, 3), (weights, 4), (sticks, 4),
                     (sticks, 0), (sticks, 1), (sticks, 2), (sticks, 3)]

            def turn(h):
                pe.wait_ge(scores_read, h * 5 + 5)
                pe.wait_ge(weights_ready, h * NB + NB)
                pe.wait_ge(sticks_ready, h + 1 + LEAD)
                for n, (src, slot) in enumerate(order):
                    at, first = (0, 0) if n < 3 else (1, 3) if n < 6 else (2, 6)
                    mm = pe.transpose(wT_ps[at][:, (n - first) * P:(n - first + 1) * P], src[:, slot, :], ident[:, :])
                mm.then_inc(transposed, 1)

            def values(h, kind):
                if kind == 0:
                    pe.wait_ge(wT_copied, h * 3 + 3)
                    pe.wait_ge(v_evacuated, h * NB + NB)
                pe.wait_ge(past_loaded[2 + kind], h * 16 + 16)
                past = (vd_past, vs_past)[kind]
                o = oT_ps[kind]
                d = slice(kind * P, (kind + 1) * P)
                past0, own0, own1, past2, own2 = ((0, 1, 2, 3, 4), (6, 7, 5, 8, 9))[kind]
                pe.matmul(o[:, 0:P], v_new[:, 0, d], weightsT[:, own0, :], start=True, stop=False,
                          skip_group_check=True)
                for j in range(STREAMS):
                    own = slice(j * FRAMES, (j + 1) * FRAMES)
                    pe.matmul(o[:, own], past[:, j, :], weightsT[:, past0, own], start=False,
                              stop=(j == STREAMS - 1), skip_group_check=True)
                pe.matmul(o[:, P:2 * P], v_new[:, 1, d], weightsT[:, own1, :], start=True, stop=True,
                          skip_group_check=True)
                pe.matmul(o[:, 2 * P:T], v_new[:, 1, d], weightsT[:, past2, :], start=True, stop=False,
                          skip_group_check=True)
                mm = pe.matmul(o[:, 2 * P:T], v_new[:, 2, d], weightsT[:, own2, :], start=False, stop=True,
                               skip_group_check=True)
                if kind == 1:
                    mm.then_inc(values_done, 1)

            for s in range(4):
                project_qk(0, s)
            for b in range(NB):
                project_v(0, b)
            pe.wait_ge(pool_init, POOL_CONSTS)
            with pe.Fori(0, H - 1) as h:
                own_scores(h)
                project_qk(h + 1, 0, {2 * j: partial(stream_scores, h, j) for j in range(STREAMS)})
                project_qk(h + 1, 1, {1: partial(past_scores, h)})
                project_qk(h + 1, 2)
                project_qk(h + 1, 3)
                turn(h)
                project_v(h + 1, 0)
                values(h, 0)
                project_v(h + 1, 1)
                values(h, 1)
                project_v(h + 1, 2)
            own_scores(H - 1)
            for j in range(STREAMS):
                stream_scores(H - 1, j)
            past_scores(H - 1)
            turn(H - 1)
            for kind in range(2):
                values(H - 1, kind)

            pe.wait_ge(oT_copied, 4 * H + LEAD)
            for j in range(6):
                pe.wait_ge(squared, j + 1)
                if j == 5:
                    pe.wait_ge(rms_ready, 1)
                pe.matmul(bank[3 + j % 5][:, :], mean_mat[:, :], squares[:, j * 512:(j + 1) * 512], start=True,
                          stop=True).then_inc(meaned, 1)

            def project_out(grp, g, slot, banks):
                for i, out in enumerate(banks):
                    for e in range(4):
                        mm = pe.matmul(out[:, :], mixedT[grp][:, ((g + 2) % 4) * 4 + e, i * P:(i + 1) * P],
                                       slot[:, e * 512:(e + 1) * 512], start=(g == 0 and e == 0),
                                       stop=(g == 3 and e == 3))
                        if e == 3 and g == 3 and i + 1 < len(banks):
                            mm.then_inc(out_projected[grp], 1)
                mm.then_inc(wo_used[grp], 1)

            def turn_x1(grp):
                for i, b in enumerate(GROUPS[grp]):
                    pe.wait_ge(ln1_done[grp], i + 1)
                    for j in range(4):
                        if i:
                            pe.wait_ge(x1T_copied[grp], j + 1)
                        for t in range(4):
                            mm = pe.transpose(bank[4 + j][:, t * P:(t + 1) * P],
                                              x1[:, b, (4 * j + t) * P:(4 * j + t + 1) * P], ident[:, :])
                        mm.then_inc(x1_transposed[grp], 1)

            def project_query(grp, j, i, c, slot):
                n = len(GROUPS[grp]) * P
                if c == 0:
                    pe.wait_ge(query_copied[grp][i], j + LEAD)
                for t in range(DT):
                    mm = pe.matmul(bank[4 + i][:, c * n:(c + 1) * n], slot[:, t * P:(t + 1) * P], x1T[grp][:, t, :],
                                   start=(t == 0), stop=(t == DT - 1))
                mm.then_inc(query_done[grp], 1)

            def score_keys(grp, j, i):
                nb = len(GROUPS[grp])
                pe.wait_ge(query_copied[grp][i], j + 1 + LEAD)
                pe.wait_ge(key_copied[grp][i], j + LEAD)
                for c in range(2):
                    for b in range(nb):
                        at = c * nb + b
                        mm = pe.matmul(bank[6 + i][:, at * KEYS:(at + 1) * KEYS], queryT[:, i, at * P:(at + 1) * P],
                                       subkT[:, j * 4 + 2 * i + c, :], start=True, stop=True)
                mm.then_inc(key_scored[grp][i], 1)

            with pe.Fori(0, 2) as n:
                for half in range(2):
                    pe.wait_ge(residual_ready[0], n * 2 + half + 1)
                    for g in range(4):
                        pe.wait_ge(wo_loaded[g], (n * 2 + half) * 16 + 16)
                        if g == 2:
                            pe.wait_ge(diff_normed, 2)
                        project_out(0, g, w_slot[g], [bank[half]])
            turn_x1(0)
            pe.wait_ge(x1T_copied[0], 4)
            pe.wait_ge(subkeys_loaded, 16)
            with pe.Fori(0, 4) as j:
                for i in range(2):
                    for c in range(2):
                        pe.wait_ge(wq_loaded[2 * i + c], j * 16 + 16)
                        project_query(0, j, i, c, wq_slot[2 * i + c])
                for i in range(2):
                    score_keys(0, j, i)

            def start_block(b):
                for j in range(4):
                    pe.matmul(bank[4 * (b % 2) + j][:, :], ident_alpha[:, :], x1[:, b, j * 512:(j + 1) * 512],
                              start=True, stop=False, skip_group_check=True)

            def add_rows(g, quarter, half):
                for k in range(4 * quarter, 4 * quarter + 4):
                    pe.wait_ge(diag_ready, g * K + k + 1)
                    pe.wait_ge(v_loaded[k % V_SLOTS], (g * (K // V_SLOTS) + k // V_SLOTS) * 16 + 16)
                    for j in range(4):
                        mm = pe.matmul(bank[4 * half + j][:, :], diag[:, k % DIAGS, :],
                                       v_row[k % V_SLOTS][:, j * 512:(j + 1) * 512], start=False, stop=True,
                                       skip_group_check=True)
                    mm.then_inc(v_added, 1)

            def project_chunk(n, g):
                pe.wait_ge(pair_loaded[g % 2], (n * 2 + g // 2) * 16 + 16)
                if g == 0 and not isinstance(n, int):
                    pe.wait_ge(residual_ready[1], n * 2)
                project_out(1, g, w_pair[g % 2], [bank[4], bank[5]])

            for i in range(2):
                pe.wait_ge(query_copied[0][i], 4 + LEAD)
                pe.wait_ge(key_copied[0][i], 4 + LEAD)
            pe.wait_ge(diff_normed, 6)
            for g in range(4):
                project_chunk(0, g)
            start_block(0)
            with pe.Fori(0, 3) as g:
                for quarter in range(4):
                    project_chunk(g + 1, quarter)
                    add_rows(g, quarter, 0)
            for quarter in range(4):
                add_rows(3, quarter, 0)
            turn_x1(1)
            pe.wait_ge(x1T_copied[1], 8)
            with pe.Fori(4, H) as g:
                for quarter in range(4):
                    pe.wait_ge(pair_loaded[quarter % 2], ((g - 4) * 2 + quarter // 2 + 8) * 16 + 16)
                    project_query(1, g - 4, quarter // 2, quarter % 2, w_pair[quarter % 2])
                    add_rows(g, quarter, 0)
                    if quarter % 2:
                        score_keys(1, g - 4, quarter // 2)
            for i in range(2):
                pe.wait_ge(key_copied[1][i], 4 + LEAD)
            start_block(1)
            with pe.Fori(H, 2 * H) as g:
                for quarter in range(4):
                    add_rows(g, quarter, 1)
            pe.wait_ge(ln2_scaled, 4)
            start_block(2)
            with pe.Fori(2 * H, HEADS) as g:
                for quarter in range(4):
                    add_rows(g, quarter, 0)

        @block.vector
        def _(dve):
            for s in half_read:
                dve.sem_inc(s, LEAD)
            dve.sem_inc(u_dotted, U_SLOTS)
            dve.sem_inc(residual_ready[0], 2)
            dve.wait_ge(consts_loaded, 32)
            for i in range(2):
                dve.tensor_tensor_reduce(lam_prod[:, i, :], lam_in[:, 2 * i, :], lam_in[:, 2 * i + 1, :], 1.0, 0.0,
                                         ALU.mult, ALU.add, lam_dot[:, i:i + 1]).then_inc(dve_init, 1)
            dve.wait_ge(pool_init, POOL_CONSTS)
            dve.tensor_scalar(frame_i[:, :], frame_i[:, :], FRAMES - 1, None, ALU.bitwise_and).then_inc(dve_init, 1)
            dve.wait_ge(dve_init, 3)
            dve.tensor_copy(frame_f[:, :], frame_i[:, :]).then_inc(dve_init, 1)
            dve.tensor_scalar(gain8[:, :], gain[:, :], 1.0 - LAM_INIT, None, ALU.mult).then_inc(dve_init, 1)
            dve.wait_ge(dve_init, 5)
            dve.tensor_scalar(dist[:, 0, 0:P], dist[:, 0, 0:P], frame_f[:, 0:1], None, ALU.add).then_inc(dve_init, 1)
            dve.wait_ge(act_init, 1)
            dve.tensor_tensor(lam_diff[:, :], lam_exp[:, 1:2], lam_exp[:, 0:1], ALU.subtract).then_inc(dve_init, 1)
            dve.wait_ge(dve_init, 7)
            dve.tensor_scalar(neg_lam[:, :], lam_diff[:, :], -LAM_INIT, None, ALU.add).then_inc(dve_init, 1)
            dve.wait_ge(dve_init, 8)

            def attend(h):
                dve.wait_ge(scores_ready, h + 1)
                for b in range(NB):
                    lo = P if b == 1 else 0
                    d = dist[:, min(b, 1):min(b, 1) + 1, lo:256].to_broadcast([P, 2, 256 - lo])
                    dve.scalar_tensor_tensor(
                        out=probs[:, b, :, lo:256], in0=d, scalar=slopes[:, bass.ds(h, 1)],
                        in1=diff_ps[b].rearrange("p (c n) -> p c n", c=2), op0=ALU.mult,
                        op1=ALU.subtract).then_inc(scores_read, 1)
                dve.scalar_tensor_tensor(out=logit[:, 0:512], in0=stick02_ps, scalar=SB_SCALE,
                                         in1=stick_mask[:, 0:512], op0=ALU.mult, op1=ALU.add).then_inc(scores_read, 1)
                dve.scalar_tensor_tensor(out=logit[:, 512:640], in0=stick1_ps, scalar=SB_SCALE,
                                         in1=stick_mask[:, 512:640], op0=ALU.mult, op1=ALU.add)\
                   .then_inc(scores_read, 1)
                for b in range(NB):
                    lo = P if b == 1 else 0
                    dve.wait_ge(scores_read, h * 5 + b + 1)
                    dve.tensor_reduce(row_min[:, b, :], probs[:, b, :, lo:256], AX_X, ALU.min).then_inc(min_ready, 1)
                dve.wait_ge(scores_read, h * 5 + 5)
                dve.scalar_tensor_tensor(out=soft, in0=logit, scalar=-1.0, in1=logit, op0=ALU.mult,
                                         op1=ALU.min).then_inc(neg_abs_ready, 1)
                dve.wait_ge(probs_ready, h * 6 + 6)
                dve.reciprocal(row_inv[:, :, :], row_sum[:, :, :]).then_inc(inv_ready, 1)
                dve.wait_ge(inv_ready, h * 2 + 1)
                dve.tensor_scalar(lam_inv[:, :, :], row_inv[:, :, 1:2], neg_lam[:, 0:1], None, ALU.mult)\
                   .then_inc(inv_ready, 1)
                dve.wait_ge(transposed, h + LEAD)
                for b in range(NB):
                    lo = P if b == 1 else 0
                    w = weights[:, (0, 2, 3)[b]:(2, 3, 5)[b], :].rearrange("p s n -> p (s n)")
                    dve.tensor_scalar(w, probs[:, b, 0, lo:256], row_inv[:, b, 0:1], None, ALU.mult)\
                       .then_inc(half_weights, 1)
                dve.wait_ge(inv_ready, h * 2 + 2)
                for b in range(NB):
                    lo = P if b == 1 else 0
                    w = weights[:, (0, 2, 3)[b]:(2, 3, 5)[b], :].rearrange("p s n -> p (s n)")
                    dve.wait_ge(half_weights, h * NB + b + 1)
                    dve.scalar_tensor_tensor(out=w, in0=probs[:, b, 1, lo:256], scalar=lam_inv[:, b, 0:1], in1=w,
                                             op0=ALU.mult, op1=ALU.add).then_inc(weights_ready, 1)
                dve.wait_ge(soft_ready, h * 2 + 2)
                dve.scalar_tensor_tensor(out=soft, in0=logit, scalar=0.0, in1=soft, op0=ALU.max, op1=ALU.add)\
                   .then_inc(softplus_ready, 1)
                dve.wait_ge(softplus_ready, h + 1)
                dve.wait_ge(sticks_ready, h + LEAD)
                for lo, hi in ((0, 256), (256, 512), (512, 640)):
                    back = slice(hi - 1, lo - 1 if lo else None, -1)
                    dve.tensor_tensor_scan(suffix[:, back], soft[:, back], zeros[:, 0:hi - lo], 0.0, ALU.add,
                                           ALU.add).then_inc(suffix_ready, 1)
                dve.wait_ge(suffix_ready, h * 3 + 3)
                dve.tensor_tensor(suffix, logit, suffix, ALU.subtract).then_inc(exponent_ready, 1)

            with dve.Fori(0, H) as h:
                attend(h)

            for j in range(6):
                cols = slice(j * 512, (j + 1) * 512)
                dve.wait_ge(rms_ready, j + 1)
                dve.reciprocal(squares[:, cols], squares[:, cols]).then_inc(rms_inv, 1)
                dve.wait_ge(rms_inv, j + 1)
                dve.scalar_tensor_tensor(out=mixed_diff[j], in0=mixed_diff[j], scalar=gain8[:, 0:1],
                                         in1=squares[:, cols], op0=ALU.mult, op1=ALU.mult).then_inc(diff_normed, 1)

            def x1_chunk(b, n):
                return x1[:, b, :].rearrange("p (n c) -> p n c", n=4)[:, n, :]

            def add_residual(grp, n, banks):
                nb = len(banks)
                for i, out in enumerate(banks):
                    b = GROUPS[grp][i]
                    if i + 1 < nb:
                        dve.wait_ge(out_projected[grp], n * (nb - 1) + i + 1)
                    else:
                        dve.wait_ge(wo_used[grp], n * 4 + 4)
                    dve.scalar_tensor_tensor(out=x1_chunk(b, n), in0=x1_chunk(b, n), scalar=ALPHA, in1=out[:, :],
                                             op0=ALU.mult, op1=ALU.add).then_inc(residual_ready[grp], 1)
                for i in range(nb):
                    b = GROUPS[grp][i]
                    dve.wait_ge(residual_ready[grp], n * nb + i + 1 + (2 if grp == 0 else 0))
                    dve.bn_stats(stats[:, b, n, :], x1_chunk(b, n)).then_inc(stats_ready[grp], 1)

            def ln1_moments(grp):
                dve.wait_ge(stats_ready[grp], 4 * len(GROUPS[grp]))
                for b in GROUPS[grp]:
                    ins = dve.bn_aggr(moments[:, b, :], stats[:, b, :, :].rearrange("p n s -> p (n s)"))
                ins.then_inc(ln1_step[grp], 1)

            def ln1_shift(grp):
                b0, b1 = GROUPS[grp][0], GROUPS[grp][-1] + 1
                dve.wait_ge(ln1_sd[grp], 1)
                dve.reciprocal(rstd[:, b0:b1], stdev[:, b0:b1]).then_inc(ln1_step[grp], 1)
                dve.wait_ge(ln1_step[grp], 2)
                dve.scalar_tensor_tensor(out=shift[:, b0:b1], in0=moments[:, b0:b1, 0], scalar=-1.0,
                                         in1=rstd[:, b0:b1], op0=ALU.mult, op1=ALU.mult).then_inc(ln1_step[grp], 1)

            def ln1_affine(grp, i):
                b = GROUPS[grp][i]
                dve.wait_ge(ln_loaded, 16)
                dve.wait_ge(ln1_scaled[grp], i + 1)
                dve.tensor_tensor(x1[:, b, :], x1[:, b, :], ln_rows[:, 0, :], ALU.mult).then_inc(ln1_step[grp], 1)
                dve.wait_ge(ln1_step[grp], 4 + i)
                dve.tensor_tensor(x1[:, b, :], x1[:, b, :], ln_rows[:, 1, :], ALU.add).then_inc(ln1_done[grp], 1)

            dve.wait_ge(rows_loaded, 16)
            with dve.Fori(0, 2) as n:
                for half in range(2):
                    add_residual(0, n * 2 + half, [bank[half]])
            ln1_moments(0)
            ln1_shift(0)
            ln1_affine(0, 0)

            STEPS = {0: 45, 1: 75}

            def choose(grp, j, rows=None):
                nb = len(GROUPS[grp])
                nl = 2 * nb
                PER = STEPS[grp]
                n = [0]

                def ahead(ins):
                    n[0] += 1
                    ins.then_inc(topk_step[grp], 1)

                def settle():
                    if rows:
                        rows()
                    wait_apart(dve, "dve", topk_step[grp], j * PER + n[0])

                for i in range(2):
                    wait_apart(dve, "dve", key_copied[grp][i], j + 1 + LEAD)
                halves = [(c, lane) for c in range(2) for lane in range(nl)]
                for c, lane in halves:
                    ahead(dve.max(half_top[:, c, lane, 0:8], key_scores[:, c, lane, :]))
                settle()
                for c, lane in halves:
                    ahead(dve.match_replace(rest[:, c, lane, :], half_top[:, c, lane, 0:8], key_scores[:, c, lane, :],
                                            LOW))
                if rows:
                    rows()
                for c, lane in halves:
                    ahead(dve.max_index(half_idx[:, c, lane, 0:8], half_top[:, c, lane, 0:8],
                                        key_scores[:, c, lane, :]))
                settle()
                for c, lane in halves:
                    ahead(dve.max(half_top[:, c, lane, 8:16], rest[:, c, lane, :]))
                settle()
                for c, lane in halves:
                    ins = dve.max_index(half_idx[:, c, lane, 8:16], half_top[:, c, lane, 8:16], rest[:, c, lane, :])
                    if (c, lane) != halves[-1]:
                        ahead(ins)
                    else:
                        ins.then_inc(half_read[grp], 1)
                wide = [P, nl, K, K]
                cand, cand_rest = sums[:, 0, 0:nl], sums[:, 1, 0:nl]
                ahead(dve.tensor_tensor(
                    cand, half_top[:, 0, 0:nl, :].rearrange("p l (i o) -> p l i o", o=1).to_broadcast(wide),
                    half_top[:, 1, 0:nl, :].rearrange("p l (o j) -> p l o j", o=1).to_broadcast(wide), ALU.add))
                settle()
                dve.wait_ge(half_read[grp], j + 1 + LEAD)
                ahead(dve.tensor_copy(half_idx_f[:, :, 0:nl, :], half_idx[:, :, 0:nl, :]))
                all_sums = [cand[:, lane, :, :].rearrange("p i j -> p (i j)") for lane in range(nl)]
                left = [cand_rest[:, lane, :, :].rearrange("p i j -> p (i j)") for lane in range(nl)]
                for lane in range(nl):
                    ahead(dve.max(top[:, lane, 0:8], all_sums[lane]))
                settle()
                for lane in range(nl):
                    ahead(dve.match_replace(left[lane], top[:, lane, 0:8], all_sums[lane], LOW))
                for lane in range(nl):
                    ahead(dve.max_index(top_pos[:, lane, 0:8], top[:, lane, 0:8], all_sums[lane]))
                settle()
                for lane in range(nl):
                    ahead(dve.max(top[:, lane, 8:16], left[lane]))
                settle()
                dve.tensor_tensor(over_max[:, 0:nl, :], top[:, 0:nl, :], top[:, 0:nl, 0:1].to_broadcast([P, nl, K]),
                                  ALU.subtract).then_inc(over_ready[grp], 1)
                for lane in range(nl):
                    ahead(dve.max_index(top_pos[:, lane, 8:16], top[:, lane, 8:16], left[lane]))
                settle()
                ahead(dve.tensor_scalar(pos_ij[:, 0, 0:nl, :], top_pos[:, 0:nl, :], 4, None,
                                        ALU.logical_shift_right))
                ahead(dve.tensor_scalar(pos_ij[:, 1, 0:nl, :], top_pos[:, 0:nl, :], K - 1, None, ALU.bitwise_and))
                settle()
                ahead(dve.tensor_copy(pos_ij_f[:, :, 0:nl, :], pos_ij[:, :, 0:nl, :]))
                settle()
                steps = iota16[:, :].rearrange("p (a b k) -> p a b k", a=1, b=1).to_broadcast(wide)
                for c in range(2):
                    ahead(dve.tensor_tensor(
                        sums[:, c, 0:nl], pos_ij_f[:, c, 0:nl, :].rearrange("p l (i o) -> p l i o", o=1)
                        .to_broadcast(wide), steps, ALU.is_equal))
                settle()
                for c in range(2):
                    ahead(dve.tensor_tensor(
                        sums[:, c, 0:nl], sums[:, c, 0:nl], half_idx_f[:, c, 0:nl, :]
                        .rearrange("p l (o j) -> p l o j", o=1).to_broadcast(wide), ALU.mult))
                settle()
                for c in range(2):
                    ahead(dve.tensor_reduce(picked[:, c, 0:nl, :], sums[:, c, 0:nl], AX_X, ALU.add))
                settle()
                ahead(dve.scalar_tensor_tensor(out=expert_f[:, 0:nl, :], in0=picked[:, 0, 0:nl, :],
                                               scalar=float(KEYS), in1=picked[:, 1, 0:nl, :], op0=ALU.mult,
                                               op1=ALU.add))
                if rows:
                    rows(every=True)
                dve.wait_ge(expo_ready[grp], j + 1)
                ahead(dve.tensor_reduce(expo_sum[:, 0:nl], expo[:, 0:nl, :], AX_X, ALU.add))
                settle()

                def place(tile):
                    if grp == 0:
                        return tile[:, 0:H, :].rearrange("p (h b) k -> p h b k", b=1)[:, bass.ds(j * 2, 2), :, :]
                    return tile[:, H:HEADS, :].rearrange("p (b h) k -> p h b k", b=nb)[:, bass.ds(j * 2, 2), :, :]

                def split(tile):
                    return tile.rearrange("p (h b) k -> p h b k", b=nb)

                ahead(dve.tensor_copy(place(expert), split(expert_f[:, 0:nl, :])))
                ahead(dve.reciprocal(expo_inv[:, 0:nl], expo_sum[:, 0:nl]))
                settle()
                ahead(dve.tensor_tensor(expo_out[:, 0:nl, :], expo[:, 0:nl, :],
                                        expo_inv[:, 0:nl].rearrange("p (l o) -> p l o", o=1)
                                        .to_broadcast([P, nl, K]), ALU.mult))
                settle()
                assert n[0] == PER, n[0]
                dve.tensor_copy(place(gate), split(expo_out[:, 0:nl, :])).then_inc(gates_ready[grp], 1)

            with dve.Fori(0, 4) as j:
                choose(0, j)
            dve.wait_ge(gates_ready[0], 4)

            def dot(b, g, k):
                slot = k % U_SLOTS
                dve.wait_ge(u_loaded[slot], (g * (K // U_SLOTS) + k // U_SLOTS) * 16 + 16)
                dve.tensor_tensor_reduce(u_row[slot], u_row[slot], x1[:, b, :], 1.0, 0.0, ALU.mult, ALU.add,
                                         dots[:, k:k + 1]).then_inc(u_dotted, 1)

            def dots_of(b, g, k0=0, k1=K):
                if k0 == 0 and not (isinstance(g, int) and g == 0):
                    dve.wait_ge(gelu_ready, g)
                for k in range(k0, k1):
                    dot(b, g, k)

            def weigh(g):
                dve.wait_ge(gelu_ready, g + 1)
                dve.tensor_tensor(coef[:, g, :], gelu[:, :], gate[:, g, :], ALU.mult).then_inc(coef_ready, 1)

            def dots_and_choice(b, g, j):
                at = [0]

                def rows(every=False):
                    if at[0] < K:
                        upto = K if every else min(at[0] + 2, K)
                        dots_of(b, g, at[0], upto)
                        at[0] = upto

                choose(1, j, rows)
                weigh(g)

            def ln2(b):
                half = b % 2
                dve.wait_ge(v_added, (b + 1) * H * K + V_SLOTS)
                for j in range(4):
                    dve.bn_stats(stats[:, b, j, :], bank[4 * half + j][:, :]).then_inc(ln2_stats, 1)
                dve.wait_ge(ln2_stats, 4 * (b + 1))
                dve.bn_aggr(moments[:, b, :], stats[:, b, :, :].rearrange("p n s -> p (n s)")).then_inc(ln2_step, 1)
                dve.wait_ge(ln2_sd, b + 1)
                dve.reciprocal(rstd[:, b:b + 1], stdev[:, b:b + 1]).then_inc(ln2_step, 1)
                dve.wait_ge(ln2_step, b * 3 + 2)
                dve.scalar_tensor_tensor(out=shift[:, b:b + 1], in0=moments[:, b, 0:1], scalar=-1.0,
                                         in1=rstd[:, b:b + 1], op0=ALU.mult, op1=ALU.mult).then_inc(ln2_step, 1)
                dve.wait_ge(ln_loaded, 32)
                dve.wait_ge(ln2_scaled, 4 * (b + 1))
                dve.tensor_tensor(normed, normed, ln_rows[:, 0, :], ALU.mult).then_inc(ln2_weighted, 1)
                dve.wait_ge(ln2_weighted, b + 1)
                dve.tensor_tensor(normed, normed, ln_rows[:, 1, :], ALU.add).then_inc(y_ready, 1)

            dots_of(0, 0)
            weigh(0)
            add_residual(1, 0, [bank[4], bank[5]])
            with dve.Fori(0, 3) as g:
                dots_of(0, g + 1)
                weigh(g + 1)
                add_residual(1, g + 1, [bank[4], bank[5]])
            ln1_moments(1)
            dots_of(0, 4, 0, 4)
            ln1_shift(1)
            dots_of(0, 4, 4, 8)
            ln1_affine(1, 0)
            dots_of(0, 4, 8, 12)
            ln1_affine(1, 1)
            dots_of(0, 4, 12, 16)
            weigh(4)
            dots_of(0, 5)
            weigh(5)
            with dve.Fori(5, H - 1) as g:
                dots_and_choice(0, g + 1, g - 5)
            dots_and_choice(1, H, 2)
            ln2(0)
            dots_and_choice(1, H + 1, 3)
            with dve.Fori(H + 1, 2 * H - 1) as g:
                dots_of(1, g + 1)
                weigh(g + 1)
            dots_of(2, 2 * H)
            weigh(2 * H)
            ln2(1)
            with dve.Fori(2 * H, HEADS - 1) as g:
                dots_of(2, g + 1)
                weigh(g + 1)
            ln2(2)


def kernel(x_prompt, x_sample, cache_diff_k, cache_diff_v, cache_sb_k, cache_sb_v, w_in, w_out, lam_q1, lam_k1,
           lam_q2, lam_k2, subln_g, ln1_g, ln1_b, ln2_g, ln2_b, peer_w_q, peer_subkeys, peer_u, peer_v):
    import numpy as np
    import concourse.bacc as bacc
    from concourse.bass_utils import run_bass_kernel_spmd

    a = np.asarray
    x = np.concatenate([a(x_sample).reshape(P, D), a(x_prompt).reshape(2 * P, D)])
    w = a(w_in)[0]
    cols = lambda k: w[:, k * 1024:(k + 1) * 1024].reshape(DT, P, H, P).transpose(2, 1, 0, 3)
    qd, kd, vd, qs, ks, vs = (cols(k) for k in range(6))
    w_heads = np.concatenate([z.reshape(H, P, ROW) for z in (qd, kd, qs, ks)]
                             + [np.concatenate([vd, vs], axis=3).reshape(H, P, 2 * ROW)], axis=2)
    keysT = lambda z: a(z)[0].reshape(STREAMS, P, H, P).transpose(2, 3, 0, 1).reshape(H, P, STREAMS * P)
    rowsT = lambda z: a(z)[0].reshape(STREAMS, P, H, P).transpose(2, 1, 0, 3).reshape(H, P, STREAMS * P)
    wo = a(w_out)[0].reshape(4, 4, P, 4, 512).transpose(3, 0, 2, 1, 4)[:, [2, 3, 0, 1]].reshape(16, P, ROW)
    wq = a(peer_w_q)[0].reshape(DT, P, 2 * H, P).transpose(2, 1, 0, 3).reshape(2 * H, P, ROW)
    wide = lambda *z: np.broadcast_to(np.stack([a(q)[0] for q in z])[None], (P, len(z), a(z[0]).shape[1]))
    ins = {
        "x_t": x.reshape(T, DT, P).transpose(2, 1, 0).reshape(P, DT * T),
        "x_rows": x.reshape(NB, P, D).transpose(1, 0, 2),
        "w_heads": w_heads,
        "kd_cache": keysT(cache_diff_k), "ks_cache": keysT(cache_sb_k),
        "vd_cache": rowsT(cache_diff_v), "vs_cache": rowsT(cache_sb_v),
        "w_out": wo,
        "lam_vecs": wide(lam_q1, lam_k1, lam_q2, lam_k2),
        "subln": a(subln_g)[0].reshape(P, 1),
        "ln1": wide(ln1_g, ln1_b), "ln2": wide(ln2_g, ln2_b),
        "w_q": wq,
        "subkeys": a(peer_subkeys)[0].reshape(2 * H, KEYS, P).transpose(2, 0, 1),
        "peer_u": a(peer_u)[0], "peer_v": a(peer_v)[0],
    }
    outs = {"y_out": (NB, P, D), "kd_out": (H, P, T), "ks_out": (H, P, T), "v_out": (H, P, NB, 256)}
    nc = bacc.Bacc("TRN2", target_bir_lowering=False, num_devices=1)
    arrays, args = {}, []
    for name, z in ins.items():
        arrays[name] = np.ascontiguousarray(z)
        args.append(nc.dram_tensor(name, z.shape, F32, kind="ExternalInput").ap())
    for name, shape in outs.items():
        args.append(nc.dram_tensor(name, shape, F32, kind="ExternalOutput").ap())
    build(nc, *args)
    r = run_bass_kernel_spmd(nc, [arrays], core_ids=[0]).results[0]

    y = a(r["y_out"]).reshape(T, D)
    kd_new, ks_new = (a(r[n]).reshape(H, P, T).transpose(2, 0, 1) for n in ("kd_out", "ks_out"))
    v_all = a(r["v_out"]).reshape(H, P, NB, 2, P).transpose(2, 1, 3, 0, 4).reshape(T, 2, H, P)
    rows = (kd_new.reshape(T, H, 2, 64), v_all[:, 0], ks_new, v_all[:, 1])
    prompt = [z[P:].reshape((1, 1, 2 * P) + z.shape[1:]) for z in rows]
    sample = [z[:P].reshape((1, STREAMS, FRAMES) + z.shape[1:]) for z in rows]
    out = [y[P:].reshape(1, 2 * P, D), y[:P].reshape(STREAMS, FRAMES, D)] + prompt + sample
    return tuple(np.ascontiguousarray(z) for z in out)
```

```python
import math
from contextlib import ExitStack
from functools import partial

import concourse.bass as bass
from concourse import mybir

F32 = mybir.dt.float32
F32R = mybir.dt.float32r
I32 = mybir.dt.int32
U32 = mybir.dt.uint32
ALU = mybir.AluOpType
ACT = mybir.ActivationFunctionType
AX_X = mybir.AxisListType.X

P = 128
D = 2048
DT = D // P
NB = 3
T = NB * P
H = 8
STREAMS, FRAMES = 8, 16
CHUNK = 64
DIFF_SCALE = 64 ** -0.5
SB_SCALE = 128 ** -0.5
LAM_INIT = 0.8 - 0.6 * math.exp(0.0)
ALPHA = 2.0 ** 0.25
EPS = 1e-5
KEYS = 128
K = 16
EXPERTS = KEYS * KEYS
HIDDEN = 1e30
LOW = -3e38
ROW = 2048
UNIT = ROW // 2
UNITS = 12
HIGH_UNITS = 4
X_PARTS = 4
U_SLOTS = V_SLOTS = 4
DIAGS = V_SLOTS
HEADS = NB * H
GROUPS = ((0,), (1, 2))
OUT_ORDER = ((0, 0), (1, 0), (2, 0), (0, 1), (1, 1), (2, 1), (0, 2), (0, 3), (1, 2), (1, 3), (2, 2), (2, 3),
             (3, 0), (3, 1), (3, 2), (3, 3))
LANES = 4


def build(nc, x_t, x_rows, w_heads, kd_cache, ks_cache, vd_cache, vs_cache, w_out, lam_vecs, subln,
          ln1, ln2, w_q, subkeys, peer_u, peer_v, y_out, kd_out, ks_out, v_out):
    ctx = ExitStack()
    with ctx:
        def sb(name, shape, dt=F32):
            return ctx.enter_context(nc.sbuf_tensor(name, shape, dt))

        def sem(name):
            return ctx.enter_context(nc.semaphore(name))

        with ExitStack() as rounded:
            arena_r, x1_r, ln_rows_r = (
                rounded.enter_context(nc.sbuf_tensor(name, shape, F32R))
                for name, shape in (("arena_rounded", [P, 12 * ROW]), ("x_high", [P, DT, T]),
                                    ("w_high", [P, HIGH_UNITS, UNIT])))
        arena = sb("arena", [P, 12, ROW])
        x1 = sb("x1", [P, NB, D])
        ln_rows = sb("ln_rows", [P, 2, D])
        flat = arena[:, :, :].rearrange("p s c -> p (s c)")
        xT = flat[:, 0:DT * T].rearrange("p (t n) -> p t n", t=DT)
        squares = flat[:, 0:H * T]
        x1T = [flat[:, 0:ROW].rearrange("p (t n) -> p t n", t=DT),
               flat[:, ROW:3 * ROW].rearrange("p (t n) -> p t n", t=DT)]
        mixedT = [flat[:, 3 * ROW:4 * ROW].rearrange("p (t n) -> p t n", t=2 * H),
                  flat[:, 4 * ROW:6 * ROW].rearrange("p (t n) -> p t n", t=2 * H)]
        mixed_diff = [flat[:, 3 * ROW + j * 512:3 * ROW + (j + 1) * 512] for j in range(2)] + \
                     [flat[:, 4 * ROW + j * 512:4 * ROW + (j + 1) * 512] for j in range(4)]
        w_slot = [arena[:, 6 + i, :] for i in range(6)]
        w_units = flat[:, 6 * ROW:12 * ROW].rearrange("p (u n) -> p u n", u=UNITS)

        x_high, w_high = x1_r[:, :, :], ln_rows_r[:, :, :]
        x_low = arena_r[:, 0:DT * T].rearrange("p (t n) -> p t n", t=DT)
        w_low = arena_r[:, 6 * ROW:12 * ROW].rearrange("p (u n) -> p u n", u=UNITS)
        w_v_low = arena_r[:, 10 * ROW:12 * ROW].rearrange("p (t n) -> p t n", t=DT)
        cache = sb("cache", [P, 4, STREAMS * P])
        kd_past, ks_past, vd_past, vs_past = (cache[:, i, :].rearrange("p (b n) -> p b n", b=STREAMS)
                                              for i in range(4))
        subkT = cache[:, 0:2, :].rearrange("p a n -> p (a n)").rearrange("p (g k) -> p g k", g=2 * H)
        queryT = cache[:, 2, :].rearrange("p (a n) -> p a n", a=2)
        key_scores = cache[:, 3, :].rearrange("p (c l k) -> p c l k", c=2, l=LANES)

        scratch = sb("scratch", [P, 9728])
        taken = [0]

        def cut(n):
            taken[0] += n
            assert taken[0] <= 9728
            return scratch[:, taken[0] - n:taken[0]]

        qk = cut(5 * T).rearrange("p (s n) -> p s n", s=5)
        qd_half = [qk[:, 0, :], qk[:, 4, :]]
        v_new = cut(NB * 256).rearrange("p (b n) -> p b n", b=NB)
        probs = cut(NB * 512).rearrange("p (b c n) -> p b c n", b=NB, c=2)
        weights = cut(5 * P).rearrange("p (s n) -> p s n", s=5)
        sticks = cut(5 * P).rearrange("p (s n) -> p s n", s=5)
        logit = cut(5 * P)
        soft = cut(5 * P)
        suffix = cut(5 * P)
        pastT = cut(3 * P).rearrange("p (s n) -> p s n", s=3)
        weightsT = cut(10 * P).rearrange("p (s n) -> p s n", s=10)
        ramp = cut(256)
        lam_in = cut(4 * 64).rearrange("p (s n) -> p s n", s=4)
        lam_prod = cut(2 * 64).rearrange("p (s n) -> p s n", s=2)
        taken[0] = 0
        rest = cut(2 * LANES * KEYS).rearrange("p (c l k) -> p c l k", c=2, l=LANES)
        sums = cut(2 * LANES * K * K).rearrange("p (c l i j) -> p c l i j", c=2, l=LANES, i=K)
        diag = cut(DIAGS * P).rearrange("p (s n) -> p s n", s=DIAGS)
        spare = [cut(ROW), cut(ROW)]
        normed = cut(D)
        u_row = w_slot[0:U_SLOTS]
        v_row = [arena[:, 3, :], arena[:, 0, :]] + spare
        wq_slot = w_slot[4:6] + spare
        w_pair = w_slot[4:6]

        ident = sb("ident", [P, P])
        ident_alpha = sb("ident_alpha", [P, P])
        mean_mat = sb("mean_mat", [P, P])
        zeros = sb("zeros", [P, 256])
        dist = sb("dist", [P, 2, 256])
        stick_mask = sb("stick_mask", [P, 5 * P])
        slopes = sb("slopes", [P, H])
        frame_i = sb("frame_i", [P, 1], I32)
        frame_f = sb("frame_f", [P, 1])
        eps = sb("eps", [P, 1])
        lam_dot = sb("lam_dot", [P, 2])
        lam_exp = sb("lam_exp", [P, 2])
        lam_diff = sb("lam_diff", [P, 1])
        neg_lam = sb("neg_lam", [P, 1])
        gain = sb("gain", [P, 1])
        gain8 = sb("gain8", [P, 1])
        row_min = sb("row_min", [P, NB, 2])
        row_sum = sb("row_sum", [P, NB, 2])
        row_inv = sb("row_inv", [P, NB, 2])
        lam_inv = sb("lam_inv", [P, NB, 1])
        stats = sb("stats", [P, NB, 4, 6])
        moments = sb("moments", [P, NB, 2])
        stdev = sb("stdev", [P, NB])
        rstd = sb("rstd", [P, NB])
        shift = sb("shift", [P, NB])
        half_top = sb("half_top", [P, 2, LANES, K])
        half_idx = sb("half_idx", [P, 2, LANES, K], U32)
        half_idx_f = sb("half_idx_f", [P, 2, LANES, K])
        top = sb("top", [P, LANES, K])
        top_pos = sb("top_pos", [P, LANES, K], U32)
        pos_ij = sb("pos_ij", [P, 2, LANES, K], U32)
        pos_ij_f = sb("pos_ij_f", [P, 2, LANES, K])
        picked = sb("picked", [P, 2, LANES, K])
        expert_f = sb("expert_f", [P, LANES, K])
        iota16 = sb("iota16", [P, K])
        over_max = sb("over_max", [P, LANES, K])
        expo = sb("expo", [P, LANES, K])
        expo_out = sb("expo_out", [P, LANES, K])
        expo_sum = sb("expo_sum", [P, LANES])
        expo_inv = sb("expo_inv", [P, LANES])
        expert = sb("expert", [P, HEADS, K], U32)
        gate = sb("gate", [P, HEADS, K])
        idx_u = sb("idx_u", [P, 2, K], U32)
        idx_v = sb("idx_v", [P, 2, K], U32)
        dots = sb("dots", [P, K])
        gelu = sb("gelu", [P, K])
        coef = sb("coef", [P, HEADS, K])

        bank = [ctx.enter_context(nc.psum_tensor(f"bank{i}", [P, 512], F32)) for i in range(8)]
        diff_ps = [bank[0][:, :], bank[2][:, 0:256], bank[1][:, :]]
        stick02_ps, stick1_ps = bank[3][:, :], bank[2][:, 256:384]
        pastT_ps = bank[4][:, 0:3 * P].rearrange("p (s n) -> p s n", s=3)
        wT_ps = [bank[0][:, 0:384], bank[1][:, 0:384], bank[2][:, 0:512]]
        oT_ps = [bank[3][:, 0:T], bank[4][:, 0:T]]

        consts_loaded, rows_loaded, ln_loaded, subkeys_loaded = map(
            sem, ("consts_loaded", "rows_loaded", "ln_loaded", "subkeys_loaded"))
        x_loaded = [sem(f"x_loaded{i}") for i in range(X_PARTS)]
        x_high_ready, x_low_ready, w_high_ready, w_low_ready, w_high_used = map(
            sem, ("x_high_ready", "x_low_ready", "w_high_ready", "w_low_ready", "w_high_used"))
        pool_init, dve_init, act_init = sem("pool_init"), sem("dve_init"), sem("act_init")
        w_loaded = [sem(f"w_loaded{i}") for i in range(5)]
        past_loaded = [sem(f"past_loaded{i}") for i in range(4)]
        stored = [sem(n) for n in ("kd_stored", "ks_stored", "v_stored")]
        qk_projected, v_projected = sem("qk_projected"), sem("v_projected")
        qd_half_copied, qk_evacuated, v_evacuated = sem("qd_half_copied"), sem("qk_evacuated"), sem("v_evacuated")
        pastT_scored, pastT_copied, scores_ready = sem("pastT_scored"), sem("pastT_copied"), sem("scores_ready")
        scores_read, logits_ready = sem("scores_read"), sem("logits_ready")
        min_ready, probs_ready, inv_ready = sem("min_ready"), sem("probs_ready"), sem("inv_ready")
        half_weights, weights_ready = sem("half_weights"), sem("weights_ready")
        neg_abs_ready, soft_ready, softplus_ready = sem("neg_abs_ready"), sem("soft_ready"), sem("softplus_ready")
        suffix_ready, exponent_ready, sticks_ready = sem("suffix_ready"), sem("exponent_ready"), sem("sticks_ready")
        transposed, wT_copied, values_done, oT_copied = (
            sem("transposed"), sem("wT_copied"), sem("values_done"), sem("oT_copied"))
        squared, meaned, rms_ready, rms_inv, diff_normed = (
            sem("squared"), sem("meaned"), sem("rms_ready"), sem("rms_inv"), sem("diff_normed"))
        def sems(name):
            return [sem(f"{name}_block0"), sem(f"{name}_blocks12")]

        wo_loaded = [sem(f"wo_loaded{i}") for i in range(4)]
        wq_loaded = [sem(f"wq_loaded{i}") for i in range(4)]
        pair_loaded = [sem(f"pair_loaded{i}") for i in range(2)]
        wo_used, out_projected, residual_ready, stats_ready = map(
            sems, ("wo_used", "out_projected", "residual_ready", "stats_ready"))
        ln1_step, ln1_sd, ln1_scaled, ln1_done = map(sems, ("ln1_step", "ln1_sd", "ln1_scaled", "ln1_done"))
        x1_transposed, x1T_copied = sems("x1_transposed"), sems("x1T_copied")
        query_done = sems("query_done")
        query_copied, key_scored, key_copied = (
            [[sem(f"{name}_group{g}_head{i}") for i in range(2)] for g in range(2)]
            for name in ("query_copied", "key_scored", "key_copied"))
        half_read, topk_step, over_ready, expo_ready, gates_ready = map(
            sems, ("half_read", "topk_step", "over_ready", "expo_ready", "gates_ready"))
        idx_copied = sem("idx_copied")
        u_loaded = [sem(f"u_loaded{i}") for i in range(U_SLOTS)]
        v_loaded = [sem(f"v_loaded{i}") for i in range(V_SLOTS)]
        u_dotted, gelu_ready, coef_ready, diag_ready, v_added = (
            sem("u_dotted"), sem("gelu_ready"), sem("coef_ready"), sem("diag_ready"), sem("v_added"))
        ln2_stats = sem("ln2_stats")
        ln2_step, ln2_weighted, ln2_sd, ln2_scaled, y_ready, y_stored = (
            sem("ln2_step"), sem("ln2_weighted"), sem("ln2_sd"), sem("ln2_scaled"), sem("y_ready"), sem("y_stored"))

        block = ctx.enter_context(nc.Block())

        LEAD = 1
        POOL_CONSTS = 35

        def x1_chunk(b, n):
            return x1[:, b, :].rearrange("p (n c) -> p n c", n=4)[:, n, :]

        waits_passed = {"dve": sem("dve_waits_passed"), "pool": sem("pool_waits_passed")}

        def wait_apart(eng, who, signal, value):
            eng.wait_ge(signal, value)
            eng.sem_inc(waits_passed[who], 1)

        @block.sync
        def _(sp):
            def load_qk(h, first=0):
                for s in range(first, 4):
                    if not isinstance(h, int) or h > 0:
                        sp.wait_ge(qk_projected, (h - 1) * 4 + s + 1)
                    sp.dma_start(w_slot[s], w_heads[h, :, s * ROW:(s + 1) * ROW]).then_inc(w_loaded[s], 16)

            def load_v(h):
                if not isinstance(h, int) or h > 0:
                    sp.wait_ge(v_projected, (h - 1) * NB + NB)
                sp.dma_start(flat[:, 10 * ROW:12 * ROW], w_heads[h, :, 4 * ROW:6 * ROW]).then_inc(w_loaded[4], 16)

            def load_past(h, part):
                for s in part:
                    if not isinstance(h, int) or h > 0:
                        sp.wait_ge(scores_ready if s < 2 else values_done, h)
                    sp.dma_start(cache[:, s, :], (kd_cache, ks_cache, vd_cache, vs_cache)[s][h])\
                      .then_inc(past_loaded[s], 16)

            part = DT * T // X_PARTS
            sp.dma_start(w_slot[0], w_heads[0, :, 0:ROW]).then_inc(w_loaded[0], 16)
            for i in range(X_PARTS):
                sp.dma_start(flat[:, i * part:(i + 1) * part], x_t[:, i * part:(i + 1) * part])\
                  .then_inc(x_loaded[i], 16)
            sp.dma_start(lam_in[:, :, :], lam_vecs).then_inc(consts_loaded, 16)
            sp.dma_start(gain[:, :], subln).then_inc(consts_loaded, 16)
            load_qk(0, first=1)
            load_v(0)
            load_past(0, (0, 1, 2, 3))
            load_qk(1)
            load_v(1)
            with sp.Fori(1, H - 1) as h:
                load_past(h, (0, 1))
                load_qk(h + 1)
                load_past(h, (2, 3))
                load_v(h + 1)
            load_past(H - 1, (0, 1))

            sp.wait_ge(qk_projected, 4 * H)

            def load_out(i):
                chunk, g = OUT_ORDER[i]
                if i >= 4:
                    sp.wait_ge(wo_used[0], i - 3)
                sp.dma_start(w_slot[i % 4], w_out[chunk * 4 + g]).then_inc(wo_loaded[i % 4], 16)

            for i in range(4):
                load_out(i)
            load_past(H - 1, (2, 3))
            sp.wait_ge(v_projected, NB * H)
            sp.dma_start(x1[:, :, :], x_rows).then_inc(rows_loaded, 16)
            for i in range(2):
                sp.dma_start(wq_slot[i], w_q[i]).then_inc(wq_loaded[i], 16)
            for i in range(4, len(OUT_ORDER)):
                if i == 8:
                    sp.dma_start(ln_rows[:, :, :], ln1).then_inc(ln_loaded, 16)
                load_out(i)
            sp.wait_ge(values_done, H)
            sp.dma_start(subkT, subkeys).then_inc(subkeys_loaded, 16)
            for s in stored:
                sp.wait_ge(s, 16 * H)
            for i in range(2, 4):
                sp.dma_start(wq_slot[i], w_q[i]).then_inc(wq_loaded[i], 16)
            with sp.Fori(1, 4) as j:
                for i in range(4):
                    sp.wait_ge(query_done[0], (j - 1) * 4 + i + 1)
                    sp.dma_start(wq_slot[i], w_q[j * 4 + i]).then_inc(wq_loaded[i], 16)

            for i in range(2):
                sp.wait_ge(query_done[0], 3 * 4 + i + 1)
                sp.dma_start(w_pair[i], w_out[i]).then_inc(pair_loaded[i], 16)
            with sp.Fori(1, 8) as n:
                for i in range(2):
                    sp.wait_ge(wo_used[1], (n - 1) * 2 + i + 1)
                    sp.dma_start(w_pair[i], w_out[n * 2 + i]).then_inc(pair_loaded[i], 16)
            for i in range(2):
                sp.wait_ge(wo_used[1], 14 + i + 1)
                sp.dma_start(w_pair[i], w_q[i]).then_inc(pair_loaded[i], 16)
            sp.wait_ge(ln1_done[1], 4 * 2)
            sp.dma_start(ln_rows[:, :, :], ln2).then_inc(ln_loaded, 16)
            with sp.Fori(1, 8) as n:
                for i in range(2):
                    sp.wait_ge(query_done[1], (n - 1) * 2 + i + 1)
                    sp.dma_start(w_pair[i], w_q[n * 2 + i]).then_inc(pair_loaded[i], 16)
            for b in range(NB):
                for half in range(2):
                    cols = slice(half * D // 2, (half + 1) * D // 2)
                    sp.wait_ge(y_ready, 4 * b + 2 * half + 2)
                    sp.dma_start(y_out[b][:, cols], normed[:, cols]).then_inc(y_stored, 16)
            sp.wait_ge(y_stored, 32 * NB)

        @block.gpsimd
        def _(pool):
            n = [0]

            def const(ins):
                n[0] += 1
                ins.then_inc(pool_init, 1)
                pool.wait_ge(pool_init, n[0])

            def hide(tile, fill, pattern, base, mult, op=ALU.is_ge):
                const(pool.affine_select(out=tile, in_=tile, pattern=pattern, compare_op=op, fill=fill,
                                         base=base, channel_multiplier=mult))

            def only_own_stream(tile, fill):
                t = tile.rearrange("p (b j) -> p b j", b=STREAMS)
                hide(t, fill, [[-FRAMES, STREAMS], [0, FRAMES]], 0, 1)
                hide(t, fill, [[FRAMES, STREAMS], [0, FRAMES]], FRAMES - 1, -1)

            const(pool.memset(qd_half[0][64:P, :], 0.0))
            const(pool.memset(qd_half[1][0:64, :], 0.0))
            const(pool.memset(ident[:, :], 0.0))
            hide(ident[:, :], 1.0, [[-1, P]], 0, 1, ALU.not_equal)
            const(pool.memset(ident_alpha[:, :], 0.0))
            hide(ident_alpha[:, :], ALPHA, [[-1, P]], 0, 1, ALU.not_equal)
            const(pool.memset(mean_mat[:, :], 1.0 / P))
            const(pool.memset(zeros[:, :], 0.0))
            const(pool.memset(eps[:, :], EPS))
            for h in range(H):
                const(pool.memset(slopes[:, h:h + 1], 2.0 ** (-8.0 * (h + 1) / H)))
            const(pool.iota(iota16[:, :], [[1, K]], base=0, channel_multiplier=0,
                            allow_small_or_imprecise_dtypes=True))
            const(pool.iota(ramp[:, :], [[-1, 256]], base=P, channel_multiplier=1,
                            allow_small_or_imprecise_dtypes=True))
            hide(ramp[:, :], 0.0, [[-1, 256]], P, 1)
            const(pool.iota(dist[:, 1, :], [[1, 256]], base=-P, channel_multiplier=-1,
                            allow_small_or_imprecise_dtypes=True))
            hide(dist[:, 1, :], 0.0, [[1, 256]], -P, -1)
            const(pool.tensor_tensor(dist[:, 1, :], dist[:, 1, :], ramp[:, :], ALU.add))
            const(pool.tensor_copy(dist[:, 0, P:256], dist[:, 1, P:256]))
            only_own_stream(dist[:, 0, P:256], HIDDEN)
            const(pool.memset(dist[0:CHUNK, 1, P + CHUNK:256], HIDDEN))
            const(pool.iota(dist[:, 0, 0:P], [[-1, P]], base=P, channel_multiplier=0,
                            allow_small_or_imprecise_dtypes=True))
            const(pool.iota(frame_i[:, :], [[0, 1]], base=0, channel_multiplier=1))
            const(pool.memset(stick_mask[:, :], 0.0))
            for at in (P, 3 * P, 4 * P):
                hide(stick_mask[:, at:at + P], -HIDDEN, [[-1, P]], 0, 1, ALU.is_gt)
            only_own_stream(stick_mask[:, P:256], -HIDDEN)
            assert n[0] == POOL_CONSTS, n[0]

            def store_head(h):
                for s, out in ((1, kd_out), (3, ks_out)):
                    wait_apart(pool, "pool", qk_evacuated, h * 4 + s + 1)
                    pool.dma_start(out[h], qk[:, s, :]).then_inc(stored[s // 2], 16)
                wait_apart(pool, "pool", v_evacuated, h * NB + NB)
                pool.dma_start(v_out[h], v_new).then_inc(stored[2], 16)

            with pool.Fori(0, H) as h:
                store_head(h)

            def take_idx(dst, g):
                pool.tensor_copy(dst, expert[:, g, :]).then_inc(idx_copied, 1)

            def gather_u(g, k, par):
                wait_apart(pool, "pool", u_dotted, g * K + k + 1)
                pool.indirect_dma_start(
                    out=u_row[k % U_SLOTS], out_offset=None, in_=peer_u,
                    in_offset=bass.IndirectOffsetOnAxis(ap=idx_u[:, par, k:k + 1], axis=0),
                ).then_inc(u_loaded[k % U_SLOTS], 16)

            def gather_v(g, k, par):
                wait_apart(pool, "pool", v_added, g * K + k + 1)
                pool.indirect_dma_start(
                    out=v_row[k % V_SLOTS], out_offset=None, in_=peer_v,
                    in_offset=bass.IndirectOffsetOnAxis(ap=idx_v[:, par, k:k + 1], axis=0),
                ).then_inc(v_loaded[k % V_SLOTS], 16)

            def step(g, par, last=False):
                if not last:
                    if not (isinstance(g, int) and g == 0):
                        wait_apart(pool, "pool", u_dotted, g * K + U_SLOTS)
                    take_idx(idx_u[:, 1 - par, :], g + 1)
                if not (isinstance(g, int) and g < 2):
                    wait_apart(pool, "pool", v_added, (g - 1) * K + V_SLOTS)
                take_idx(idx_v[:, par, :], g)
                wait_apart(pool, "pool", idx_copied, g * 2 + (2 if last else 3))
                for k in range(K):
                    gather_v(g, k, par)
                    if not last:
                        gather_u(g + 1, k, 1 - par)

            pool.wait_ge(gates_ready[0], 1)
            pool.wait_ge(wo_used[0], 4 * 4)
            take_idx(idx_u[:, 0, :], 0)
            pool.wait_ge(idx_copied, 1)
            for k in range(K):
                gather_u(0, k, 0)
            pool.wait_ge(query_done[0], 4 * 4)
            step(0, 0)
            pool.wait_ge(gates_ready[0], 2)
            step(1, 1)
            with pool.Fori(1, H // 2 - 1) as pair:
                step(pair * 2, 0)
                wait_apart(pool, "pool", gates_ready[0], pair + 2)
                step(pair * 2 + 1, 1)
            step(H - 2, 0)
            pool.wait_ge(gates_ready[1], 1)
            step(H - 1, 1)
            with pool.Fori(0, H // 2 - 1) as pair:
                step(pair * 2 + H, 0)
                wait_apart(pool, "pool", gates_ready[1], pair + 2)
                step(pair * 2 + H + 1, 1)
            with pool.Fori(H - 1, HEADS // 2 - 1) as pair:
                step(pair * 2, 0)
                step(pair * 2 + 1, 1)
            step(HEADS - 2, 0)
            step(HEADS - 1, 1, last=True)

        @block.scalar
        def _(act):
            for s in (oT_copied, sticks_ready, *query_copied[0], *query_copied[1], *key_copied[0], *key_copied[1]):
                act.sem_inc(s, LEAD)

            def round_x(i):
                tiles = slice(i * DT // X_PARTS, (i + 1) * DT // X_PARTS)
                act.wait_ge(x_loaded[i], 16)
                act.activation(x_high[:, tiles, :], xT[:, tiles, :], ACT.Copy)\
                   .then_inc(x_high_ready, 1)

            def round_w(h, u):
                s = min(u // 2, 4)
                if u in (0, 2, 4, 6, 8):
                    act.wait_ge(w_loaded[s], h * 16 + 16)
                act.wait_ge(w_high_used, h * UNITS + u + 1)
                act.activation(w_high[:, u % HIGH_UNITS, :], w_units[:, u, :], ACT.Copy)\
                   .then_inc(w_high_ready, 1)

            def copy_qk(h, s):
                act.wait_ge(qk_projected, h * 4 + s + 1)
                if s in (1, 3) and not (isinstance(h, int) and h == 0):
                    act.wait_ge(stored[s // 2], h * 16)
                src = bank[5 + s % 3][:, 0:T]
                if s == 0:
                    act.activation(qd_half[0][0:64, :], src[0:64, :], ACT.Copy, scale=DIFF_SCALE)\
                       .then_inc(qd_half_copied, 1)
                    act.activation(qd_half[1][64:P, :], src[64:P, :], ACT.Copy, scale=DIFF_SCALE)\
                       .then_inc(qk_evacuated, 1)
                else:
                    act.activation(qk[:, s, :], src, ACT.Copy).then_inc(qk_evacuated, 1)

            def copy_v(h):
                for b in range(NB):
                    act.wait_ge(v_projected, h * NB + b + 1)
                    if b == 0 and not (isinstance(h, int) and h == 0):
                        act.wait_ge(stored[2], h * 16)
                    act.activation(v_new[:, b, :], bank[5 + (4 + b) % 3][:, 0:256], ACT.Copy)\
                       .then_inc(v_evacuated, 1)

            def attend(h, ahead):
                if ahead:
                    for u in range(6):
                        round_w(h + 1, u)
                act.wait_ge(pastT_scored, h + 1)
                act.activation(pastT, pastT_ps, ACT.Copy).then_inc(pastT_copied, 1)
                for b in range(NB):
                    act.wait_ge(min_ready, h * NB + b + 1)
                    lo = P if b == 1 else 0
                    for c in range(2):
                        act.activation(probs[:, b, c, lo:256], probs[:, b, c, lo:256], ACT.Exp,
                                       bias=row_min[:, b, c:c + 1], scale=-1.0,
                                       accum_out=row_sum[:, b, c:c + 1]).then_inc(probs_ready, 1)
                if ahead:
                    copy_qk(h + 1, 0)
                act.wait_ge(neg_abs_ready, h + 1)
                act.activation(soft, soft, ACT.Exp).then_inc(soft_ready, 1)
                act.wait_ge(soft_ready, h * 2 + 1)
                act.activation(soft, soft, ACT.Ln, bias=1.0).then_inc(soft_ready, 1)
                if ahead:
                    round_w(h + 1, 6)
                    round_w(h + 1, 7)
                    copy_qk(h + 1, 1)
                act.wait_ge(exponent_ready, h + 1)
                act.activation(sticks.rearrange("p s n -> p (s n)"), suffix, ACT.Exp).then_inc(sticks_ready, 1)
                if ahead:
                    round_w(h + 1, 8)
                    round_w(h + 1, 9)
                    copy_qk(h + 1, 2)
                    round_w(h + 1, 10)
                    round_w(h + 1, 11)
                    copy_qk(h + 1, 3)
                act.wait_ge(transposed, h + 1 + LEAD)
                for j, (lo, hi) in enumerate(((0, 3), (3, 6), (6, 10))):
                    act.activation(weightsT[:, lo:hi, :].rearrange("p s n -> p (s n)"), wT_ps[j], ACT.Copy)\
                       .then_inc(wT_copied, 1)
                act.wait_ge(values_done, h + 1)
                for kind in range(2):
                    act.activation(mixedT[0][:, h + kind * H, :], oT_ps[kind][:, 0:P], ACT.Copy)\
                       .then_inc(oT_copied, 1)
                    act.activation(mixedT[1][:, h + kind * H, :], oT_ps[kind][:, P:T], ACT.Copy)\
                       .then_inc(oT_copied, 1)
                if ahead:
                    copy_v(h + 1)

            round_w(0, 0)
            for i in range(X_PARTS):
                round_x(i)
            for u in range(1, 6):
                round_w(0, u)
            for s in range(3):
                copy_qk(0, s)
                round_w(0, 6 + 2 * s)
                round_w(0, 7 + 2 * s)
            copy_qk(0, 3)
            copy_v(0)
            act.wait_ge(dve_init, 2)
            act.activation(lam_exp[:, :], lam_dot[:, :], ACT.Exp).then_inc(act_init, 1)
            with act.Fori(0, H - 1) as h:
                attend(h, True)
            attend(H - 1, False)

            act.wait_ge(oT_copied, 4 * H + LEAD)
            for j in range(6):
                act.activation(squares[:, j * 512:(j + 1) * 512], mixed_diff[j], ACT.Square).then_inc(squared, 1)
            for j in range(6):
                act.wait_ge(meaned, j + 1)
                act.activation(squares[:, j * 512:(j + 1) * 512], bank[j % 5][:, :], ACT.Sqrt,
                               bias=eps[:, :]).then_inc(rms_ready, 1)

            def ln1_deviation(grp):
                b0, b1 = GROUPS[grp][0], GROUPS[grp][-1] + 1
                act.wait_ge(ln1_step[grp], 1)
                act.activation(stdev[:, b0:b1], moments[:, b0:b1, 1], ACT.Sqrt, bias=eps[:, :])\
                   .then_inc(ln1_sd[grp], 1)

            def ln1_scale(grp):
                act.wait_ge(ln1_step[grp], 3)
                for b in GROUPS[grp]:
                    for q in range(4):
                        act.activation(x1_chunk(b, q), x1_chunk(b, q), ACT.Identity, scale=rstd[:, b:b + 1],
                                       bias=shift[:, b:b + 1]).then_inc(ln1_scaled[grp], 1)

            def copy_x1T(grp):
                for i in range(len(GROUPS[grp])):
                    for j in range(4):
                        act.wait_ge(x1_transposed[grp], i * 4 + j + 1)
                        act.activation(x1T[grp][:, 4 * j:4 * j + 4, i * P:(i + 1) * P],
                                       bank[4 + j][:, :].rearrange("p (t n) -> p t n", t=4),
                                       ACT.Copy).then_inc(x1T_copied[grp], 1)

            def copy_query(grp, j, i):
                n = len(GROUPS[grp]) * P
                act.wait_ge(query_done[grp], j * 4 + 2 * i + 2)
                act.activation(queryT[:, i, 0:2 * n], bank[4 + i][:, 0:2 * n], ACT.Copy)\
                   .then_inc(query_copied[grp][i], 1)

            def copy_keys(grp, j, i):
                nb = len(GROUPS[grp])
                act.wait_ge(key_scored[grp][i], j + 1)
                act.wait_ge(half_read[grp], j + LEAD)
                act.activation(key_scores[:, :, i * nb:(i + 1) * nb, :],
                               bank[6 + i][:, 0:2 * nb * KEYS].rearrange("p (c b k) -> p c b k", c=2, b=nb),
                               ACT.Copy).then_inc(key_copied[grp][i], 1)

            def gate_numerators(grp, j):
                n = 2 * len(GROUPS[grp])
                act.wait_ge(over_ready[grp], j + 1)
                act.activation(expo[:, 0:n, :], over_max[:, 0:n, :], ACT.Exp).then_inc(expo_ready[grp], 1)

            ln1_deviation(0)
            ln1_scale(0)
            copy_x1T(0)

            def copies(j):
                for i in range(2):
                    copy_query(0, j, i)
                for i in range(2):
                    copy_keys(0, j, i)

            copies(0)
            copies(1)
            gate_numerators(0, 0)
            copies(2)
            for i in range(2):
                copy_query(0, 3, i)
            gate_numerators(0, 1)

            def activate(g):
                act.wait_ge(u_dotted, g * K + K + U_SLOTS)
                act.activation(gelu[:, :], dots[:, :], ACT.Gelu).then_inc(gelu_ready, 1)

            def spread(g, quarter):
                if quarter == 0:
                    act.wait_ge(coef_ready, g + 1)
                for k in range(4 * quarter, 4 * quarter + 4):
                    act.wait_ge(v_added, g * K + k + 1)
                    act.activation(diag[:, k % DIAGS, :], ident[:, :], ACT.Copy, scale=coef[:, g, k:k + 1])\
                       .then_inc(diag_ready, 1)

            def spread_all(g):
                for quarter in range(4):
                    spread(g, quarter)

            def ln2_scale(b):
                act.wait_ge(ln2_step, b * 3 + 1)
                act.activation(stdev[:, b:b + 1], moments[:, b, 1:2], ACT.Sqrt, bias=eps[:, :]).then_inc(ln2_sd, 1)
                act.wait_ge(ln2_step, b * 3 + 3)
                if b > 0:
                    act.wait_ge(y_stored, 32 * b)
                for j in range(4):
                    act.activation(normed[:, j * 512:(j + 1) * 512], bank[4 * (b % 2) + j][:, :], ACT.Identity,
                                   scale=rstd[:, b:b + 1], bias=shift[:, b:b + 1]).then_inc(ln2_scaled, 1)

            activate(0)
            spread(0, 0)
            for i in range(2):
                copy_keys(0, 3, i)
            for quarter in range(1, 4):
                spread(0, quarter)
            for g in range(2):
                if g:
                    spread_all(g)
                gate_numerators(0, g + 2)
                activate(g + 1)
            spread_all(2)
            activate(3)
            spread(3, 0)
            ln1_deviation(1)
            spread(3, 1)
            ln1_scale(1)
            spread(3, 2)
            spread(3, 3)
            copy_x1T(1)
            activate(4)

            def spread_with_queries(g, j):
                spread(g, 0)
                spread(g, 1)
                copy_query(1, j, 0)
                spread(g, 2)
                copy_keys(1, j, 0)
                spread(g, 3)
                copy_query(1, j, 1)
                copy_keys(1, j, 1)

            spread_with_queries(4, 0)
            activate(5)
            with act.Fori(5, H) as g:
                spread_with_queries(g, g - 4)
                gate_numerators(1, g - 5)
                activate(g + 1)
            ln2_scale(0)
            spread_all(H)
            gate_numerators(1, 3)
            activate(H + 1)
            with act.Fori(H + 1, 2 * H) as g:
                spread_all(g)
                activate(g + 1)
            ln2_scale(1)
            with act.Fori(2 * H, HEADS - 1) as g:
                spread_all(g)
                activate(g + 1)
            spread_all(HEADS - 1)
            ln2_scale(2)

        @block.tensor
        def _(pe):
            pe.sem_inc(transposed, LEAD)
            pe.sem_inc(v_added, V_SLOTS)
            pe.sem_inc(w_high_used, HIGH_UNITS)

            def project_qk(h, s, between={}):
                if s == 3:
                    pe.wait_ge(qk_evacuated, h * 4 + 1)
                    pe.wait_ge(qd_half_copied, h + 1)
                elif not isinstance(h, int) or h > 0:
                    pe.wait_ge(v_evacuated, (h - 1) * NB + (3, 1, 2)[s])
                for t in range(DT):
                    u, at = 2 * s + t // 8, (t % 8) * P
                    if t % 8 == 0:
                        pe.wait_ge(w_low_ready, h * UNITS + u + 1)
                    if isinstance(h, int) and s == 0 and t % (DT // X_PARTS) == 0:
                        pe.wait_ge(x_low_ready, t // (DT // X_PARTS) + 1)
                    out = bank[5 + s % 3][:, 0:T]
                    high = w_high[:, u % HIGH_UNITS, at:at + P]
                    low = w_low[:, u, at:at + P]
                    pe.matmul(out, high, x_high[:, t, :], start=(t == 0), stop=False)
                    mm = pe.matmul(out, high, x_low[:, t, :], start=False, stop=False)
                    if t % 8 == 7:
                        mm.then_inc(w_high_used, 1)
                    mm = pe.matmul(out, low, x_high[:, t, :], start=False, stop=(t == DT - 1))
                    if t in between:
                        between[t]()
                mm.then_inc(qk_projected, 1)

            def project_v(h, b):
                pe.wait_ge(qk_evacuated, h * 4 + b + 2)
                for t in range(DT):
                    if b == 0 and t % 4 == 0:
                        pe.wait_ge(w_low_ready, h * UNITS + 8 + t // 4 + 1)
                    out = bank[5 + (4 + b) % 3][:, 0:256]
                    high = w_high[:, t // 4, (t % 4) * 256:(t % 4 + 1) * 256]
                    tokens = slice(b * P, (b + 1) * P)
                    pe.matmul(out, x_high[:, t, tokens], high, start=(t == 0), stop=False)
                    mm = pe.matmul(out, x_low[:, t, tokens], high, start=False, stop=False)
                    if b == NB - 1 and t % 4 == 3:
                        mm.then_inc(w_high_used, 1)
                    mm = pe.matmul(out, x_high[:, t, tokens], w_v_low[:, t, :], start=False,
                                   stop=(t == DT - 1))
                mm.then_inc(v_projected, 1)

            def own_scores(h):
                pe.wait_ge(qk_evacuated, h * 4 + 4)
                pe.wait_ge(qd_half_copied, h + 1)
                pe.wait_ge(oT_copied, 4 * h + LEAD)
                for b in range(NB):
                    q = slice(b * P, (b + 1) * P)
                    k = slice(P, 3 * P) if b == 2 else q
                    n = k.stop - k.start
                    lo = {0: P, 1: 0, 2: 0}[b]
                    width = P if b == 1 else 256
                    for c in range(2):
                        pe.matmul(diff_ps[b][:, c * width + lo:c * width + lo + n], qd_half[c][:, q], qk[:, 1, k],
                                  start=True, stop=True)
                    out = {0: bank[3][:, P:256], 1: stick1_ps, 2: bank[3][:, 256:512]}[b]
                    pe.matmul(out, qk[:, 2, q], qk[:, 3, k], start=True, stop=True)

            def stream_scores(h, j):
                if j == 0:
                    pe.wait_ge(past_loaded[0], h * 16 + 16)
                    pe.wait_ge(past_loaded[1], h * 16 + 16)
                own = slice(j * FRAMES, (j + 1) * FRAMES)
                pe.matmul(pastT_ps[:, 0:2, own], kd_past[:, j, :], qk[:, 0:5:4, own], start=True, stop=True)
                mm = pe.matmul(pastT_ps[:, 2, own], ks_past[:, j, :], qk[:, 2, own], start=True, stop=True)
                if j == STREAMS - 1:
                    mm.then_inc(pastT_scored, 1)

            def past_scores(h):
                pe.wait_ge(pastT_copied, h + 1)
                pe.transpose(diff_ps[0][:, 0:P], pastT[:, 0, :], ident[:, :])
                pe.transpose(diff_ps[0][:, 256:256 + P], pastT[:, 1, :], ident[:, :])
                pe.transpose(bank[3][:, 0:P], pastT[:, 2, :], ident[:, :]).then_inc(scores_ready, 1)

            order = [(weights, 0), (weights, 1), (weights, 2), (weights, 3), (weights, 4), (sticks, 4),
                     (sticks, 0), (sticks, 1), (sticks, 2), (sticks, 3)]

            def turn(h):
                pe.wait_ge(scores_read, h * 5 + 5)
                pe.wait_ge(weights_ready, h * NB + NB)
                pe.wait_ge(sticks_ready, h + 1 + LEAD)
                for n, (src, slot) in enumerate(order):
                    at, first = (0, 0) if n < 3 else (1, 3) if n < 6 else (2, 6)
                    mm = pe.transpose(wT_ps[at][:, (n - first) * P:(n - first + 1) * P], src[:, slot, :], ident[:, :])
                mm.then_inc(transposed, 1)

            def values(h, kind):
                if kind == 0:
                    pe.wait_ge(wT_copied, h * 3 + 3)
                    pe.wait_ge(v_evacuated, h * NB + NB)
                pe.wait_ge(past_loaded[2 + kind], h * 16 + 16)
                past = (vd_past, vs_past)[kind]
                o = oT_ps[kind]
                d = slice(kind * P, (kind + 1) * P)
                past0, own0, own1, past2, own2 = ((0, 1, 2, 3, 4), (6, 7, 5, 8, 9))[kind]
                pe.matmul(o[:, 0:P], v_new[:, 0, d], weightsT[:, own0, :], start=True, stop=False,
                          skip_group_check=True)
                for j in range(STREAMS):
                    own = slice(j * FRAMES, (j + 1) * FRAMES)
                    pe.matmul(o[:, own], past[:, j, :], weightsT[:, past0, own], start=False,
                              stop=(j == STREAMS - 1), skip_group_check=True)
                pe.matmul(o[:, P:2 * P], v_new[:, 1, d], weightsT[:, own1, :], start=True, stop=True,
                          skip_group_check=True)
                pe.matmul(o[:, 2 * P:T], v_new[:, 1, d], weightsT[:, past2, :], start=True, stop=False,
                          skip_group_check=True)
                mm = pe.matmul(o[:, 2 * P:T], v_new[:, 2, d], weightsT[:, own2, :], start=False, stop=True,
                               skip_group_check=True)
                if kind == 1:
                    mm.then_inc(values_done, 1)

            for s in range(4):
                project_qk(0, s)
            for b in range(NB):
                project_v(0, b)
            pe.wait_ge(pool_init, POOL_CONSTS)
            with pe.Fori(0, H - 1) as h:
                own_scores(h)
                project_qk(h + 1, 0, {2 * j: partial(stream_scores, h, j) for j in range(STREAMS)})
                project_qk(h + 1, 1, {1: partial(past_scores, h)})
                project_qk(h + 1, 2)
                project_qk(h + 1, 3)
                turn(h)
                project_v(h + 1, 0)
                values(h, 0)
                project_v(h + 1, 1)
                values(h, 1)
                project_v(h + 1, 2)
            def project_out(grp, g, slot, banks, between={}):
                for i, out in enumerate(banks):
                    for e in range(4):
                        mm = pe.matmul(out[:, :], mixedT[grp][:, ((g + 2) % 4) * 4 + e, i * P:(i + 1) * P],
                                       slot[:, e * 512:(e + 1) * 512], start=(g == 0 and e == 0),
                                       stop=(g == 3 and e == 3))
                        for step in between.get(e, ()):
                            step()
                        if e == 3 and g == 3 and i + 1 < len(banks):
                            mm.then_inc(out_projected[grp], 1)
                mm.then_inc(wo_used[grp], 1)

            def turn_x1(grp):
                for i, b in enumerate(GROUPS[grp]):
                    for j in range(4):
                        pe.wait_ge(ln1_done[grp], 4 * i + j + 1)
                        if i:
                            pe.wait_ge(x1T_copied[grp], j + 1)
                        for t in range(4):
                            mm = pe.transpose(bank[4 + j][:, t * P:(t + 1) * P],
                                              x1[:, b, (4 * j + t) * P:(4 * j + t + 1) * P], ident[:, :])
                        mm.then_inc(x1_transposed[grp], 1)

            def project_query(grp, j, i, c, slot):
                n = len(GROUPS[grp]) * P
                if c == 0:
                    pe.wait_ge(query_copied[grp][i], j + LEAD)
                for t in range(DT):
                    mm = pe.matmul(bank[4 + i][:, c * n:(c + 1) * n], slot[:, t * P:(t + 1) * P], x1T[grp][:, t, :],
                                   start=(t == 0), stop=(t == DT - 1))
                mm.then_inc(query_done[grp], 1)

            def score_keys(grp, j, i):
                nb = len(GROUPS[grp])
                pe.wait_ge(query_copied[grp][i], j + 1 + LEAD)
                pe.wait_ge(key_copied[grp][i], j + LEAD)
                for c in range(2):
                    for b in range(nb):
                        at = c * nb + b
                        mm = pe.matmul(bank[6 + i][:, at * KEYS:(at + 1) * KEYS], queryT[:, i, at * P:(at + 1) * P],
                                       subkT[:, j * 4 + 2 * i + c, :], start=True, stop=True)
                mm.then_inc(key_scored[grp][i], 1)

            def project_block0(i, between={}):
                chunk, g = OUT_ORDER[i]
                pe.wait_ge(wo_loaded[i % 4], (i // 4) * 16 + 16)
                project_out(0, g, w_slot[i % 4], [bank[5 + chunk % 3]], between)

            def mean_of_squares(j):
                pe.wait_ge(squared, j + 1)
                if j == 5:
                    pe.wait_ge(rms_ready, 1)
                pe.matmul(bank[j % 5][:, :], mean_mat[:, :], squares[:, j * 512:(j + 1) * 512], start=True,
                          stop=True).then_inc(meaned, 1)

            own_scores(H - 1)
            pe.wait_ge(v_evacuated, NB * H)
            streams = [partial(stream_scores, H - 1, j) for j in range(STREAMS)]
            project_block0(0, {0: streams[0:3], 1: streams[3:6], 2: streams[6:8]})
            past_scores(H - 1)
            project_block0(1)
            turn(H - 1)
            project_block0(2, {1: [partial(values, H - 1, 0)], 2: [partial(values, H - 1, 1)]})
            pe.wait_ge(oT_copied, 4 * H + LEAD)
            project_block0(3)
            for j in range(2):
                mean_of_squares(j)
            project_block0(4)
            project_block0(5)
            for j in range(2, 6):
                mean_of_squares(j)
            pe.wait_ge(diff_normed, 2)
            for i in range(6, len(OUT_ORDER)):
                if i == 12:
                    pe.wait_ge(residual_ready[0], 1)
                project_block0(i)
            pe.wait_ge(rms_ready, 6)
            turn_x1(0)
            pe.wait_ge(x1T_copied[0], 4)
            pe.wait_ge(subkeys_loaded, 16)
            with pe.Fori(0, 4) as j:
                for i in range(2):
                    for c in range(2):
                        pe.wait_ge(wq_loaded[2 * i + c], j * 16 + 16)
                        project_query(0, j, i, c, wq_slot[2 * i + c])
                for i in range(2):
                    score_keys(0, j, i)

            def start_block(b):
                for j in range(4):
                    pe.matmul(bank[4 * (b % 2) + j][:, :], ident_alpha[:, :], x1[:, b, j * 512:(j + 1) * 512],
                              start=True, stop=False, skip_group_check=True)

            def add_rows(g, quarter, half):
                for k in range(4 * quarter, 4 * quarter + 4):
                    pe.wait_ge(diag_ready, g * K + k + 1)
                    pe.wait_ge(v_loaded[k % V_SLOTS], (g * (K // V_SLOTS) + k // V_SLOTS) * 16 + 16)
                    for j in range(4):
                        mm = pe.matmul(bank[4 * half + j][:, :], diag[:, k % DIAGS, :],
                                       v_row[k % V_SLOTS][:, j * 512:(j + 1) * 512], start=False, stop=True,
                                       skip_group_check=True)
                    mm.then_inc(v_added, 1)

            def project_chunk(n, g):
                pe.wait_ge(pair_loaded[g % 2], (n * 2 + g // 2) * 16 + 16)
                if g == 0 and not isinstance(n, int):
                    pe.wait_ge(residual_ready[1], n * 2)
                project_out(1, g, w_pair[g % 2], [bank[4], bank[5]])

            for i in range(2):
                pe.wait_ge(query_copied[0][i], 4 + LEAD)
            pe.wait_ge(diff_normed, 6)
            for g in range(4):
                project_chunk(0, g)
            start_block(0)
            with pe.Fori(0, 3) as g:
                for quarter in range(4):
                    project_chunk(g + 1, quarter)
                    add_rows(g, quarter, 0)
            for quarter in range(4):
                add_rows(3, quarter, 0)
            for i in range(2):
                pe.wait_ge(key_copied[0][i], 4 + LEAD)
            turn_x1(1)
            pe.wait_ge(x1T_copied[1], 8)
            with pe.Fori(4, H) as g:
                for quarter in range(4):
                    pe.wait_ge(pair_loaded[quarter % 2], ((g - 4) * 2 + quarter // 2 + 8) * 16 + 16)
                    project_query(1, g - 4, quarter // 2, quarter % 2, w_pair[quarter % 2])
                    add_rows(g, quarter, 0)
                    if quarter % 2:
                        score_keys(1, g - 4, quarter // 2)
            for i in range(2):
                pe.wait_ge(key_copied[1][i], 4 + LEAD)
            start_block(1)
            with pe.Fori(H, 2 * H) as g:
                for quarter in range(4):
                    add_rows(g, quarter, 1)
            pe.wait_ge(ln2_scaled, 4)
            start_block(2)
            with pe.Fori(2 * H, HEADS) as g:
                for quarter in range(4):
                    add_rows(g, quarter, 0)

        @block.vector
        def _(dve):
            for s in half_read:
                dve.sem_inc(s, LEAD)
            dve.sem_inc(u_dotted, U_SLOTS)

            def low_x(i):
                tiles = slice(i * DT // X_PARTS, (i + 1) * DT // X_PARTS)
                dve.wait_ge(x_high_ready, i + 1)
                dve.tensor_tensor(x_low[:, tiles, :], xT[:, tiles, :], x_high[:, tiles, :], ALU.subtract)\
                   .then_inc(x_low_ready, 1)

            def low_w(h, u):
                dve.wait_ge(w_high_ready, h * UNITS + u + 1)
                dve.tensor_tensor(w_low[:, u, :], w_units[:, u, :], w_high[:, u % HIGH_UNITS, :],
                                  ALU.subtract).then_inc(w_low_ready, 1)

            low_w(0, 0)
            for i in range(X_PARTS):
                low_x(i)
            for u in range(1, UNITS):
                low_w(0, u)
            dve.wait_ge(consts_loaded, 32)
            for i in range(2):
                dve.tensor_tensor_reduce(lam_prod[:, i, :], lam_in[:, 2 * i, :], lam_in[:, 2 * i + 1, :], 1.0, 0.0,
                                         ALU.mult, ALU.add, lam_dot[:, i:i + 1]).then_inc(dve_init, 1)
            dve.wait_ge(pool_init, POOL_CONSTS)
            dve.tensor_scalar(frame_i[:, :], frame_i[:, :], FRAMES - 1, None, ALU.bitwise_and).then_inc(dve_init, 1)
            dve.wait_ge(dve_init, 3)
            dve.tensor_copy(frame_f[:, :], frame_i[:, :]).then_inc(dve_init, 1)
            dve.tensor_scalar(gain8[:, :], gain[:, :], 1.0 - LAM_INIT, None, ALU.mult).then_inc(dve_init, 1)
            dve.wait_ge(dve_init, 5)
            dve.tensor_scalar(dist[:, 0, 0:P], dist[:, 0, 0:P], frame_f[:, 0:1], None, ALU.add).then_inc(dve_init, 1)
            dve.wait_ge(act_init, 1)
            dve.tensor_tensor(lam_diff[:, :], lam_exp[:, 1:2], lam_exp[:, 0:1], ALU.subtract).then_inc(dve_init, 1)
            dve.wait_ge(dve_init, 7)
            dve.tensor_scalar(neg_lam[:, :], lam_diff[:, :], -LAM_INIT, None, ALU.add).then_inc(dve_init, 1)
            dve.wait_ge(dve_init, 8)

            def attend(h, ahead):
                if ahead:
                    for u in range(6):
                        low_w(h + 1, u)
                dve.wait_ge(scores_ready, h + 1)
                for b in range(NB):
                    lo = P if b == 1 else 0
                    d = dist[:, min(b, 1):min(b, 1) + 1, lo:256].to_broadcast([P, 2, 256 - lo])
                    dve.scalar_tensor_tensor(
                        out=probs[:, b, :, lo:256], in0=d, scalar=slopes[:, bass.ds(h, 1)],
                        in1=diff_ps[b].rearrange("p (c n) -> p c n", c=2), op0=ALU.mult,
                        op1=ALU.subtract).then_inc(scores_read, 1)
                dve.scalar_tensor_tensor(out=logit[:, 0:512], in0=stick02_ps, scalar=SB_SCALE,
                                         in1=stick_mask[:, 0:512], op0=ALU.mult, op1=ALU.add).then_inc(scores_read, 1)
                dve.scalar_tensor_tensor(out=logit[:, 512:640], in0=stick1_ps, scalar=SB_SCALE,
                                         in1=stick_mask[:, 512:640], op0=ALU.mult, op1=ALU.add)\
                   .then_inc(scores_read, 1)
                for b in range(NB):
                    lo = P if b == 1 else 0
                    dve.wait_ge(scores_read, h * 5 + b + 1)
                    dve.tensor_reduce(row_min[:, b, :], probs[:, b, :, lo:256], AX_X, ALU.min).then_inc(min_ready, 1)
                dve.wait_ge(scores_read, h * 5 + 5)
                dve.scalar_tensor_tensor(out=soft, in0=logit, scalar=-1.0, in1=logit, op0=ALU.mult,
                                         op1=ALU.min).then_inc(neg_abs_ready, 1)
                dve.wait_ge(probs_ready, h * 6 + 6)
                dve.reciprocal(row_inv[:, :, :], row_sum[:, :, :]).then_inc(inv_ready, 1)
                dve.wait_ge(inv_ready, h * 2 + 1)
                dve.tensor_scalar(lam_inv[:, :, :], row_inv[:, :, 1:2], neg_lam[:, 0:1], None, ALU.mult)\
                   .then_inc(inv_ready, 1)
                dve.wait_ge(transposed, h + LEAD)
                for b in range(NB):
                    lo = P if b == 1 else 0
                    w = weights[:, (0, 2, 3)[b]:(2, 3, 5)[b], :].rearrange("p s n -> p (s n)")
                    dve.tensor_scalar(w, probs[:, b, 0, lo:256], row_inv[:, b, 0:1], None, ALU.mult)\
                       .then_inc(half_weights, 1)
                dve.wait_ge(inv_ready, h * 2 + 2)
                for b in range(NB):
                    lo = P if b == 1 else 0
                    w = weights[:, (0, 2, 3)[b]:(2, 3, 5)[b], :].rearrange("p s n -> p (s n)")
                    dve.wait_ge(half_weights, h * NB + b + 1)
                    dve.scalar_tensor_tensor(out=w, in0=probs[:, b, 1, lo:256], scalar=lam_inv[:, b, 0:1], in1=w,
                                             op0=ALU.mult, op1=ALU.add).then_inc(weights_ready, 1)
                dve.wait_ge(soft_ready, h * 2 + 2)
                dve.scalar_tensor_tensor(out=soft, in0=logit, scalar=0.0, in1=soft, op0=ALU.max, op1=ALU.add)\
                   .then_inc(softplus_ready, 1)
                dve.wait_ge(softplus_ready, h + 1)
                dve.wait_ge(sticks_ready, h + LEAD)
                for lo, hi in ((0, 256), (256, 512), (512, 640)):
                    back = slice(hi - 1, lo - 1 if lo else None, -1)
                    dve.tensor_tensor_scan(suffix[:, back], soft[:, back], zeros[:, 0:hi - lo], 0.0, ALU.add,
                                           ALU.add).then_inc(suffix_ready, 1)
                dve.wait_ge(suffix_ready, h * 3 + 3)
                dve.tensor_tensor(suffix, logit, suffix, ALU.subtract).then_inc(exponent_ready, 1)
                if ahead:
                    for u in range(6, UNITS):
                        low_w(h + 1, u)

            with dve.Fori(0, H - 1) as h:
                attend(h, True)
            attend(H - 1, False)

            for j in range(6):
                cols = slice(j * 512, (j + 1) * 512)
                dve.wait_ge(rms_ready, j + 1)
                dve.reciprocal(squares[:, cols], squares[:, cols]).then_inc(rms_inv, 1)
                dve.wait_ge(rms_inv, j + 1)
                dve.scalar_tensor_tensor(out=mixed_diff[j], in0=mixed_diff[j], scalar=gain8[:, 0:1],
                                         in1=squares[:, cols], op0=ALU.mult, op1=ALU.mult).then_inc(diff_normed, 1)

            def add_residual(grp, n, banks, groups):
                nb = len(banks)
                for i, out in enumerate(banks):
                    b = GROUPS[grp][i]
                    if i + 1 < nb:
                        dve.wait_ge(out_projected[grp], n * (nb - 1) + i + 1)
                    else:
                        dve.wait_ge(wo_used[grp], groups)
                    dve.scalar_tensor_tensor(out=x1_chunk(b, n), in0=x1_chunk(b, n), scalar=ALPHA, in1=out[:, :],
                                             op0=ALU.mult, op1=ALU.add).then_inc(residual_ready[grp], 1)
                for i in range(nb):
                    b = GROUPS[grp][i]
                    dve.wait_ge(residual_ready[grp], n * nb + i + 1)
                    dve.bn_stats(stats[:, b, n, :], x1_chunk(b, n)).then_inc(stats_ready[grp], 1)

            def ln1_moments(grp):
                dve.wait_ge(stats_ready[grp], 4 * len(GROUPS[grp]))
                for b in GROUPS[grp]:
                    ins = dve.bn_aggr(moments[:, b, :], stats[:, b, :, :].rearrange("p n s -> p (n s)"))
                ins.then_inc(ln1_step[grp], 1)

            def ln1_shift(grp):
                b0, b1 = GROUPS[grp][0], GROUPS[grp][-1] + 1
                dve.wait_ge(ln1_sd[grp], 1)
                dve.reciprocal(rstd[:, b0:b1], stdev[:, b0:b1]).then_inc(ln1_step[grp], 1)
                dve.wait_ge(ln1_step[grp], 2)
                dve.scalar_tensor_tensor(out=shift[:, b0:b1], in0=moments[:, b0:b1, 0], scalar=-1.0,
                                         in1=rstd[:, b0:b1], op0=ALU.mult, op1=ALU.mult).then_inc(ln1_step[grp], 1)

            def ln1_affine(grp, i):
                b = GROUPS[grp][i]
                dve.wait_ge(ln_loaded, 16)
                for q in range(4):
                    dve.wait_ge(ln1_scaled[grp], 4 * i + q + 1)
                    dve.tensor_tensor(x1_chunk(b, q), x1_chunk(b, q), ln_rows[:, 0, q * 512:(q + 1) * 512],
                                      ALU.mult).then_inc(ln1_step[grp], 1)
                    dve.wait_ge(ln1_step[grp], 3 + 4 * i + q + 1)
                    dve.tensor_tensor(x1_chunk(b, q), x1_chunk(b, q), ln_rows[:, 1, q * 512:(q + 1) * 512],
                                      ALU.add).then_inc(ln1_done[grp], 1)

            dve.wait_ge(rows_loaded, 16)
            for n in range(4):
                add_residual(0, n, [bank[5 + n % 3]], OUT_ORDER.index((n, 3)) + 1)
            ln1_moments(0)
            ln1_shift(0)
            ln1_affine(0, 0)

            STEPS = {0: 45, 1: 75}

            def choose(grp, j, rows=None):
                nb = len(GROUPS[grp])
                nl = 2 * nb
                PER = STEPS[grp]
                n = [0]

                def ahead(ins):
                    n[0] += 1
                    ins.then_inc(topk_step[grp], 1)

                def settle(fill=True):
                    if rows and fill:
                        rows()
                    wait_apart(dve, "dve", topk_step[grp], j * PER + n[0])

                for i in range(2):
                    wait_apart(dve, "dve", key_copied[grp][i], j + 1 + LEAD)
                halves = [(c, lane) for c in range(2) for lane in range(nl)]
                for c, lane in halves:
                    ahead(dve.max(half_top[:, c, lane, 0:8], key_scores[:, c, lane, :]))
                settle(fill=False)
                for c, lane in halves:
                    ahead(dve.match_replace(rest[:, c, lane, :], half_top[:, c, lane, 0:8], key_scores[:, c, lane, :],
                                            LOW))
                for c, lane in halves:
                    ahead(dve.max_index(half_idx[:, c, lane, 0:8], half_top[:, c, lane, 0:8],
                                        key_scores[:, c, lane, :]))
                settle(fill=False)
                for c, lane in halves:
                    ahead(dve.max(half_top[:, c, lane, 8:16], rest[:, c, lane, :]))
                settle(fill=False)
                for c, lane in halves:
                    ins = dve.max_index(half_idx[:, c, lane, 8:16], half_top[:, c, lane, 8:16], rest[:, c, lane, :])
                    if (c, lane) != halves[-1]:
                        ahead(ins)
                    else:
                        ins.then_inc(half_read[grp], 1)
                wide = [P, nl, K, K]
                cand, cand_rest = sums[:, 0, 0:nl], sums[:, 1, 0:nl]
                ahead(dve.tensor_tensor(
                    cand, half_top[:, 0, 0:nl, :].rearrange("p l (i o) -> p l i o", o=1).to_broadcast(wide),
                    half_top[:, 1, 0:nl, :].rearrange("p l (o j) -> p l o j", o=1).to_broadcast(wide), ALU.add))
                settle()
                dve.wait_ge(half_read[grp], j + 1 + LEAD)
                ahead(dve.tensor_copy(half_idx_f[:, :, 0:nl, :], half_idx[:, :, 0:nl, :]))
                all_sums = [cand[:, lane, :, :].rearrange("p i j -> p (i j)") for lane in range(nl)]
                left = [cand_rest[:, lane, :, :].rearrange("p i j -> p (i j)") for lane in range(nl)]
                for lane in range(nl):
                    ahead(dve.max(top[:, lane, 0:8], all_sums[lane]))
                settle()
                for lane in range(nl):
                    ahead(dve.match_replace(left[lane], top[:, lane, 0:8], all_sums[lane], LOW))
                for lane in range(nl):
                    ahead(dve.max_index(top_pos[:, lane, 0:8], top[:, lane, 0:8], all_sums[lane]))
                settle()
                for lane in range(nl):
                    ahead(dve.max(top[:, lane, 8:16], left[lane]))
                settle()
                dve.tensor_tensor(over_max[:, 0:nl, :], top[:, 0:nl, :], top[:, 0:nl, 0:1].to_broadcast([P, nl, K]),
                                  ALU.subtract).then_inc(over_ready[grp], 1)
                for lane in range(nl):
                    ahead(dve.max_index(top_pos[:, lane, 8:16], top[:, lane, 8:16], left[lane]))
                settle()
                ahead(dve.tensor_scalar(pos_ij[:, 0, 0:nl, :], top_pos[:, 0:nl, :], 4, None,
                                        ALU.logical_shift_right))
                ahead(dve.tensor_scalar(pos_ij[:, 1, 0:nl, :], top_pos[:, 0:nl, :], K - 1, None, ALU.bitwise_and))
                settle()
                ahead(dve.tensor_copy(pos_ij_f[:, :, 0:nl, :], pos_ij[:, :, 0:nl, :]))
                settle()
                steps = iota16[:, :].rearrange("p (a b k) -> p a b k", a=1, b=1).to_broadcast(wide)
                for c in range(2):
                    ahead(dve.tensor_tensor(
                        sums[:, c, 0:nl], pos_ij_f[:, c, 0:nl, :].rearrange("p l (i o) -> p l i o", o=1)
                        .to_broadcast(wide), steps, ALU.is_equal))
                settle()
                for c in range(2):
                    ahead(dve.tensor_tensor(
                        sums[:, c, 0:nl], sums[:, c, 0:nl], half_idx_f[:, c, 0:nl, :]
                        .rearrange("p l (o j) -> p l o j", o=1).to_broadcast(wide), ALU.mult))
                settle()
                for c in range(2):
                    ahead(dve.tensor_reduce(picked[:, c, 0:nl, :], sums[:, c, 0:nl], AX_X, ALU.add))
                settle()
                ahead(dve.scalar_tensor_tensor(out=expert_f[:, 0:nl, :], in0=picked[:, 0, 0:nl, :],
                                               scalar=float(KEYS), in1=picked[:, 1, 0:nl, :], op0=ALU.mult,
                                               op1=ALU.add))
                if rows:
                    rows(every=True)
                dve.wait_ge(expo_ready[grp], j + 1)
                ahead(dve.tensor_reduce(expo_sum[:, 0:nl], expo[:, 0:nl, :], AX_X, ALU.add))
                settle()

                def place(tile):
                    if grp == 0:
                        return tile[:, 0:H, :].rearrange("p (h b) k -> p h b k", b=1)[:, bass.ds(j * 2, 2), :, :]
                    return tile[:, H:HEADS, :].rearrange("p (b h) k -> p h b k", b=nb)[:, bass.ds(j * 2, 2), :, :]

                def split(tile):
                    return tile.rearrange("p (h b) k -> p h b k", b=nb)

                ahead(dve.tensor_copy(place(expert), split(expert_f[:, 0:nl, :])))
                ahead(dve.reciprocal(expo_inv[:, 0:nl], expo_sum[:, 0:nl]))
                settle()
                ahead(dve.tensor_tensor(expo_out[:, 0:nl, :], expo[:, 0:nl, :],
                                        expo_inv[:, 0:nl].rearrange("p (l o) -> p l o", o=1)
                                        .to_broadcast([P, nl, K]), ALU.mult))
                settle()
                assert n[0] == PER, n[0]
                dve.tensor_copy(place(gate), split(expo_out[:, 0:nl, :])).then_inc(gates_ready[grp], 1)

            choose(0, 0)

            def dot(b, g, k):
                slot = k % U_SLOTS
                dve.wait_ge(u_loaded[slot], (g * (K // U_SLOTS) + k // U_SLOTS) * 16 + 16)
                dve.tensor_tensor_reduce(u_row[slot], u_row[slot], x1[:, b, :], 1.0, 0.0, ALU.mult, ALU.add,
                                         dots[:, k:k + 1]).then_inc(u_dotted, 1)

            def dots_of(b, g, k0=0, k1=K):
                if k0 == 0 and not (isinstance(g, int) and g == 0):
                    dve.wait_ge(gelu_ready, g)
                for k in range(k0, k1):
                    dot(b, g, k)

            def weigh(g):
                dve.wait_ge(gelu_ready, g + 1)
                dve.tensor_tensor(coef[:, g, :], gelu[:, :], gate[:, g, :], ALU.mult).then_inc(coef_ready, 1)

            def dots_and_choice(b, g, grp, j):
                at = [0]

                def rows(every=False):
                    if at[0] < K:
                        upto = K if every else min(at[0] + 2, K)
                        dots_of(b, g, at[0], upto)
                        at[0] = upto

                choose(grp, j, rows)
                dve.wait_ge(gates_ready[grp], j + 1)
                weigh(g)

            def ln2(b):
                half = b % 2
                dve.wait_ge(v_added, (b + 1) * H * K + V_SLOTS)
                for j in range(4):
                    dve.bn_stats(stats[:, b, j, :], bank[4 * half + j][:, :]).then_inc(ln2_stats, 1)
                dve.wait_ge(ln2_stats, 4 * (b + 1))
                dve.bn_aggr(moments[:, b, :], stats[:, b, :, :].rearrange("p n s -> p (n s)")).then_inc(ln2_step, 1)
                dve.wait_ge(ln2_sd, b + 1)
                dve.reciprocal(rstd[:, b:b + 1], stdev[:, b:b + 1]).then_inc(ln2_step, 1)
                dve.wait_ge(ln2_step, b * 3 + 2)
                dve.scalar_tensor_tensor(out=shift[:, b:b + 1], in0=moments[:, b, 0:1], scalar=-1.0,
                                         in1=rstd[:, b:b + 1], op0=ALU.mult, op1=ALU.mult).then_inc(ln2_step, 1)
                dve.wait_ge(ln_loaded, 32)
                for q in range(4):
                    cols = slice(q * 512, (q + 1) * 512)
                    dve.wait_ge(ln2_scaled, 4 * b + q + 1)
                    dve.tensor_tensor(normed[:, cols], normed[:, cols], ln_rows[:, 0, cols], ALU.mult)\
                       .then_inc(ln2_weighted, 1)
                    dve.wait_ge(ln2_weighted, 4 * b + q + 1)
                    dve.tensor_tensor(normed[:, cols], normed[:, cols], ln_rows[:, 1, cols], ALU.add)\
                       .then_inc(y_ready, 1)

            def dots_choice_residual(g):
                dots_and_choice(0, g, 0, g + 1)
                add_residual(1, g, [bank[4], bank[5]], g * 4 + 4)

            dots_choice_residual(0)
            with dve.Fori(1, 3) as g:
                dots_choice_residual(g)
            dots_of(0, 3)
            weigh(3)
            add_residual(1, 3, [bank[4], bank[5]], 4 * 4)
            ln1_moments(1)
            dots_of(0, 4, 0, 4)
            ln1_shift(1)
            dots_of(0, 4, 4, 8)
            ln1_affine(1, 0)
            dots_of(0, 4, 8, 12)
            ln1_affine(1, 1)
            dots_of(0, 4, 12, 16)
            weigh(4)
            dots_of(0, 5)
            weigh(5)
            with dve.Fori(5, H - 1) as g:
                dots_and_choice(0, g + 1, 1, g - 5)
            dots_and_choice(1, H, 1, 2)
            ln2(0)
            dots_and_choice(1, H + 1, 1, 3)
            with dve.Fori(H + 1, 2 * H - 1) as g:
                dots_of(1, g + 1)
                weigh(g + 1)
            dots_of(2, 2 * H)
            weigh(2 * H)
            ln2(1)
            with dve.Fori(2 * H, HEADS - 1) as g:
                dots_of(2, g + 1)
                weigh(g + 1)
            ln2(2)


def kernel(x_prompt, x_sample, cache_diff_k, cache_diff_v, cache_sb_k, cache_sb_v, w_in, w_out, lam_q1, lam_k1,
           lam_q2, lam_k2, subln_g, ln1_g, ln1_b, ln2_g, ln2_b, peer_w_q, peer_subkeys, peer_u, peer_v):
    import numpy as np
    import concourse.bacc as bacc
    from concourse.bass_utils import run_bass_kernel_spmd

    a = np.asarray
    x = np.concatenate([a(x_sample).reshape(P, D), a(x_prompt).reshape(2 * P, D)])
    w = a(w_in)[0]
    cols = lambda k: w[:, k * 1024:(k + 1) * 1024].reshape(DT, P, H, P).transpose(2, 1, 0, 3)
    qd, kd, vd, qs, ks, vs = (cols(k) for k in range(6))
    w_heads = np.concatenate([z.reshape(H, P, ROW) for z in (qd, kd, qs, ks)]
                             + [np.concatenate([vd, vs], axis=3).reshape(H, P, 2 * ROW)], axis=2)
    keysT = lambda z: a(z)[0].reshape(STREAMS, P, H, P).transpose(2, 3, 0, 1).reshape(H, P, STREAMS * P)
    rowsT = lambda z: a(z)[0].reshape(STREAMS, P, H, P).transpose(2, 1, 0, 3).reshape(H, P, STREAMS * P)
    wo = a(w_out)[0].reshape(4, 4, P, 4, 512).transpose(3, 0, 2, 1, 4)[:, [2, 3, 0, 1]].reshape(16, P, ROW)
    wq = a(peer_w_q)[0].reshape(DT, P, 2 * H, P).transpose(2, 1, 0, 3).reshape(2 * H, P, ROW)
    wide = lambda *z: np.broadcast_to(np.stack([a(q)[0] for q in z])[None], (P, len(z), a(z[0]).shape[1]))
    ins = {
        "x_t": x.reshape(T, DT, P).transpose(2, 1, 0).reshape(P, DT * T),
        "x_rows": x.reshape(NB, P, D).transpose(1, 0, 2),
        "w_heads": w_heads,
        "kd_cache": keysT(cache_diff_k), "ks_cache": keysT(cache_sb_k),
        "vd_cache": rowsT(cache_diff_v), "vs_cache": rowsT(cache_sb_v),
        "w_out": wo,
        "lam_vecs": wide(lam_q1, lam_k1, lam_q2, lam_k2),
        "subln": a(subln_g)[0].reshape(P, 1),
        "ln1": wide(ln1_g, ln1_b), "ln2": wide(ln2_g, ln2_b),
        "w_q": wq,
        "subkeys": a(peer_subkeys)[0].reshape(2 * H, KEYS, P).transpose(2, 0, 1),
        "peer_u": a(peer_u)[0], "peer_v": a(peer_v)[0],
    }
    outs = {"y_out": (NB, P, D), "kd_out": (H, P, T), "ks_out": (H, P, T), "v_out": (H, P, NB, 256)}
    nc = bacc.Bacc("TRN2", target_bir_lowering=False, num_devices=1)
    arrays, args = {}, []
    for name, z in ins.items():
        arrays[name] = np.ascontiguousarray(z)
        args.append(nc.dram_tensor(name, z.shape, F32, kind="ExternalInput").ap())
    for name, shape in outs.items():
        args.append(nc.dram_tensor(name, shape, F32, kind="ExternalOutput").ap())
    build(nc, *args)
    r = run_bass_kernel_spmd(nc, [arrays], core_ids=[0]).results[0]

    y = a(r["y_out"]).reshape(T, D)
    kd_new, ks_new = (a(r[n]).reshape(H, P, T).transpose(2, 0, 1) for n in ("kd_out", "ks_out"))
    v_all = a(r["v_out"]).reshape(H, P, NB, 2, P).transpose(2, 1, 3, 0, 4).reshape(T, 2, H, P)
    rows = (kd_new.reshape(T, H, 2, 64), v_all[:, 0], ks_new, v_all[:, 1])
    prompt = [z[P:].reshape((1, 1, 2 * P) + z.shape[1:]) for z in rows]
    sample = [z[:P].reshape((1, STREAMS, FRAMES) + z.shape[1:]) for z in rows]
    out = [y[P:].reshape(1, 2 * P, D), y[:P].reshape(STREAMS, FRAMES, D)] + prompt + sample
    return tuple(np.ascontiguousarray(z) for z in out)
```
